# Optimizing a Trainium2 kernel written in Bass

```python
import math
import jax
import jax.numpy as jnp
from jax import lax
import numpy as np

D_MODEL = 1024
BATCH = 1
SEQ = 512
DEPTH = 1
DEC_BATCH = 1
DEC_SEQ = 1024
PAST_LEN = 128

RMS_EPS = 1e-6
ATT_HEADS = 4
ATT_QK_DIM = 64
ATT_V_DIM = 2 * ATT_QK_DIM
ATT_WIDTH = ATT_HEADS * ATT_V_DIM
ROPE_DIM = ATT_QK_DIM // 4
ROPE_THETA = 500000.0
Q_BLOCK = 128
SSM_HEADS = 8
SSM_HEAD_DIM = 64
SSM_WIDTH = SSM_HEADS * SSM_HEAD_DIM
SSM_GROUPS = 2
SSM_STATE = 128
CONV_WIDTH = 5
CHUNK = 128
DT_MIN = 0.001
DT_MAX = 0.1
MIX_WIDTH = ATT_WIDTH + SSM_WIDTH
Q_COLS = ATT_HEADS * 2 * ATT_QK_DIM
K_COLS = ATT_HEADS * 2 * ATT_QK_DIM
V_COLS = ATT_WIDTH
Z_COLS = SSM_WIDTH
XBC_COLS = SSM_WIDTH + 2 * SSM_GROUPS * SSM_STATE
DT_COLS = 2 * SSM_HEADS
IN_COLS = Q_COLS + K_COLS + V_COLS + Z_COLS + XBC_COLS + DT_COLS
IN_SPLITS = (Q_COLS, Q_COLS + K_COLS, Q_COLS + K_COLS + V_COLS,
             Q_COLS + K_COLS + V_COLS + Z_COLS,
             Q_COLS + K_COLS + V_COLS + Z_COLS + XBC_COLS)
N_EXPERTS = 16
EXPERT_FF = 1024
CAPACITY_FACTOR = 2

kernel_name = 'hybrid_diffattn_ssd_expert_choice_encoder'

def rmsnorm(x, g):
    xf = x.astype(jnp.float32)
    y = xf * lax.rsqrt(jnp.mean(xf * xf, axis=-1, keepdims=True) + RMS_EPS)
    return (y * g.astype(jnp.float32)).astype(x.dtype)

def apply_partial_rope(t, positions):
    half = ROPE_DIM // 2
    inv_freq = jnp.power(ROPE_THETA, -jnp.arange(half, dtype=jnp.float32) * 2.0 / ROPE_DIM)
    ang = positions.astype(jnp.float32)[:, None] * inv_freq[None, :]
    cos = jnp.cos(ang)[None, :, None, None, :].astype(t.dtype)
    sin = jnp.sin(ang)[None, :, None, None, :].astype(t.dtype)
    t1 = t[..., :half]
    t2 = t[..., half:ROPE_DIM]
    rest = t[..., ROPE_DIM:]
    return jnp.concatenate([t1 * cos - t2 * sin, t2 * cos + t1 * sin, rest], axis=-1)

def differential_attention(q, k, v, lam, sub_g, lam_init):
    b, s = q.shape[0], q.shape[1]
    nb = s // Q_BLOCK
    qs = q * jnp.asarray(ATT_QK_DIM ** -0.5, q.dtype)
    qb = qs.reshape(b, nb, Q_BLOCK, ATT_HEADS, 2, ATT_QK_DIM).transpose(1, 0, 2, 3, 4, 5)

    def block(q_blk):
        sc = jnp.einsum('bqhcd,bkhcd->bhcqk', q_blk, k, preferred_element_type=jnp.float32)
        p = jax.nn.softmax(sc, axis=-1)
        w = p[:, :, 0] - lam * p[:, :, 1]
        return jnp.einsum('bhqk,bkhe->bqhe', w.astype(v.dtype), v)

    o = lax.map(block, qb)
    o = o.transpose(1, 0, 2, 3, 4).reshape(b, s, ATT_HEADS, ATT_V_DIM)
    o = rmsnorm(o, sub_g) * jnp.asarray(1.0 - lam_init, o.dtype)
    return o.reshape(b, s, ATT_WIDTH)

def centred_depthwise_conv(u, w, bias):
    pad = CONV_WIDTH // 2
    out = lax.conv_general_dilated(
        u, w[:, None, :].astype(u.dtype), window_strides=(1,), padding=[(pad, pad)],
        dimension_numbers=('NWC', 'WIO', 'NWC'), feature_group_count=u.shape[-1])
    return out + bias.astype(u.dtype)

def segsum_exp(a):
    cs = jnp.cumsum(a, axis=-1)
    diff = cs[..., :, None] - cs[..., None, :]
    n = a.shape[-1]
    mask = jnp.tril(jnp.ones((n, n), dtype=bool))
    return jnp.exp(jnp.where(mask, diff, -jnp.inf))

def ssd_chunked_scan(x, dt, a_neg, bm, cm):
    b, l = x.shape[0], x.shape[1]
    nc = l // CHUNK
    r = SSM_HEADS // SSM_GROUPS
    xf = (x.astype(jnp.float32) * dt[..., None]).reshape(b, nc, CHUNK, SSM_GROUPS, r, SSM_HEAD_DIM)
    a = (dt * a_neg).reshape(b, nc, CHUNK, SSM_GROUPS, r).transpose(0, 1, 3, 4, 2)
    bc = bm.astype(jnp.float32).reshape(b, nc, CHUNK, SSM_GROUPS, SSM_STATE)
    cc = cm.astype(jnp.float32).reshape(b, nc, CHUNK, SSM_GROUPS, SSM_STATE)
    a_cs = jnp.cumsum(a, axis=-1)
    lmat = segsum_exp(a)
    cb = jnp.einsum('bclgn,bcsgn->bcgls', cc, bc)
    y_diag = jnp.einsum('bcgls,bcgrls,bcsgrp->bclgrp', cb, lmat, xf)
    decay_states = jnp.exp(a_cs[..., -1:] - a_cs)
    states = jnp.einsum('bclgn,bcgrl,bclgrp->bcgrpn', bc, decay_states, xf)
    chunk_decay = jnp.exp(a_cs[..., -1])

    def step(h, inp):
        st, dec = inp
        return h * dec[..., None, None] + st, h

    h0 = jnp.zeros((b, SSM_GROUPS, r, SSM_HEAD_DIM, SSM_STATE), jnp.float32)
    _, prev = lax.scan(step, h0, (states.transpose(1, 0, 2, 3, 4, 5), chunk_decay.transpose(1, 0, 2, 3)))
    prev = prev.transpose(1, 0, 2, 3, 4, 5)
    y_off = jnp.einsum('bclgn,bcgrpn,bcgrl->bclgrp', cc, prev, jnp.exp(a_cs))
    return (y_diag + y_off).reshape(b, l, SSM_HEADS, SSM_HEAD_DIM)

def flip_seq(t):
    return jnp.flip(t, axis=1)

def bidirectional_ssd(z, xbc, dt_raw, conv_w, conv_b, dt_bias, a_log, d_skip, norm_g):
    b, s = z.shape[0], z.shape[1]
    xbc = jax.nn.silu(centred_depthwise_conv(xbc, conv_w, conv_b))
    xs, bm, cm = jnp.split(xbc, (SSM_WIDTH, SSM_WIDTH + SSM_GROUPS * SSM_STATE), axis=-1)
    xs = xs.reshape(b, s, SSM_HEADS, SSM_HEAD_DIM)
    bm = bm.reshape(b, s, SSM_GROUPS, SSM_STATE)
    cm = cm.reshape(b, s, SSM_GROUPS, SSM_STATE)
    y = xs.astype(jnp.float32) * d_skip.astype(jnp.float32)[:, None]
    for direction in range(2):
        dt = jax.nn.softplus((dt_raw[:, :, direction] + dt_bias[direction]).astype(jnp.float32))
        a_neg = -jnp.exp(a_log[direction].astype(jnp.float32))
        if direction == 0:
            y = y + ssd_chunked_scan(xs, dt, a_neg, bm, cm)
        else:
            y = y + flip_seq(ssd_chunked_scan(flip_seq(xs), flip_seq(dt), a_neg, flip_seq(bm), flip_seq(cm)))
    y = y.reshape(b, s, SSM_WIDTH).astype(z.dtype) * jax.nn.silu(z)
    gs = SSM_WIDTH // SSM_GROUPS
    y = rmsnorm(y.reshape(b, s, SSM_GROUPS, gs), norm_g.reshape(SSM_GROUPS, gs))
    return y.reshape(b, s, SSM_WIDTH)

def token_mixers(h, w_in, lam_qk, attn_sub_g, conv_w, conv_b, dt_bias, a_log, d_skip, ssm_norm_g, w_out, lam_init):
    b, s = h.shape[0], h.shape[1]
    proj = jnp.einsum('bsd,dc->bsc', h, w_in)
    q, k, v, z, xbc, dt_raw = jnp.split(proj, IN_SPLITS, axis=-1)
    pos = jnp.arange(s)
    q = apply_partial_rope(q.reshape(b, s, ATT_HEADS, 2, ATT_QK_DIM), pos)
    k = apply_partial_rope(k.reshape(b, s, ATT_HEADS, 2, ATT_QK_DIM), pos)
    v = v.reshape(b, s, ATT_HEADS, ATT_V_DIM)
    lq = lam_qk.astype(jnp.float32)
    lam = jnp.exp(jnp.sum(lq[0] * lq[1])) - jnp.exp(jnp.sum(lq[2] * lq[3])) + lam_init
    att = differential_attention(q, k, v, lam, attn_sub_g, lam_init)
    ssm = bidirectional_ssd(z, xbc, dt_raw.reshape(b, s, 2, SSM_HEADS), conv_w, conv_b,
                            dt_bias, a_log, d_skip, ssm_norm_g)
    return jnp.einsum('bsc,cd->bsd', jnp.concatenate([att, ssm], axis=-1), w_out)

def expert_choice_ffn(x, w_router, w_gate, w_up, w_down):
    b, s, d = x.shape
    t = b * s
    cap = CAPACITY_FACTOR * t // N_EXPERTS
    xf = x.reshape(t, d)
    logits = jnp.einsum('td,de->te', xf, w_router, preferred_element_type=jnp.float32)
    aff = jax.nn.softmax(logits, axis=-1)
    gate, idx = lax.top_k(aff.T, cap)
    xe = xf[idx]
    hid = jax.nn.silu(jnp.einsum('ecd,edf->ecf', xe, w_gate)) * jnp.einsum('ecd,edf->ecf', xe, w_up)
    ye = jnp.einsum('ecf,efd->ecd', hid, w_down) * gate[..., None].astype(x.dtype)
    out = jnp.zeros_like(xf).at[idx.reshape(-1)].add(ye.reshape(-1, d))
    return out.reshape(b, s, d)

def setup_inputs(seed: int = 0) -> dict:
    key = jax.random.key(seed)
    ks = jax.random.split(key, 20)
    f = jnp.float32
    dt0 = jnp.exp(jax.random.uniform(ks[8], (DEPTH, 2, SSM_HEADS), f)
                  * (math.log(DT_MAX) - math.log(DT_MIN)) + math.log(DT_MIN))
    dt_bias = dt0 + jnp.log(-jnp.expm1(-dt0))
    a_log = jnp.log(jax.random.uniform(ks[9], (DEPTH, 2, SSM_HEADS), f, 1.0, 16.0))
    return {
        'x_prompt': jax.random.normal(ks[0], (BATCH, SEQ, D_MODEL), f),
        'x_sample': jax.random.normal(ks[1], (DEC_BATCH, DEC_SEQ, D_MODEL), f),
        'norm1_g': 1.0 + 0.01 * jax.random.normal(ks[2], (DEPTH, D_MODEL), f),
        'w_in': jax.random.normal(ks[3], (DEPTH, D_MODEL, IN_COLS), f) * D_MODEL ** -0.5,
        'lam_qk': 0.1 * jax.random.normal(ks[4], (DEPTH, 4, ATT_QK_DIM), f),
        'attn_sub_g': 1.0 + 0.01 * jax.random.normal(ks[5], (DEPTH, ATT_V_DIM), f),
        'conv_w': jax.random.normal(ks[6], (DEPTH, CONV_WIDTH, XBC_COLS), f) * CONV_WIDTH ** -0.5,
        'conv_b': 0.01 * jax.random.normal(ks[7], (DEPTH, XBC_COLS), f),
        'dt_bias': dt_bias,
        'a_log': a_log,
        'd_skip': 1.0 + 0.01 * jax.random.normal(ks[10], (DEPTH, SSM_HEADS), f),
        'ssm_norm_g': 1.0 + 0.01 * jax.random.normal(ks[11], (DEPTH, SSM_WIDTH), f),
        'w_out': jax.random.normal(ks[12], (DEPTH, MIX_WIDTH, D_MODEL), f) * MIX_WIDTH ** -0.5,
        'norm2_g': 1.0 + 0.01 * jax.random.normal(ks[13], (DEPTH, D_MODEL), f),
        'w_router': jax.random.normal(ks[14], (DEPTH, D_MODEL, N_EXPERTS), f) * D_MODEL ** -0.5,
        'w_gate': jax.random.normal(ks[15], (DEPTH, N_EXPERTS, D_MODEL, EXPERT_FF), f) * D_MODEL ** -0.5,
        'w_up': jax.random.normal(ks[16], (DEPTH, N_EXPERTS, D_MODEL, EXPERT_FF), f) * D_MODEL ** -0.5,
        'w_down': jax.random.normal(ks[17], (DEPTH, N_EXPERTS, EXPERT_FF, D_MODEL), f) * EXPERT_FF ** -0.5,
        'final_g': 1.0 + 0.01 * jax.random.normal(ks[18], (D_MODEL,), f),
    }

def reference(x_prompt, x_sample, norm1_g, w_in, lam_qk, attn_sub_g, conv_w, conv_b, dt_bias, a_log,
              d_skip, ssm_norm_g, w_out, norm2_g, w_router, w_gate, w_up, w_down, final_g):
    def trunk(x):
        for l in range(DEPTH):
            lam_init = 0.8 - 0.6 * math.exp(-0.3 * l)
            h = rmsnorm(x, norm1_g[l])
            x = x + token_mixers(h, w_in[l], lam_qk[l], attn_sub_g[l], conv_w[l], conv_b[l], dt_bias[l],
                                 a_log[l], d_skip[l], ssm_norm_g[l], w_out[l], lam_init)
            h = rmsnorm(x, norm2_g[l])
            x = x + expert_choice_ffn(h, w_router[l], w_gate[l], w_up[l], w_down[l])
        return rmsnorm(x, final_g)

    y_prompt = trunk(x_prompt)
    y_sample = trunk(x_sample)
    return (y_prompt, y_sample)


_drawn_inputs = setup_inputs


def setup_inputs(seed=0):
    import zlib

    import numpy as np

    out = dict(_drawn_inputs(seed))
    spreads = {}
    factors = {'norm1_g': 3.66,
     'lam_qk': 5.982,
     'attn_sub_g': 7.52,
     'conv_b': 4.994,
     'd_skip': 200.0,
     'ssm_norm_g': 7.103,
     'norm2_g': 5.722,
     'final_g': 195.204}
    for name, (base, spread) in spreads.items():
        noise = np.random.default_rng([zlib.crc32(name.encode()), seed]).standard_normal(out[name].shape)
        drawn = base * np.exp(spread * noise) if base else spread * noise
        out[name] = jnp.asarray(drawn.astype(out[name].dtype))
    for name, factor in factors.items():
        out[name] = (out[name] * factor).astype(out[name].dtype)
    return out
```

```python
from contextlib import ExitStack

import concourse.bass as bass
from concourse import mybir

ALU = mybir.AluOpType
ACT = mybir.ActivationFunctionType
AX = mybir.AxisListType
F32 = mybir.dt.float32
F32R = mybir.dt.float32r
BF16 = mybir.dt.bfloat16
U32 = mybir.dt.uint32

P = 128
D = 1024
KT = D // P
CW = 256
BLK = 512
TPB = BLK // P
EPS = 1e-6
LAM_INIT = 0.2
HEADS = 4
SH = 8
NE = 16
NM = 25
NCH = 13
NR = 13
SEQS = [(0, 8, (0, 1), 128), (8, 4, (2,), 64)]
NT = 12
FIRST_CHUNK = {0: 0, 1: 13, 2: 30}
FIRST_OUT_CHUNK = (26, 43)
MOE_CHUNK = 47
ECH = 12
TOK = 192

PAR = {}
_at = 0
for _name, _w in (("conv_w", 40), ("conv_b", 8), ("d_skip", 4), ("ssm_g", 4), ("sub_g", 1), ("dt_bias", 16),
                  ("a_log", 16), ("lam", 256), ("router", KT * NE)):
    PAR[_name] = (_at, _at + _w)
    _at += _w
NPAR = _at
CST = {n: (i * P, i * P + P) for i, n in enumerate(("ident", "cum_f", "cum_b", "neg_f", "neg_b", "rot", "ones"))}
NCST = P * len(CST)


class Order:

    def __init__(self, engine, sem):
        self.engine, self.sem, self.n = engine, sem, 0

    def step(self, ins):
        self.n += 1
        ins.then_inc(self.sem, 1)

    def wait(self):
        self.engine.wait_ge(self.sem, self.n)

    def link(self, ins):
        self.step(ins)
        self.wait()


def hybrid_encoder(nc, x, w_in, w_out, w_moe, params, consts, rope, gains, y):
    ctx = ExitStack()
    KB = 1024
    base = 16640

    def at(name, kb, shape, dt=F32):
        return nc.alloc_sbuf_tensor_at(name, shape, dt, offset=base + int(kb * KB) // 32 * 32)

    def sem(name):
        return ctx.enter_context(nc.semaphore(name))

    with ctx:
        wraw = at("wraw", 0, [P, 2, KT * CW])
        whi = at("whi", 16, [P, 2, KT, CW], F32R)
        wlo = at("wlo", 32, [P, 2, KT, CW], F32R)
        ht_hi = at("ht_hi", 48, [P, KT, BLK], F32R)
        ht_lo = at("ht_lo", 64, [P, KT, BLK], F32R)
        qT = at("qT", 80, [P, HEADS, 1024])
        kT = at("kT", 96, [P, HEADS, 1024])
        v = at("v", 112, [P, 8, 512])
        LX = 1028
        xbc = at("xbc", 128, [P, 8, LX])
        S0 = 160.25
        conv_acc = at("conv_acc", S0, [P, 1024])
        cos_t = at("cos_t", S0 + 4, [P, BLK])
        sin_t = at("sin_t", S0 + 6, [P, BLK])
        stage = at("stage", S0 + 8, [P, 2, BLK])
        tmp = at("tmp", S0 + 12, [P, 2, BLK])
        xin = at("xin", S0 + 16, [P, 2, D])
        pr = at("pr", 48, [P, 2, 2, 1024])
        wgt = at("wgt", 64, [P, 2, 1024])
        wgtT = at("wgtT", 72, [P, 2, 1024])
        oatt = at("oatt", S0, [P, 8, 512])
        xf = at("xf", 48, [P, 8, 2, 512])
        state = [at("state_f", 96, [P, 8, 512]), at("state_b", 112, [P, 8, 512])]
        xs = at("xs", S0, [P, 2, 2, 512])
        btok = at("btok", S0 + 8, [P, 2, 256])
        scan_t = [at("scan_f", S0 + 10, [P, 512]), at("scan_b", S0 + 12, [P, 512])]
        er = at("er", S0, [P, 2, 512])
        dr = at("dr", S0 + 4, [P, 2, 512])
        lr = at("lr", S0 + 8, [P, 2, 512])
        mr = at("mr", S0 + 12, [P, 2, 512])
        cr = at("cr", S0 + 16, [P, 2, 512])
        zin = at("zin", S0 + 20, [P, 2, 512])
        sq = at("sq", S0, [P, 2, BLK])
        rs = at("rs", S0 + 4, [P, 2, BLK])
        mix_hi = at("mix_hi", 48, [P, KT, 1024], F32R)
        mix_lo = at("mix_lo", 96, [P, KT, 1024], F32R)
        x2 = at("x2", 128, [P, 8, D])
        h2 = at("h2", S0, [P, 2, D])
        h2T = at("h2T", S0 + 8, [P, 2, KT, P])
        aff = at("aff", 80, [P, P])
        aff2 = at("aff2", 80.5, [P, P])
        affT = at("affT", 84, [NE, 1024])
        xe_s = at("xe_s", 48, [P, D])
        xe_p = at("xe_p", 52, [64, D])
        xT = at("xT", 56, [P, KT, 2 * TOK], F32R)
        hid = at("hid", 68, [P, KT, 2 * TOK], F32R)
        gr = at("gr", 80, [P, 2, TOK])
        ur = at("ur", 82, [P, 2, TOK])
        sg = at("sg", 84, [P, 2, TOK])
        hm = at("hm", 86, [P, 2, TOK])
        ye_s = at("ye_s", 88, [P, D])
        ye_p = at("ye_p", 92, [64, D])
        tp = at("tp", 96, [64, 2, CW])
        yin = at("yin", 100, [P, 2, D])
        yout = at("yout", 108, [P, 2, D])
        gain = at("gain", 184.5, [P, D])
        junk = at("junk", 188.5, [P, D], BF16)
        cst = at("cst", 190.5, [P, NCST])
        par = at("par", 194, [P, NPAR])
        o = 194 + NPAR * 4 / KB + 0.1
        small = at("small", o, [P, 8, NT])
        dts = at("dts", o + 0.5, [P, 10, P])
        o += 5.6
        stat = at("stat", o, [P, 2, 16])
        ostat = at("ostat", o + 0.25, [P, 3, 32])
        lamt = at("lamt", o + 0.75, [P, 16])
        topv = at("topv", o + 0.9, [NE, P])
        topi = at("topi", o + 1.4, [NE, P], U32)
        topf = at("topf", o + 1.9, [NE, P])
        gate_s = at("gate_s", o + 2.4, [P, NE])
        gate_p = at("gate_p", o + 2.5, [64, NE])
        idx_s = at("idx_s", o + 2.6, [P, NE], U32)
        idx_p = at("idx_p", o + 2.7, [64, NE], U32)
        gcur_s = at("gcur_s", o + 2.8, [P, 1])
        gcur_p = at("gcur_p", o + 2.85, [64, 1])
        gi_s = at("gi_s", o + 2.9, [P, 1], U32)
        gi_p = at("gi_p", o + 2.95, [64, 1], U32)
        si_s = at("si_s", o + 3.0, [P, 1], U32)
        si_p = at("si_p", o + 3.05, [64, 1], U32)
        pmark2 = at("pmark2", o + 3.3, [1, 8])
        pmark = at("pmark", o + 3.2, [1, 8])
        mark = at("mark", o + 3.1, [1, 16])
        pb = [ctx.enter_context(nc.psum_tensor(f"bank{i}", [P, 512], F32)) for i in range(8)]

        z_dram = nc.dram_tensor("z_scratch", (3, P, 4, BLK), F32).ap()
        h2_dram = nc.dram_tensor("h2_scratch", (NT * P, D), F32).ap()
        acc_dram = nc.dram_tensor("acc_scratch", (NT * P, D), F32).ap()

        def c(name):
            a, b = CST[name]
            return cst[:, a:b]

        def p_(name, i=None, n=None):
            a, b = PAR[name]
            return par[:, a:b] if i is None else par[:, a + i:a + i + (n or 1)]

        ident = c("ident")

        cst_in, par_in = sem("cst_in"), sem("par_in")
        gain_in = sem("gain_in")
        rope_in = sem("rope_in")
        raw_in = [sem("raw_in0"), sem("raw_in1")]
        w_hi_done, w_lo_done = sem("w_hi_done"), sem("w_lo_done")
        xin_in = [sem("xin_in0"), sem("xin_in1")]
        ss_done, ms_done, rms_done, hn_done = sem("ss_done"), sem("ms_done"), sem("rms_done"), sem("hn_done")
        h_turned, ht_hi_done, ht_lo_done = sem("h_turned"), sem("ht_hi_done"), sem("ht_lo_done")
        col_done, col_out, turn_done, rot_out = sem("col_done"), sem("col_out"), sem("turn_done"), sem("rot_out")
        z_out = [sem("z_out0"), sem("z_out1")]
        conv_done, conv_act = sem("conv_done"), sem("conv_act")
        phase_act, phase_dve, phase_pool = sem("phase_act"), sem("phase_dve"), sem("phase_pool")
        sc_done, mx_done, exp_done, sc_free = sem("sc_done"), sem("mx_done"), sem("exp_done"), sem("sc_free")
        wg_done, wt_done, wt_out, av_done, av_out = sem("wg_done"), sem("wt_done"), sem("wt_out"), sem("av_done"), sem("av_out")
        osum_done, orms_done, on_done, ot_done, ot_out = (sem("osum_done"), sem("orms_done"), sem("on_done"),
                                                          sem("ot_done"), sem("ot_out"))
        dt_v, dt_a, cs_done = sem("dt_v"), sem("dt_a"), sem("cs_done")
        xt_done, bt_done, xf_done, bt_out, xs_done = (sem("xt_done"), sem("bt_done"), sem("xf_done"), sem("bt_out"),
                                                      sem("xs_done"))
        st_done, st_out = sem("st_done"), sem("st_out")
        cb_done, cb_used, row_done, e_done, d_done, l_done = (sem("cb_done"), sem("cb_used"), sem("row_done"),
                                                              sem("e_done"), sem("d_done"), sem("l_done"))
        m_done, c_done, yh_done, y_done, y_used = (sem("m_done"), sem("c_done"), sem("yh_done"), sem("y_done"),
                                                   sem("y_used"))
        z_in = [sem("z_in0"), sem("z_in1")]
        z_used = sem("z_used")
        sq_done, nsum_done, nms_done, nrms_done, nrm_done = (sem("sq_done"), sem("nsum_done"), sem("nms_done"),
                                                             sem("nrms_done"), sem("nrm_done"))
        mix_hi_done, mix_lo_done = sem("mix_hi_done"), sem("mix_lo_done")
        x2_in = sem("x2_in")
        op_done, op_out = sem("op_done"), sem("op_out")
        ss2_done, rms2_done, h2_done, h2_turned, h2T_out = (sem("ss2_done"), sem("rms2_done"), sem("h2_done"),
                                                            sem("h2_turned"), sem("h2T_out"))
        x2_out = sem("x2_out")
        h2_out = [sem("h2_out0"), sem("h2_out1")]
        lg_done = sem("lg_done")
        rt_v, rt_a, rt_p = sem("rt_v"), sem("rt_a"), sem("rt_p")
        own_dve, own_act, own_pool = sem("own_dve"), sem("own_act"), sem("own_pool")
        idx_ready, cur_ready = sem("idx_ready"), sem("cur_ready")
        xs_in, xp_in = sem("xs_in"), sem("xp_in")
        xturn, xhi_done, xlo_done = sem("xturn"), sem("xhi_done"), sem("xlo_done")
        tile_done, red_done, silu_done, hm_done = sem("tile_done"), sem("red_done"), sem("silu_done"), sem("hm_done")
        hhi_done, hlo_done = sem("hhi_done"), sem("hlo_done")
        ys_done, tp_done, yp_done = sem("ys_done"), sem("tp_done"), sem("yp_done")
        sc_s, sc_p = sem("sc_s"), sem("sc_p")
        y_in = [sem("y_in0"), sem("y_in1")]
        fss, fms, frms, fy = sem("fss"), sem("fms"), sem("frms"), sem("fy")
        y_out = [sem("y_out0"), sem("y_out1")]
        half_added, adds_done, scattered = sem("half_added"), sem("adds_done"), sem("scattered")

        block = ctx.enter_context(nc.Block())

        def block_tile(b):
            return {0: 0, 1: TPB, 2: 0}[b]

        def chunk_used(eng, g):
            if g < 0:
                return
            for s in (1, 0):
                if g >= FIRST_OUT_CHUNK[s] and (s == 1 or g < FIRST_CHUNK[2]):
                    nt = SEQS[s][1]
                    done = 4 * SEQS[0][1] if s else 0
                    eng.wait_ge(op_done, done + nt * (g - FIRST_OUT_CHUNK[s] + 1))
                    return
            b = max(b for b in range(3) if g >= FIRST_CHUNK[b])
            eng.wait_ge(col_done, NM * b + min(2 * (g - FIRST_CHUNK[b] + 1), NM))

        def phase(eng, n, but=None):
            for s in (phase_act, phase_dve, phase_pool):
                if s is not but:
                    eng.wait_ge(s, n)


        @block.sync
        def _(sp):
            sp.dma_start(cst[:, :], consts).then_inc(cst_in, 16)
            sp.dma_start(par[:, :], params).then_inc(par_in, 16)

            def load(g, src):
                if g >= 2:
                    sp.wait_ge(w_lo_done, g - 1)
                sp.dma_start(wraw[:, g % 2, :], src).then_inc(raw_in[g % 2], 16)

            for s, (_, _, blocks, _) in enumerate(SEQS):
                for b in blocks:
                    for j in range(NCH):
                        load(FIRST_CHUNK[b] + j, w_in[j])
                for j in range(4):
                    load(FIRST_OUT_CHUNK[s] + j, w_out[j])
            with sp.Fori(0, NE) as e:
                for j in range(ECH):
                    sp.wait_ge(w_lo_done, e * ECH + (MOE_CHUNK + j - 1))
                    sp.dma_start(wraw[:, (MOE_CHUNK + j) % 2, :],
                                 w_moe[bass.ds(e * ECH + j, 1), :, :].rearrange("a p n -> (a p) n")
                                 ).then_inc(raw_in[(MOE_CHUNK + j) % 2], 16)
            sp.wait_ge(sc_s, 16 * NE)
            sp.wait_ge(sc_p, 16 * NE)
            for t in range(NT):
                if t >= 2:
                    sp.wait_ge(fy, t - 1)
                sp.dma_start(yin[:, t % 2, :], acc_dram[t * P:(t + 1) * P, :]).then_inc(y_in[t % 2], 16)
                if t >= 1:
                    sp.wait_ge(fy, t)
                    sp.dma_start(y[(t - 1) * P:t * P, :], yout[:, (t - 1) % 2, :]).then_inc(y_out[(t - 1) % 2], 16)
            sp.wait_ge(fy, NT)
            sp.dma_start(y[(NT - 1) * P:NT * P, :], yout[:, (NT - 1) % 2, :]).then_inc(y_out[(NT - 1) % 2], 16)
            for i in range(2):
                sp.wait_ge(y_out[i], 16 * (NT // 2))

        @block.gpsimd
        def _(pool):
            own = Order(pool, own_pool)
            for s, (t0, nt, blocks, cap) in enumerate(SEQS):
                ph = 7 * s
                if s:
                    phase(pool, ph, phase_pool)
                pool.dma_start(gain[:, :], gains[0]).then_inc(gain_in, 16)
                for b in blocks:
                    if b:
                        pool.wait_ge(rot_out, NR * b)
                    c0 = block_tile(b) * P
                    pool.dma_start(cos_t[:, :], rope[0][:, c0:c0 + BLK]).then_inc(rope_in, 16)
                    pool.dma_start(sin_t[:, :], rope[1][:, c0:c0 + BLK]).then_inc(rope_in, 16)
                    for j in range(TPB):
                        t = TPB * b + j
                        if t >= 2:
                            pool.wait_ge(h_turned, 2 * (t - 1))
                        pool.dma_start(xin[:, t % 2, :], x[t * P:(t + 1) * P, :]).then_inc(xin_in[t % 2], 16)
                    for j in range(4):
                        pool.wait_ge(col_out, NM * b + 21 + j)
                        pool.dma_start(z_dram[b][:, j, :], tmp[:, j % 2, :]).then_inc(z_out[j % 2], 16)
                for i in range(2):
                    pool.wait_ge(z_out[i], 16 * 2 * (blocks[-1] + 1))
                pool.memset(mark[0:1, 0:1], 0.0).then_inc(phase_pool, 1)
                pool.memset(mark[0:1, 1:2], 0.0).then_inc(phase_pool, 1)

                phase(pool, ph + 2, phase_pool)
                pool.wait_ge(dt_a, 3 * s + 3)
                for cc in range(nt):
                    k = 8 * s + cc
                    pool.wait_ge(xf_done, 2 * (k + 1))
                    if k >= 2:
                        pool.wait_ge(st_done, 4 * (k - 1))
                    for d in range(2):
                        ins = pool.tensor_tensor(
                            xs[:, cc % 2, d, :].rearrange("p (h q) -> p h q", h=SH),
                            xf[:, cc, d, :].rearrange("p (h q) -> p h q", h=SH),
                            dts[:, 9, cc * 16 + 8 * d:cc * 16 + 8 * d + 8].unsqueeze(2).to_broadcast([P, SH, 64]),
                            ALU.mult)
                        ins.then_inc(xs_done, 1)
                pool.wait_ge(st_out, 2 * (8 * s + nt))
                for cc in range(nt - 2, 0, -1):
                    own.link(pool.tensor_tensor(
                        scan_t[1][:, :].rearrange("p (h q) -> p h q", h=SH),
                        state[1][:, cc, :].rearrange("p (h q) -> p h q", h=SH),
                        dts[:, 8, cc * 16 + 8:cc * 16 + 16].unsqueeze(2).to_broadcast([P, SH, 64]), ALU.mult))
                    own.link(pool.tensor_tensor(state[1][:, cc - 1, :], state[1][:, cc - 1, :], scan_t[1][:, :],
                                                ALU.add))
                pool.memset(mark[0:1, 0:1], 0.0).then_inc(phase_pool, 1)

                phase(pool, ph + 3, phase_pool)
                for cc in range(nt):
                    k = 8 * s + cc
                    if cc >= 2:
                        pool.wait_ge(z_used, k - 1)
                    b = blocks[cc // TPB]
                    pool.dma_start(zin[:, k % 2, :].rearrange("p (j l) -> p j l", j=4),
                                   z_dram[b][:, :, (cc % TPB) * P:(cc % TPB + 1) * P]).then_inc(z_in[k % 2], 16)
                    for u in range(4):
                        g, d, n = u // 2, u % 2, 4 * k + u
                        pool.wait_ge(e_done, n + 1)
                        if n >= 2:
                            pool.wait_ge(yh_done, n - 1)
                        pool.tensor_tensor(
                            cr[:, n % 2, :].rearrange("p (h l) -> p h l", h=4),
                            er[:, n % 2, :].rearrange("p (h l) -> p h l", h=4),
                            xbc[:, 6 + g, 2 + cc * P:2 + cc * P + P].unsqueeze(1).to_broadcast([P, 4, P]),
                            ALU.mult).then_inc(c_done, 1)
                pool.memset(mark[0:1, 0:1], 0.0).then_inc(phase_pool, 1)
                pool.memset(mark[0:1, 1:2], 0.0).then_inc(phase_pool, 1)

                phase(pool, ph + 5, phase_pool)
                pool.dma_start(gain[:, :], gains[1]).then_inc(gain_in, 16)
                pool.dma_start(x2[:, 0:nt, :], x[t0 * P:(t0 + nt) * P, :].rearrange("(t p) d -> p t d", p=P)
                               ).then_inc(x2_in, 16)
                pool.wait_ge(op_out, 4 * (t0 + nt))
                pool.dma_start(acc_dram[t0 * P:(t0 + nt) * P, :].rearrange("(t p) d -> p t d", p=P), x2[:, 0:nt, :]
                               ).then_inc(x2_out, 16)
                for j in range(nt):
                    t = t0 + j
                    pool.wait_ge(h2_done, t + 1)
                    pool.dma_start(h2_dram[t * P:(t + 1) * P, :], h2[:, t % 2, :]).then_inc(h2_out[t % 2], 16)
                pool.wait_ge(x2_out, 16 * (s + 1))
                for i in range(2):
                    pool.wait_ge(h2_out[i], 16 * (t0 + nt) // 2)
                pool.memset(mark[0:1, 0:1], 0.0).then_inc(phase_pool, 1)
                pool.memset(mark[0:1, 1:2], 0.0).then_inc(phase_pool, 1)

            phase(pool, 14, phase_pool)
            pool.dma_start(gain[:, :], gains[2]).then_inc(gain_in, 16)

            def gather(e1, first=False):
                if not first:
                    pool.wait_ge(adds_done, e1 * 2 - 1)
                pool.wait_ge(idx_ready, e1 + 1)
                pool.tensor_tensor(pmark[:, 0:1], pmark[:, 1:2], pmark[:, 2:3], ALU.add).then_inc(adds_done, 1)
                pool.indirect_dma_start(out=xe_s[:, :], out_offset=None, in_=h2_dram,
                                        in_offset=bass.IndirectOffsetOnAxis(ap=gi_s[:, 0:1], axis=0)
                                        ).then_inc(xs_in, 16)
                pool.indirect_dma_start(out=xe_p[:, :], out_offset=None, in_=h2_dram,
                                        in_offset=bass.IndirectOffsetOnAxis(ap=gi_p[:, 0:1], axis=0)
                                        ).then_inc(xp_in, 16)

            def expert(e, last):
                if not last:
                    pool.wait_ge(xturn, (e + 1) * 4)
                    gather(e + 1)
                pool.wait_ge(cur_ready, e + 1)
                pool.wait_ge(ys_done, (e + 1) * 4)
                pool.wait_ge(yp_done, e * 4 + 6)
                pool.wait_ge(adds_done, e * 2 + (1 if last else 2))
                pool.tensor_tensor(pmark[:, 0:1], pmark[:, 1:2], pmark[:, 2:3], ALU.add).then_inc(adds_done, 1)
                pool.indirect_dma_start(out=acc_dram, in_=ye_s[:, :], in_offset=None, compute_op=ALU.add,
                                        out_offset=bass.IndirectOffsetOnAxis(ap=si_s[:, 0:1], axis=0)
                                        ).then_inc(sc_s, 16)
                pool.indirect_dma_start(out=acc_dram, in_=ye_p[:, :], in_offset=None, compute_op=ALU.add,
                                        out_offset=bass.IndirectOffsetOnAxis(ap=si_p[:, 0:1], axis=0)
                                        ).then_inc(sc_p, 16)
                pool.wait_ge(sc_s, e * 16 + 16)
                pool.wait_ge(sc_p, e * 16 + 16)
                pool.wait_ge(scattered, e + 1)
                pool.tensor_tensor(pmark[:, 3:4], pmark[:, 1:2], pmark[:, 2:3], ALU.add).then_inc(scattered, 1)

            pool.wait_ge(x2_out, 32)
            pool.memset(pmark[:, :], 0.0).then_inc(own_pool, 1)
            pool.memset(pmark2[:, :], 0.0).then_inc(scattered, 1)
            own.n += 1
            own.wait()
            gather(0, True)
            with pool.Fori(0, NE - 1) as e:
                expert(e, False)
            expert(NE - 1, True)

        @block.scalar
        def _(act):
            own = Order(act, own_act)

            def split(g):
                act.wait_ge(raw_in[g % 2], 16 * (g // 2 + 1))
                chunk_used(act, g - 2)
                act.activation(whi[:, g % 2, :, :], wraw[:, g % 2, :].rearrange("p (k n) -> p k n", k=KT), ACT.Copy
                               ).then_inc(w_hi_done, 1)

            def end():
                act.activation(mark[0:1, 4:5], mark[0:1, 5:6], ACT.Copy).then_inc(phase_act, 1)

            act.wait_ge(cst_in, 16)
            act.wait_ge(par_in, 16)
            act.wait_ge(own_dve, 1)
            act.wait_ge(own_dve, 5)
            act.activation(lamt[:, 2:4], lamt[:, 0:2], ACT.Exp).then_inc(own_act, 1)
            act.activation(stat[:, 0, :], p_("a_log"), ACT.Exp).then_inc(own_act, 1)
            own.n = 2
            split(0)
            for s, (t0, nt, blocks, cap) in enumerate(SEQS):
                ph = 7 * s
                L = nt * P
                if s:
                    phase(act, ph, phase_act)
                for b in blocks:
                    for j in range(TPB):
                        t = TPB * b + j
                        act.wait_ge(xin_in[t % 2], 16 * (t // 2 + 1))
                        act.activation(junk[:, :], xin[:, t % 2, :], ACT.Square, accum_out=small[:, 0, t:t + 1]
                                       ).then_inc(ss_done, 1)
                        act.wait_ge(ms_done, t + 1)
                        act.activation(small[:, 2, t:t + 1], small[:, 1, t:t + 1], ACT.Sqrt).then_inc(rms_done, 1)
                        if b and j == 0:
                            act.wait_ge(col_done, NM * b)
                            if b == 2:
                                act.wait_ge(op_done, 4 * 8)
                        for q in range(2):
                            act.wait_ge(h_turned, 2 * t + q + 1)
                            act.activation(ht_hi[:, 4 * q:4 * q + 4, j * P:(j + 1) * P],
                                           pb[6 + q][:, :].rearrange("p (k n) -> p k n", k=4), ACT.Copy
                                           ).then_inc(ht_hi_done, 1)
                    for m in range(NM):
                        n = NM * b + m
                        if m % 2 == 0:
                            split(FIRST_CHUNK[b] + m // 2 + 1)
                        act.wait_ge(col_done, n + 1)
                        src = pb[m % 4][:, :]
                        tok = block_tile(b) * P
                        if m < 8:
                            ins = act.activation(xbc[:, m, 2 + tok:2 + tok + BLK], src, ACT.Copy)
                        elif m < 20 or m == 24:
                            r = NR * b + min(m - 8, 12)
                            if r >= 2:
                                act.wait_ge(rot_out, r - 1)
                            ins = act.activation(stage[:, r % 2, :], src, ACT.Copy, scale=0.125 if m < 12 else 1.0)
                        else:
                            act.wait_ge(rot_out, NR * b + 8)
                            if m >= 22:
                                act.wait_ge(z_out[m % 2], 16 * (2 * b + 1))
                            ins = act.activation(tmp[:, m % 2, :], src, ACT.Silu)
                        ins.then_inc(col_out, 1)
                        if b == blocks[-1] and 9 <= m < 17:
                            i = m - 9
                            act.wait_ge(conv_done, 8 * s + i + 1)
                            act.activation(xbc[:, i, 2:2 + L], conv_acc[:, 0:L], ACT.Silu, bias=p_("conv_b", i)
                                           ).then_inc(conv_act, 1)
                end()

                phase(act, ph + 1, phase_act)
                nh = (L + 511) // 512
                for u in range(4 * nt + 1):
                    U = 4 * t0 + u
                    if u < 4 * nt:
                        for h in range(2):
                            act.wait_ge(mx_done, 2 * U + h + 1)
                            if U >= 2:
                                act.wait_ge(wg_done, U - 1)
                            for q in range(nh):
                                ins = (act.activation(pr[:, u % 2, h, q * 512:(q + 1) * 512], pb[2 * h + q][:, :],
                                                        ACT.Exp, bias=ostat[:, 0, 2 * (u % 2) + h:2 * (u % 2) + h + 1],
                                                        accum_out=ostat[:, 1, 4 * (u % 2) + 2 * h + q:
                                                                        4 * (u % 2) + 2 * h + q + 1]))
                            ins.then_inc(exp_done, 1)
                    if u >= 1:
                        w = u - 1
                        W = 4 * t0 + w
                        for q in range(nt // 4):
                            act.wait_ge(wt_done, (64 if s else 0) + (nt // 4) * w + q + 1)
                            if W >= 2:
                                act.wait_ge(av_done, W - 1)
                            act.activation(wgtT[:, w % 2, q * 512:(q + 1) * 512], pb[4 + q][:, :], ACT.Copy
                                           ).then_inc(wt_out, 1)
                        if w % 4 == 3:
                            i = w // 4
                            act.wait_ge(av_done, W + 1)
                            own.link(act.activation(oatt[:, i, :], pb[6 + i % 2][:, :], ACT.Copy))
                            if i:
                                act.wait_ge(av_out, t0 + i)
                            for h in range(4):
                                ins = act.activation(junk[:, h * P:(h + 1) * P], oatt[:, i, h * P:(h + 1) * P], ACT.Square,
                                                     accum_out=dts[:, 0, 4 * i + h:4 * i + h + 1])
                            ins.then_inc(av_out, 1)
                act.wait_ge(osum_done, s + 1)
                act.activation(dts[:, 2, 0:4 * nt], dts[:, 1, 0:4 * nt], ACT.Sqrt).then_inc(orms_done, 1)
                for i in range(nt):
                    act.wait_ge(ot_done, t0 + i + 1)
                    act.activation(qT[:, :, i * P:(i + 1) * P], pb[i % 2][:, :].rearrange("p (h n) -> p h n", h=4),
                                   ACT.Copy, scale=lamt[:, 8:9]).then_inc(ot_out, 1)
                end()

                phase(act, ph + 2, phase_act)
                act.wait_ge(dt_v, 4 * s + 1)
                act.activation(dts[:, 2, 0:16 * nt], dts[:, 1, 0:16 * nt], ACT.Exp).then_inc(dt_a, 1)
                act.wait_ge(dt_v, 4 * s + 2)
                act.activation(dts[:, 4, 0:16 * nt], dts[:, 3, 0:16 * nt], ACT.Ln).then_inc(dt_a, 1)
                act.wait_ge(dt_v, 4 * s + 4)
                act.activation(dts[:, 8, 0:16 * nt], dts[:, 3, 0:16 * nt], ACT.Exp).then_inc(own_act, 1)
                act.activation(dts[:, 9, 0:16 * nt], dts[:, 4, 0:16 * nt], ACT.Exp).then_inc(dt_a, 1)
                own.n += 1
                for cc in range(nt):
                    k = 8 * s + cc
                    act.wait_ge(bt_done, k + 1)
                    if k >= 2:
                        act.wait_ge(st_done, 4 * (k - 1))
                    act.activation(btok[:, cc % 2, :], pb[1 if cc % 2 == 0 else 3][:, 0:256], ACT.Copy
                                   ).then_inc(bt_out, 1)
                    for d in range(2):
                        act.wait_ge(st_done, 4 * k + 2 * d + 2)
                        to = cc + 1 if d == 0 else cc - 1
                        if 0 <= to < nt:
                            ins = act.activation(state[d][:, to, :], pb[4 + d][:, :], ACT.Copy)
                        else:
                            ins = act.activation(mark[0:1, 6:7], mark[0:1, 5:6], ACT.Copy)
                        ins.then_inc(st_out, 1)
                end()

                phase(act, ph + 3, phase_act)
                for n4 in range(4 * nt):
                    n = 32 * s + n4
                    cc, g, d = n4 // 4, (n4 // 2) % 2, n4 % 2
                    act.wait_ge(row_done, n + 1)
                    if n >= 2:
                        act.wait_ge(c_done, n - 1)
                    act.activation(er[:, n % 2, :], pb[2 + n % 2][:, :], ACT.Exp).then_inc(e_done, 1)
                    act.wait_ge(d_done, n + 1)
                    if n >= 2:
                        act.wait_ge(m_done, n - 1)
                    for hh in range(4):
                        col = cc * 16 + 8 * d + 4 * g + hh
                        ins = act.activation(lr[:, n % 2, hh * P:(hh + 1) * P], dr[:, n % 2, hh * P:(hh + 1) * P],
                                             ACT.Exp, bias=dts[:, 7, col:col + 1])
                    ins.then_inc(l_done, 1)
                end()

                phase(act, ph + 4, phase_act)
                for q in range(2 * (L // BLK)):
                    N = (4 if s else 0) + q
                    hf, g = q // 2, q % 2
                    for i in range(2):
                        if q >= 1:
                            act.wait_ge(nsum_done, N)
                        act.activation(sq[:, i, :], xbc[:, 2 * g + i, 2 + hf * BLK:2 + (hf + 1) * BLK], ACT.Square
                                       ).then_inc(sq_done, 1)
                    act.wait_ge(nms_done, N + 1)
                    act.activation(rs[:, 0, :], rs[:, 1, :], ACT.Sqrt).then_inc(nrms_done, 1)
                for k in range(KT):
                    src = qT[:, k, 0:L] if k < 4 else xbc[:, k - 4, 2:2 + L]
                    if k == 4:
                        act.wait_ge(nrm_done, 2 * ((4 if s else 0) + 2 * (L // BLK)))
                    act.activation(mix_hi[:, k, 0:L], src, ACT.Copy).then_inc(mix_hi_done, 1)
                end()

                phase(act, ph + 5, phase_act)
                for jo in range(4):
                    g = FIRST_OUT_CHUNK[s] + jo + 1
                    if g < MOE_CHUNK:
                        split(g)
                    else:
                        act.wait_ge(raw_in[g % 2], 16 * (g // 2 + 1))
                        chunk_used(act, g - 2)
                        act.activation(whi[:, g % 2, :, :], wraw[:, g % 2, :].rearrange("p (k n) -> p k n", k=KT),
                                       ACT.Copy).then_inc(w_hi_done, 1)
                for i in range(nt):
                    act.wait_ge(op_out, 4 * t0 + 3 * nt + i + 1)
                    ins = act.activation(junk[:, :], x2[:, i, :], ACT.Square, accum_out=small[:, 0, i:i + 1])
                    ins.then_inc(ss2_done, 1)
                    act.wait_ge(ss2_done, t0 + i + 1)
                act.wait_ge(rms2_done, 2 * s + 1)
                act.activation(small[:, 2, 0:nt], small[:, 1, 0:nt], ACT.Sqrt).then_inc(rms2_done, 1)
                for i in range(nt):
                    t = t0 + i
                    for q in range(2):
                        act.wait_ge(h2_turned, 2 * t + q + 1)
                        if t >= 2:
                            act.wait_ge(lg_done, t - 1)
                        act.activation(h2T[:, t % 2, 4 * q:4 * q + 4, :],
                                       pb[6 + q][:, :].rearrange("p (k n) -> p k n", k=4), ACT.Copy
                                       ).then_inc(h2T_out, 1)
                end()

                phase(act, ph + 6, phase_act)
                act.wait_ge(rt_v, 4 * s + 1)
                act.activation(aff[:, 0:16 * nt], aff[:, 0:16 * nt], ACT.Exp).then_inc(rt_a, 1)
                end()

            phase(act, 14, phase_act)

            def turned_out(n):
                for kk in range(4):
                    act.wait_ge(xturn, n * 4 + kk + 1)
                    act.activation(xT[:, 2 * kk:2 * kk + 2, 0:TOK],
                                   pb[6 + kk % 2][:, 0:2 * TOK].rearrange("p (k n) -> p k n", k=2), ACT.Copy
                                   ).then_inc(xhi_done, 1)

            def expert(e, last):
                for j in range(ECH):
                    if not (last and j == ECH - 1):
                        g = MOE_CHUNK + j + 1
                        act.wait_ge(raw_in[g % 2], e * (16 * ECH // 2) + 16 * (g // 2 + 1))
                        act.wait_ge(tile_done, e * 24 + 2 * j + 2)
                        act.activation(whi[:, g % 2, :, :], wraw[:, g % 2, :].rearrange("p (k n) -> p k n", k=KT),
                                       ACT.Copy).then_inc(w_hi_done, 1)
                    if j < 8 and j % 2 == 0:
                        for ft in range(2):
                            act.wait_ge(red_done, e * 16 + 4 + 2 * j + ft + 1)
                            act.wait_ge(hm_done, e * 8 + j + 2 - 1 + 1)
                            act.activation(sg[:, ft, :], gr[:, ft, :], ACT.Silu).then_inc(silu_done, 1)
                    elif j < 8:
                        for ft in range(2):
                            act.wait_ge(hm_done, e * 8 + 2 + (j - 1) + ft + 1)
                            act.activation(hid[:, j - 1 + ft, 0:TOK], hm[:, ft, :], ACT.Copy).then_inc(hhi_done, 1)
                    if j == 7 and not last:
                        turned_out(e + 1)
                    if j >= 8:
                        dc = j - 8
                        bank = pb[4 + dc % 2]
                        act.wait_ge(tile_done, e * 24 + 2 + 2 * j + 2)
                        if dc == 0:
                            act.wait_ge(cur_ready, e + 1)
                        act.wait_ge(yp_done, e * 4 + dc + 1 - 0)
                        act.activation(tp[:, dc % 2, :], bank[64:P, CW:2 * CW], ACT.Copy).then_inc(tp_done, 1)
                        act.activation(ye_s[:, dc * CW:(dc + 1) * CW], bank[:, 0:CW], ACT.Copy,
                                       scale=gcur_s[:, 0:1]).then_inc(ys_done, 1)

            turned_out(0)
            with act.Fori(0, NE - 1) as e:
                expert(e, False)
            expert(NE - 1, True)

            for t in range(NT):
                act.wait_ge(y_in[t % 2], 16 * (t // 2 + 1))
                act.activation(junk[:, :], yin[:, t % 2, :], ACT.Square, accum_out=small[:, 0, t:t + 1]
                               ).then_inc(fss, 1)
                act.wait_ge(fms, t + 1)
                act.activation(small[:, 2, t:t + 1], small[:, 1, t:t + 1], ACT.Sqrt).then_inc(frms, 1)

        @block.vector
        def _(dve):
            own = Order(dve, own_dve)
            tt, ts, stt = dve.tensor_tensor, dve.tensor_scalar, dve.scalar_tensor_tensor

            def split(g):
                dve.wait_ge(w_hi_done, g + 1)
                tt(wlo[:, g % 2, :, :], wraw[:, g % 2, :].rearrange("p (k n) -> p k n", k=KT),
                   whi[:, g % 2, :, :].bitcast(F32), ALU.subtract).then_inc(w_lo_done, 1)

            def end():
                dve.memset(mark[0:1, 8:9], 0.0).then_inc(phase_dve, 1)

            own.link(dve.memset(mark[0:1, :], 0.0))
            dve.wait_ge(par_in, 16)
            lam4 = p_("lam").rearrange("p (i j) -> p i j", i=4)
            own.link(tt(conv_acc[:, 0:64], lam4[:, 0, :], lam4[:, 1, :], ALU.mult))
            own.link(tt(conv_acc[:, 64:128], lam4[:, 2, :], lam4[:, 3, :], ALU.mult))
            own.link(dve.tensor_reduce(lamt[:, 0:2], conv_acc[:, 0:128].rearrange("p (i j) -> p i j", i=2), AX.X,
                                       ALU.add))
            own.link(ts(lamt[:, 8:9], p_("sub_g"), 1.0 - LAM_INIT, None, ALU.mult))
            dve.wait_ge(own_act, 2)
            own.link(tt(lamt[:, 4:5], lamt[:, 2:3], lamt[:, 3:4], ALU.subtract))
            own.link(ts(lamt[:, 5:6], lamt[:, 4:5], LAM_INIT, None, ALU.add))
            own.link(ts(stat[:, 1, :], stat[:, 0, :], -1.0, None, ALU.mult))
            split(0)
            for s, (t0, nt, blocks, cap) in enumerate(SEQS):
                ph = 7 * s
                L = nt * P
                if s:
                    phase(dve, ph, phase_dve)
                own.step(dve.memset(xbc[:, :, 0:2], 0.0))
                own.link(dve.memset(xbc[:, :, 2 + L:4 + L], 0.0))
                dve.wait_ge(gain_in, 16 * (2 * s + 1))
                for b in blocks:
                    for j in range(TPB):
                        t = TPB * b + j
                        dve.wait_ge(ss_done, t + 1)
                        ts(small[:, 1, t:t + 1], small[:, 0, t:t + 1], 1.0 / D, EPS, ALU.mult, ALU.add
                           ).then_inc(ms_done, 1)
                        dve.wait_ge(rms_done, t + 1)
                        own.link(dve.reciprocal(small[:, 3, t:t + 1], small[:, 2, t:t + 1]))
                        stt(out=xin[:, t % 2, :], in0=xin[:, t % 2, :], scalar=small[:, 3, t:t + 1], in1=gain[:, :],
                            op0=ALU.mult, op1=ALU.mult).then_inc(hn_done, 1)
                        for q in range(2):
                            dve.wait_ge(ht_hi_done, 2 * t + q + 1)
                            sl = (slice(None), slice(4 * q, 4 * q + 4), slice(j * P, (j + 1) * P))
                            tt(ht_lo[sl], pb[6 + q][:, :].rearrange("p (k n) -> p k n", k=4),
                               ht_hi[sl].bitcast(F32), ALU.subtract).then_inc(ht_lo_done, 1)
                    tok = block_tile(b) * P
                    dve.wait_ge(rope_in, 32 * (b + 1))

                    def second_step(m):
                        r = NR * b + min(m - 8, 12)
                        st = stage[:, r % 2, :]
                        bank = pb[4 + r % 2]
                        if m < 16:
                            if r % NR == 0 and b:
                                for i in range(2):
                                    dve.wait_ge(z_out[i], 16 * 2 * b)
                            if r:
                                dve.wait_ge(rot_out, r)
                            dve.wait_ge(col_out, NM * b + m + 1)
                            own.step(tt(tmp[:, 0, :], st, cos_t[:, :], ALU.mult))
                            dve.wait_ge(turn_done, r + 1)
                            own.link(tt(tmp[:, 1, :], bank[:, :], sin_t[:, :], ALU.mult))
                            dst = (qT if m < 12 else kT)[:, (m - 8) % 4, tok:tok + BLK]
                            tt(dst, tmp[:, 0, :], tmp[:, 1, :], ALU.add).then_inc(rot_out, 1)
                        elif m < 20:
                            dve.wait_ge(turn_done, r + 1)
                            h = m - 16
                            dve.tensor_copy(v[:, block_tile(b):block_tile(b) + TPB, h * P:(h + 1) * P],
                                            bank[:, :].rearrange("p (t n) -> p t n", t=TPB)).then_inc(rot_out, 1)
                        else:
                            dve.wait_ge(turn_done, r + 1)
                            i = block_tile(b)
                            dve.tensor_copy(
                                dts[:, 6, 16 * i:16 * (i + TPB)].rearrange("p (t n) -> p t n", t=TPB),
                                bank[:, :].rearrange("p (t n) -> p t n", t=TPB)[:, :, 112:128]).then_inc(rot_out, 1)

                    for m in range(NM):
                        if m % 2 == 0:
                            split(FIRST_CHUNK[b] + m // 2 + 1)
                        if 9 <= m < 21:
                            second_step(m - 1)
                        if b == blocks[-1] and 8 <= m < 16:
                            i = m - 8
                            if i == 0:
                                dve.wait_ge(col_out, NM * b + 8)
                            else:
                                dve.wait_ge(conv_act, 8 * s + i)
                            own.link(ts(conv_acc[:, 0:L], xbc[:, i, 0:L], p_("conv_w", 5 * i), None, ALU.mult))
                            for w in range(1, 5):
                                ins = stt(out=conv_acc[:, 0:L], in0=xbc[:, i, w:w + L], scalar=p_("conv_w", 5 * i + w),
                                          in1=conv_acc[:, 0:L], op0=ALU.mult, op1=ALU.add)
                                if w < 4:
                                    own.link(ins)
                                else:
                                    ins.then_inc(conv_done, 1)
                    second_step(24)
                end()

                phase(dve, ph + 1, phase_dve)
                nh = L // 512

                def weights(u):
                    U = 4 * t0 + u
                    sl = u % 2
                    dve.wait_ge(exp_done, 2 * U + 2)
                    if nh == 2:
                        own.link(dve.tensor_reduce(ostat[:, 2, 4 * sl:4 * sl + 2],
                                                   ostat[:, 1, 4 * sl:4 * sl + 4].rearrange("p (c q) -> p c q", c=2),
                                                   AX.X, ALU.add))
                        own.link(dve.reciprocal(ostat[:, 2, 4 * sl + 2:4 * sl + 4], ostat[:, 2, 4 * sl:4 * sl + 2]))
                    else:
                        own.link(dve.reciprocal(ostat[:, 2, 4 * sl + 2:4 * sl + 4], ostat[:, 1, 4 * sl:4 * sl + 3:2]))
                    own.link(ts(ostat[:, 2, 4 * sl + 3:4 * sl + 4], ostat[:, 2, 4 * sl + 3:4 * sl + 4],
                                lamt[:, 5:6], None, ALU.mult))
                    own.link(ts(pr[:, sl, 1, 0:L], pr[:, sl, 1, 0:L], ostat[:, 2, 4 * sl + 3:4 * sl + 4], None,
                                ALU.mult))
                    if U >= 2:
                        dve.wait_ge(wt_out, (64 if s else 0) + (nt // 4) * max(u - 1, 0))
                    stt(out=wgt[:, sl, 0:L], in0=pr[:, sl, 0, 0:L], scalar=ostat[:, 2, 4 * sl + 2:4 * sl + 3],
                        in1=pr[:, sl, 1, 0:L], op0=ALU.mult, op1=ALU.subtract).then_inc(wg_done, 1)

                for u in range(4 * nt + 1):
                    U = 4 * t0 + u
                    if u < 4 * nt:
                        for h in range(2):
                            dve.wait_ge(sc_done, 2 * U + h + 1)
                            src = pb[2 * h][:, :]
                            col = 2 * (u % 2) + h
                            if nh == 2:
                                for q in range(2):
                                    own.step(dve.tensor_reduce(small[:, 4 + q, col:col + 1], pb[2 * h + q][:, :], AX.X,
                                                               ALU.max))
                                own.wait()
                                own.link(tt(small[:, 4, col:col + 1], small[:, 4, col:col + 1],
                                            small[:, 5, col:col + 1], ALU.max))
                            else:
                                own.link(dve.tensor_reduce(small[:, 4, col:col + 1], src, AX.X, ALU.max))
                            ts(ostat[:, 0, col:col + 1], small[:, 4, col:col + 1], -1.0, None, ALU.mult
                               ).then_inc(mx_done, 1)
                    if u >= 1:
                        weights(u - 1)
                dve.wait_ge(av_out, t0 + nt)
                ts(dts[:, 1, 0:4 * nt], dts[:, 0, 0:4 * nt], 1.0 / P, EPS, ALU.mult, ALU.add).then_inc(osum_done, 1)
                dve.wait_ge(orms_done, s + 1)
                own.link(dve.reciprocal(dts[:, 3, 0:4 * nt], dts[:, 2, 0:4 * nt]))
                for i in range(nt):
                    tt(oatt[:, i, :].rearrange("p (h n) -> p h n", h=4),
                       oatt[:, i, :].rearrange("p (h n) -> p h n", h=4),
                       dts[:, 3, 4 * i:4 * i + 4].unsqueeze(2).to_broadcast([P, 4, P]), ALU.mult
                       ).then_inc(on_done, 1)
                end()

                phase(dve, ph + 2, phase_dve)
                W = 16 * nt
                sl = slice(0, W)

                def rep(ap):
                    return ap.unsqueeze(1).to_broadcast([P, nt, 16])

                def grid(i):
                    return dts[:, i, sl].rearrange("p (t n) -> p t n", n=16)

                own.link(tt(grid(5), grid(6), rep(p_("dt_bias")), ALU.add))
                own.link(ts(dts[:, 1, sl], dts[:, 5, sl], -1.0, None, ALU.mult))
                tt(dts[:, 1, sl], dts[:, 5, sl], dts[:, 1, sl], ALU.min).then_inc(dt_v, 1)
                dve.wait_ge(dt_a, 3 * s + 1)
                ts(dts[:, 3, sl], dts[:, 2, sl], 1.0, None, ALU.add).then_inc(dt_v, 1)
                dve.wait_ge(dt_v, 4 * s + 2)
                own.step(ts(dts[:, 8, sl], dts[:, 3, sl], -1.0, None, ALU.add))
                own.link(dve.reciprocal(dts[:, 9, sl], dts[:, 3, sl]))
                own.link(tt(dts[:, 8, sl], dts[:, 2, sl], dts[:, 8, sl], ALU.subtract))
                own.link(tt(dts[:, 8, sl], dts[:, 8, sl], dts[:, 9, sl], ALU.mult))
                dve.wait_ge(dt_a, 3 * s + 2)
                own.link(tt(dts[:, 8, sl], dts[:, 8, sl], dts[:, 4, sl], ALU.add))
                own.link(ts(dts[:, 5, sl], dts[:, 5, sl], 0.0, None, ALU.max))
                own.link(tt(dts[:, 5, sl], dts[:, 5, sl], dts[:, 8, sl], ALU.add))
                tt(grid(6), grid(5), rep(stat[:, 1, :]), ALU.mult).then_inc(dt_v, 1)
                dve.wait_ge(cs_done, s + 1)
                cs = pb[7]
                own.step(ts(grid(7)[:, :, 0:8], cs[:, 0:8 * nt].rearrange("p (t n) -> p t n", n=8), -1.0, None,
                            ALU.mult))
                own.step(ts(grid(7)[:, :, 8:16], cs[:, 64:64 + 8 * nt].rearrange("p (t n) -> p t n", n=8), -1.0, None,
                            ALU.mult))
                own.link(dve.tensor_copy(dts[:, 3, sl], cs[:, 128:128 + W]))
                tt(dts[:, 4, sl], dts[:, 3, sl], dts[:, 7, sl], ALU.add).then_inc(dt_v, 1)
                for cc in range(nt):
                    k = 8 * s + cc
                    dve.wait_ge(xt_done, k + 1)
                    for d in range(2):
                        tt(xf[:, cc, d, :].rearrange("p (h q) -> p h q", h=SH),
                           pb[0 if cc % 2 == 0 else 2][:, :].rearrange("p (h q) -> p h q", h=SH),
                           dts[:, 5, cc * 16 + 8 * d:cc * 16 + 8 * d + 8].unsqueeze(2).to_broadcast([P, SH, 64]),
                           ALU.mult).then_inc(xf_done, 1)
                dve.wait_ge(st_out, 2 * (8 * s + nt))
                dve.wait_ge(dt_a, 3 * s + 3)
                for cc in range(1, nt - 1):
                    own.link(tt(scan_t[0][:, :].rearrange("p (h q) -> p h q", h=SH),
                                state[0][:, cc, :].rearrange("p (h q) -> p h q", h=SH),
                                dts[:, 8, cc * 16:cc * 16 + 8].unsqueeze(2).to_broadcast([P, SH, 64]), ALU.mult))
                    own.link(tt(state[0][:, cc + 1, :], state[0][:, cc + 1, :], scan_t[0][:, :], ALU.add))
                end()

                phase(dve, ph + 3, phase_dve)
                for n4 in range(4 * nt):
                    n = 32 * s + n4
                    cc, g, d = n4 // 4, (n4 // 2) % 2, n4 % 2
                    k = 8 * s + cc
                    dve.wait_ge(row_done, n + 1)
                    dve.wait_ge(e_done, n + 1)
                    if n >= 2:
                        dve.wait_ge(l_done, n - 1)
                    tt(dr[:, n % 2, :].rearrange("p (h l) -> p h l", h=4),
                       pb[2 + n % 2][:, :].rearrange("p (h l) -> p h l", h=4),
                       c("neg_b" if d else "neg_f").unsqueeze(1).to_broadcast([P, 4, P]), ALU.add
                       ).then_inc(d_done, 1)
                    dve.wait_ge(l_done, n + 1)
                    dve.wait_ge(cb_done, k + 1)
                    if n >= 2:
                        dve.wait_ge(yh_done, n - 1)
                    tt(mr[:, n % 2, :].rearrange("p (h l) -> p h l", h=4),
                       lr[:, n % 2, :].rearrange("p (h l) -> p h l", h=4),
                       pb[cc % 2][:, g * P:(g + 1) * P].unsqueeze(1).to_broadcast([P, 4, P]), ALU.mult
                       ).then_inc(m_done, 1)
                    if n4 % 4 == 3:
                        tk = slice(2 + cc * P, 2 + (cc + 1) * P)
                        dve.wait_ge(yh_done, n + 1)
                        for jj in range(4):
                            own.step(stt(out=xbc[:, jj, tk], in0=xbc[:, jj, tk], scalar=p_("d_skip", jj),
                                         in1=pb[4 + cc % 2][:, jj * P:(jj + 1) * P], op0=ALU.mult, op1=ALU.add))
                        own.wait()
                        dve.wait_ge(z_in[k % 2], 16 * (k // 2 + 1))
                        tt(xbc[:, 0:4, tk], xbc[:, 0:4, tk],
                           zin[:, k % 2, :].rearrange("p (j l) -> p j l", j=4), ALU.mult).then_inc(z_used, 1)
                end()

                phase(dve, ph + 4, phase_dve)
                for q in range(2 * (L // BLK)):
                    N = (4 if s else 0) + q
                    hf, g = q // 2, q % 2
                    dve.wait_ge(nsum_done, N + 1)
                    if q:
                        dve.wait_ge(nrms_done, N)
                    ts(rs[:, 1, :], pb[6 + q % 2][:, :], 1.0 / 256, EPS, ALU.mult, ALU.add).then_inc(nms_done, 1)
                    dve.wait_ge(nrms_done, N + 1)
                    own.link(dve.reciprocal(rs[:, 0, :], rs[:, 0, :]))
                    for i in range(2):
                        a = xbc[:, 2 * g + i, 2 + hf * BLK:2 + (hf + 1) * BLK]
                        stt(out=a, in0=a, scalar=p_("ssm_g", 2 * g + i), in1=rs[:, 0, :], op0=ALU.mult, op1=ALU.mult
                            ).then_inc(nrm_done, 1)
                for k in range(KT):
                    src = qT[:, k, 0:L] if k < 4 else xbc[:, k - 4, 2:2 + L]
                    dve.wait_ge(mix_hi_done, KT * s + k + 1)
                    tt(mix_lo[:, k, 0:L], src, mix_hi[:, k, 0:L].bitcast(F32), ALU.subtract
                       ).then_inc(mix_lo_done, 1)
                end()

                phase(dve, ph + 5, phase_dve)
                dve.wait_ge(x2_in, 16 * (s + 1))
                for jo in range(4):
                    split(FIRST_OUT_CHUNK[s] + jo + 1)
                    for i in range(nt):
                        u = nt * jo + i
                        dve.wait_ge(op_done, 4 * t0 + u + 1)
                        a = x2[:, i, jo * CW:(jo + 1) * CW]
                        tt(a, a, pb[u % 4][:, 0:CW], ALU.add).then_inc(op_out, 1)
                dve.wait_ge(ss2_done, t0 + nt)
                ts(small[:, 1, 0:nt], small[:, 0, 0:nt], 1.0 / D, EPS, ALU.mult, ALU.add).then_inc(rms2_done, 1)
                dve.wait_ge(rms2_done, 2 * s + 2)
                own.link(dve.reciprocal(small[:, 3, 0:nt], small[:, 2, 0:nt]))
                dve.wait_ge(gain_in, 16 * (2 * s + 2))
                for i in range(nt):
                    t = t0 + i
                    if t >= 2:
                        dve.wait_ge(h2_out[t % 2], 16 * (t // 2))
                        dve.wait_ge(h2_turned, 2 * (t - 1))
                    stt(out=h2[:, t % 2, :], in0=x2[:, i, :], scalar=small[:, 3, i:i + 1], in1=gain[:, :],
                        op0=ALU.mult, op1=ALU.mult).then_inc(h2_done, 1)
                dve.wait_ge(lg_done, t0 + nt)
                end()

                phase(dve, ph + 6, phase_dve)
                lg = pb[5][:, sl].rearrange("p (t n) -> p t n", n=NE)
                af = aff[:, sl].rearrange("p (t n) -> p t n", n=NE)
                own.link(dve.tensor_reduce(aff2[:, 0:nt], lg, AX.X, ALU.max))
                tt(af, lg, aff2[:, 0:nt].unsqueeze(2).to_broadcast([P, nt, NE]), ALU.subtract).then_inc(rt_v, 1)
                dve.wait_ge(rt_a, s + 1)
                own.link(dve.tensor_reduce(aff2[:, 16:16 + nt], af, AX.X, ALU.add))
                own.link(dve.reciprocal(aff2[:, 32:32 + nt], aff2[:, 16:16 + nt]))
                tt(af, af, aff2[:, 32:32 + nt].unsqueeze(2).to_broadcast([P, nt, NE]), ALU.mult).then_inc(rt_v, 1)
                dve.wait_ge(rt_p, 2 * s + 1)
                for q in range(L // 512):
                    own.step(dve.tensor_copy(affT[:, q * 512:(q + 1) * 512], pb[6 + q][0:NE, :]))
                own.wait()
                for r in range(cap // 8):
                    tv, ti = topv[:, 8 * r:8 * r + 8], topi[:, 8 * r:8 * r + 8]
                    own.link(dve.max(tv, affT[:, 0:L]))
                    own.link(dve.max_index(ti, tv, affT[:, 0:L]))
                    own.link(dve.match_replace(affT[:, 0:L], tv, affT[:, 0:L], -1.0))
                own.link(dve.tensor_copy(topf[:, 0:cap], topi[:, 0:cap]))
                own.link(ts(topf[:, 0:cap], topf[:, 0:cap], float(t0 * P), None, ALU.add))
                dve.memset(mark[0:1, 9:10], 0.0).then_inc(rt_v, 1)
                dve.wait_ge(rt_p, 2 * s + 2)
                own.step(dve.tensor_copy((gate_s if s == 0 else gate_p)[:, :], pb[4][0:cap, 0:NE]))
                own.link(dve.tensor_copy((idx_s if s == 0 else idx_p)[:, :], pb[4][0:cap, 16:16 + NE]))
                dve.memset(mark[0:1, 9:10], 0.0).then_inc(rt_v, 1)
                end()

            phase(dve, 14, phase_dve)
            dve.memset(mark[0:1, 10:11], 0.0).then_inc(tile_done, 2)
            dve.memset(mark[0:1, 11:12], 0.0).then_inc(red_done, 4)
            dve.memset(mark[0:1, 12:13], 0.0).then_inc(hm_done, 2)
            dve.memset(mark[0:1, 13:14], 0.0).then_inc(yp_done, 2)

            def next_indices(e1):
                dve.tensor_copy(gi_s[:, :], idx_s[:, bass.ds(e1, 1)])
                dve.tensor_copy(gi_p[:, :], idx_p[:, bass.ds(e1, 1)]).then_inc(idx_ready, 1)

            def turned_out(n):
                for kk in range(4):
                    dve.wait_ge(xhi_done, n * 4 + kk + 1)
                    tt(xT[:, 2 * kk:2 * kk + 2, TOK:2 * TOK],
                       pb[6 + kk % 2][:, 0:2 * TOK].rearrange("p (k n) -> p k n", k=2),
                       xT[:, 2 * kk:2 * kk + 2, 0:TOK].bitcast(F32), ALU.subtract).then_inc(xlo_done, 1)

            def expert(e, last):
                for j in range(ECH):
                    if j == 0 and not last:
                        dve.wait_ge(xs_in, e * 16 + 16)
                        dve.wait_ge(xp_in, e * 16 + 16)
                        next_indices(e + 1)
                    if j == 1:
                        dve.wait_ge(scattered, e + 1)
                        dve.tensor_copy(gcur_s[:, :], gate_s[:, bass.ds(e, 1)])
                        dve.tensor_copy(gcur_p[:, :], gate_p[:, bass.ds(e, 1)])
                        dve.tensor_copy(si_s[:, :], idx_s[:, bass.ds(e, 1)])
                        dve.tensor_copy(si_p[:, :], idx_p[:, bass.ds(e, 1)]).then_inc(cur_ready, 1)
                    if not (last and j == ECH - 1):
                        g = MOE_CHUNK + j + 1
                        dve.wait_ge(w_hi_done, e * ECH + g + 1)
                        tt(wlo[:, g % 2, :, :], wraw[:, g % 2, :].rearrange("p (k n) -> p k n", k=KT),
                           whi[:, g % 2, :, :].bitcast(F32), ALU.subtract).then_inc(w_lo_done, 1)
                    if j < 8:
                        for ft in range(2):
                            dve.wait_ge(tile_done, e * 24 + 2 + 2 * j + ft + 1)
                            dve.tensor_reduce((ur if j % 2 else gr)[:, ft, :],
                                              pb[2 * (j % 2) + ft][:, 0:2 * TOK].rearrange("p (a n) -> p n a", a=2),
                                              AX.X, ALU.add).then_inc(red_done, 1)
                    if j < 8 and j % 2:
                        for ft in range(2):
                            dve.wait_ge(silu_done, e * 8 + (j - 1) + ft + 1)
                            dve.wait_ge(red_done, e * 16 + 4 + 2 * j + ft + 1)
                            if j > 1:
                                dve.wait_ge(hlo_done, e * 8 + (j - 3) + ft + 1)
                            tt(hm[:, ft, :], sg[:, ft, :], ur[:, ft, :], ALU.mult).then_inc(hm_done, 1)
                        for ft in range(2):
                            f = j - 1 + ft
                            dve.wait_ge(hhi_done, e * 8 + f + 1)
                            tt(hid[:, f, 256:384], hm[:, ft, 0:P], hid[:, f, 0:P].bitcast(F32), ALU.subtract)
                            tt(hid[:, f, 192:256], hm[:, ft, P:TOK], hid[:, f, P:TOK].bitcast(F32), ALU.subtract
                               ).then_inc(hlo_done, 1)
                    if j == 7 and not last:
                        turned_out(e + 1)
                    if j >= 8:
                        dc = j - 8
                        bank = pb[4 + dc % 2]
                        dve.wait_ge(tp_done, e * 4 + dc + 1)
                        dve.wait_ge(ys_done, e * 4 + dc + 1)
                        a = ye_p[:, dc * CW:(dc + 1) * CW]
                        own_tp = tt(a, bank[0:64, CW:2 * CW], tp[:, dc % 2, :], ALU.add)
                        own_tp.then_inc(half_added, 1)
                        dve.wait_ge(half_added, e * 4 + dc + 1)
                        ts(a, a, gcur_p[:, 0:1], None, ALU.mult).then_inc(yp_done, 1)

            next_indices(0)
            turned_out(0)
            with dve.Fori(0, NE - 1) as e:
                expert(e, False)
            expert(NE - 1, True)

            dve.wait_ge(gain_in, 16 * 5)
            for t in range(NT):
                dve.wait_ge(fss, t + 1)
                ts(small[:, 1, t:t + 1], small[:, 0, t:t + 1], 1.0 / D, EPS, ALU.mult, ALU.add).then_inc(fms, 1)
                dve.wait_ge(frms, t + 1)
                own.link(dve.reciprocal(small[:, 3, t:t + 1], small[:, 2, t:t + 1]))
                if t >= 2:
                    dve.wait_ge(y_out[t % 2], 16 * (t // 2))
                stt(out=yout[:, t % 2, :], in0=yin[:, t % 2, :], scalar=small[:, 3, t:t + 1], in1=gain[:, :],
                    op0=ALU.mult, op1=ALU.mult).then_inc(fy, 1)

        @block.tensor
        def _(pe):
            mm = pe.matmul
            pe.wait_ge(cst_in, 16)
            pe.wait_ge(par_in, 16)

            def split3(out, wh, wl, xh, xl, first, final, **kw):
                mm(out, wh, xh, start=first, stop=False, **kw)
                mm(out, wh, xl, start=False, stop=False, **kw)
                return mm(out, wl, xh, start=False, stop=final, **kw)

            for s, (t0, nt, blocks, cap) in enumerate(SEQS):
                ph = 7 * s
                L = nt * P
                if s:
                    phase(pe, ph)
                for b in blocks:
                    for j in range(TPB):
                        t = TPB * b + j
                        pe.wait_ge(hn_done, t + 1)
                        if t:
                            pe.wait_ge(ht_lo_done, 2 * t)
                        for q in range(2):
                            for i in range(4):
                                k = 4 * q + i
                                last = pe.transpose(pb[6 + q][:, i * P:(i + 1) * P],
                                                    xin[:, t % 2, k * P:(k + 1) * P], ident)
                            last.then_inc(h_turned, 1)
                    pe.wait_ge(ht_lo_done, 2 * TPB * (b + 1))

                    def second_step(m):
                        r = NR * b + min(m - 8, 12)
                        pe.wait_ge(col_out, NM * b + m + 1)
                        if r >= 2:
                            pe.wait_ge(rot_out, r - 1)
                        bank = pb[4 + r % 2]
                        if m < 16:
                            mm(bank[:, :], c("rot"), stage[:, r % 2, :], start=True, stop=True
                               ).then_inc(turn_done, 1)
                        else:
                            for i in range(TPB):
                                last = pe.transpose(bank[:, i * P:(i + 1) * P], stage[:, r % 2, i * P:(i + 1) * P],
                                                    ident)
                            last.then_inc(turn_done, 1)

                    for m in range(NM):
                        n = NM * b + m
                        g = FIRST_CHUNK[b] + m // 2
                        if m % 2 == 0:
                            pe.wait_ge(w_lo_done, g + 1)
                        if n >= 4:
                            pe.wait_ge(col_out, n - (3 if m >= 4 else m))
                        cols = slice(P, 2 * P) if (m % 2 or m == 24) else slice(0, P)
                        for k in range(KT):
                            last = split3(pb[m % 4][:, :], whi[:, g % 2, k, cols], wlo[:, g % 2, k, cols],
                                          ht_hi[:, k, :], ht_lo[:, k, :], k == 0, k == KT - 1)
                        last.then_inc(col_done, 1)
                        if 9 <= m < 21:
                            second_step(m - 1)
                    second_step(24)

                phase(pe, ph + 1)
                nh = L // 512

                def apply(w):
                    W = 4 * t0 + w
                    i, h = w // 4, w % 4
                    pe.wait_ge(wg_done, W + 1)
                    for q in range(nt // 4):
                        if W >= 1:
                            pe.wait_ge(wt_out, (64 if s else 0) + (nt // 4) * w if w else (64 if s else 0))
                        for kk in range(4):
                            last = pe.transpose(pb[4 + q][:, kk * P:(kk + 1) * P],
                                                wgt[:, w % 2, (4 * q + kk) * P:(4 * q + kk + 1) * P], ident)
                        last.then_inc(wt_done, 1)
                    pe.wait_ge(wt_out, (64 if s else 0) + (nt // 4) * (w + 1))
                    if h == 0 and i >= 2:
                        pe.wait_ge(av_out, t0 + i - 1)
                    for kk in range(nt):
                        last = mm(pb[6 + i % 2][:, h * P:(h + 1) * P], wgtT[:, w % 2, kk * P:(kk + 1) * P],
                                  v[:, kk, h * P:(h + 1) * P], start=(kk == 0), stop=(kk == nt - 1))
                    last.then_inc(av_done, 1)

                for u in range(4 * nt + 1):
                    U = 4 * t0 + u
                    if u < 4 * nt:
                        i, h = u // 4, u % 4
                        for hf in range(2):
                            if u:
                                pe.wait_ge(exp_done, 2 * (U - 1) + hf + 1)
                            rows = slice(64 * hf, 64 * hf + 64)
                            for q in range(nh):
                                last = mm(pb[2 * hf + q][:, :], qT[rows, h, i * P:(i + 1) * P],
                                          kT[rows, h, q * 512:(q + 1) * 512], start=True, stop=True)
                            last.then_inc(sc_done, 1)
                    if u >= 1:
                        apply(u - 1)
                for i in range(nt):
                    pe.wait_ge(on_done, t0 + i + 1)
                    if i >= 2:
                        pe.wait_ge(ot_out, t0 + i - 1)
                    for h in range(4):
                        last = pe.transpose(pb[i % 2][:, h * P:(h + 1) * P], oatt[:, i, h * P:(h + 1) * P], ident)
                    last.then_inc(ot_done, 1)

                phase(pe, ph + 2)
                a3 = dts[:, 6, 0:16 * nt].rearrange("p (t n) -> p t n", n=16)
                pe.wait_ge(dt_v, 4 * s + 3)
                mm(pb[7][:, 0:8 * nt], c("cum_f"), a3[:, :, 0:8], start=True, stop=True)
                mm(pb[7][:, 64:64 + 8 * nt], c("cum_b"), a3[:, :, 8:16], start=True, stop=True)
                mm(pb[7][:, 128:128 + 16 * nt], c("ones"), dts[:, 6, 0:16 * nt], start=True, stop=True
                   ).then_inc(cs_done, 1)
                for cc in range(nt + 1):
                    k = 8 * s + cc
                    if cc < nt:
                        tk = slice(2 + cc * P, 2 + (cc + 1) * P)
                        if cc >= 2:
                            pe.wait_ge(xf_done, 2 * (k - 1))
                            pe.wait_ge(bt_out, k - 1)
                        for i in range(4):
                            last = pe.transpose(pb[0 if cc % 2 == 0 else 2][:, i * P:(i + 1) * P], xbc[:, i, tk], ident)
                        last.then_inc(xt_done, 1)
                        for i in range(2):
                            last = pe.transpose(pb[1 if cc % 2 == 0 else 3][:, i * P:(i + 1) * P], xbc[:, 4 + i, tk],
                                                ident)
                        last.then_inc(bt_done, 1)
                    if cc >= 1:
                        k -= 1
                        c1 = cc - 1
                        pe.wait_ge(bt_out, k + 1)
                        for d in range(2):
                            pe.wait_ge(xs_done, 2 * k + d + 1)
                            if c1:
                                pe.wait_ge(st_out, 2 * k + d - 1)
                            for g in range(2):
                                mm(pb[4 + d][:, g * 256:(g + 1) * 256], btok[:, c1 % 2, g * P:(g + 1) * P],
                                   xs[:, c1 % 2, d, g * 256:(g + 1) * 256], start=True, stop=True
                                   ).then_inc(st_done, 1)

                phase(pe, ph + 3)

                def rows_of(n4):
                    n = 32 * s + n4
                    cc, g, d = n4 // 4, (n4 // 2) % 2, n4 % 2
                    if n4 >= 2:
                        pe.wait_ge(d_done, n - 1)
                    for hh in range(4):
                        col = cc * 16 + 8 * d + 4 * g + hh
                        last = mm(pb[2 + n % 2][:, hh * P:(hh + 1) * P],
                                  dts[:, 6, col:col + 1].to_broadcast([P, P]), c("cum_b" if d else "cum_f"),
                                  start=True, stop=True)
                    last.then_inc(row_done, 1)

                rows_of(0)
                for n4 in range(4 * nt):
                    n = 32 * s + n4
                    cc, g, d = n4 // 4, (n4 // 2) % 2, n4 % 2
                    k = 8 * s + cc
                    if n4 % 4 == 0:
                        tk = slice(2 + cc * P, 2 + (cc + 1) * P)
                        if cc >= 2:
                            pe.wait_ge(m_done, n - 4)
                        for gg in range(2):
                            last = mm(pb[cc % 2][:, gg * P:(gg + 1) * P], xbc[:, 4 + gg, tk], xbc[:, 6 + gg, tk],
                                      start=True, stop=True)
                        last.then_inc(cb_done, 1)
                        if cc >= 2:
                            pe.wait_ge(z_used, k - 1)
                    if n4 + 1 < 4 * nt:
                        rows_of(n4 + 1)
                    pe.wait_ge(m_done, n + 1)
                    pe.wait_ge(c_done, n + 1)
                    ybank = pb[4 + cc % 2]
                    for hh in range(4):
                        h = 4 * g + hh
                        out = ybank[64 * (h % 2):64 * (h % 2) + 64, (h // 2) * P:(h // 2 + 1) * P]
                        last = mm(out, xf[:, cc, d, h * 64:(h + 1) * 64], mr[:, n % 2, hh * P:(hh + 1) * P],
                                  start=(g == 0 and d == 0 and hh < 2), stop=(d == 1), skip_group_check=True)
                        if cc > 0 if d == 0 else cc < nt - 1:
                            last = mm(out, state[d][:, cc, h * 64:(h + 1) * 64], cr[:, n % 2, hh * P:(hh + 1) * P],
                                      start=False, stop=(d == 1), skip_group_check=True)
                    last.then_inc(yh_done, 1)

                phase(pe, ph + 4)
                for q in range(2 * (L // BLK)):
                    N = (4 if s else 0) + q
                    pe.wait_ge(sq_done, 2 * (N + 1))
                    if q >= 2:
                        pe.wait_ge(nms_done, N - 1)
                    for i in range(2):
                        last = mm(pb[6 + q % 2][:, :], c("ones"), sq[:, i, :], start=(i == 0), stop=(i == 1))
                    last.then_inc(nsum_done, 1)

                phase(pe, ph + 5)
                for jo in range(4):
                    g = FIRST_OUT_CHUNK[s] + jo
                    pe.wait_ge(w_lo_done, g + 1)
                    for i in range(nt):
                        u = nt * jo + i
                        if u >= 4:
                            pe.wait_ge(op_out, 4 * t0 + u - 3)
                        for k in range(KT):
                            last = split3(pb[u % 4][:, 0:CW], mix_hi[:, k, i * P:(i + 1) * P],
                                          mix_lo[:, k, i * P:(i + 1) * P], whi[:, g % 2, k, :], wlo[:, g % 2, k, :],
                                          k == 0, k == KT - 1)
                        last.then_inc(op_done, 1)
                for i in range(nt + 1):
                    t = t0 + i
                    if i < nt:
                        pe.wait_ge(h2_done, t + 1)
                        if i:
                            pe.wait_ge(h2T_out, 2 * t)
                        for q in range(2):
                            for kk in range(4):
                                k = 4 * q + kk
                                last = pe.transpose(pb[6 + q][:, kk * P:(kk + 1) * P], h2[:, t % 2, k * P:(k + 1) * P],
                                                    ident)
                            last.then_inc(h2_turned, 1)
                    if i >= 1:
                        pe.wait_ge(h2T_out, 2 * t)
                        for k in range(KT):
                            last = mm(pb[5][:, (i - 1) * NE:i * NE], h2T[:, (t - 1) % 2, k, :],
                                      p_("router", k * NE, NE), start=(k == 0), stop=(k == KT - 1))
                        last.then_inc(lg_done, 1)

                phase(pe, ph + 6)
                pe.wait_ge(rt_v, 4 * s + 2)
                for i in range(nt):
                    last = pe.transpose(pb[6 + i // 4][0:NE, (i % 4) * P:(i % 4 + 1) * P], aff[:, i * NE:(i + 1) * NE],
                                        ident)
                last.then_inc(rt_p, 1)
                pe.wait_ge(rt_v, 4 * s + 3)
                pe.transpose(pb[4][0:cap, 0:NE], topv[:, 0:cap], ident[0:NE, 0:NE])
                pe.transpose(pb[4][0:cap, 16:16 + NE], topf[:, 0:cap], ident[0:NE, 0:NE]).then_inc(rt_p, 1)

            phase(pe, 14)
            pe.wait_ge(hm_done, 2)

            def turn(n):
                pe.wait_ge(xs_in, n * 16 + 16)
                pe.wait_ge(xp_in, n * 16 + 16)
                for kk in range(4):
                    if kk >= 2:
                        pe.wait_ge(xlo_done, n * 4 + kk - 1)
                    for i in range(2):
                        k = 2 * kk + i
                        bank = pb[6 + kk % 2]
                        pe.transpose(bank[:, i * TOK:i * TOK + P], xe_s[:, k * P:(k + 1) * P], ident)
                        last = pe.transpose(bank[:, i * TOK + P:(i + 1) * TOK], xe_p[:, k * P:(k + 1) * P],
                                            ident[0:64, 0:64])
                    last.then_inc(xturn, 1)

            def expert(e, last_one):
                pe.wait_ge(xlo_done, e * 4 + 4)
                for j in range(8):
                    g = MOE_CHUNK + j
                    pe.wait_ge(w_lo_done, e * ECH + g + 1)
                    for ft in range(2):
                        q = 2 * j + ft
                        pe.wait_ge(red_done, e * 16 + q + 1)
                        bank = pb[2 * (j % 2) + ft]
                        cols = slice(ft * P, (ft + 1) * P)
                        for k in range(KT):
                            mm(bank[:, 0:2 * TOK], whi[:, g % 2, k, cols], xT[:, k, :], start=(k == 0), stop=False)
                            last = mm(bank[:, 0:TOK], wlo[:, g % 2, k, cols], xT[:, k, 0:TOK], start=False,
                                      stop=(k == KT - 1))
                        last.then_inc(tile_done, 1)
                if not last_one:
                    turn(e + 1)
                pe.wait_ge(hlo_done, e * 8 + 8)
                for j in range(8, ECH):
                    g = MOE_CHUNK + j
                    dc = j - 8
                    pe.wait_ge(w_lo_done, e * ECH + g + 1)
                    pe.wait_ge(yp_done, e * 4 + dc + 1)
                    bank = pb[4 + dc % 2]
                    for k in range(KT):
                        last = split3(bank[:, 0:CW], hid[:, k, 0:P], hid[:, k, 256:384], whi[:, g % 2, k, :],
                                      wlo[:, g % 2, k, :], k == 0, k == KT - 1)
                    last.then_inc(tile_done, 1)
                    for k in range(KT):
                        mm(bank[:, CW:2 * CW], hid[:, k, P:256], whi[:, g % 2, k, :], start=(k == 0), stop=False)
                        last = mm(bank[:, CW:2 * CW], hid[:, k, P:256], wlo[:, g % 2, k, :], start=False,
                                  stop=(k == KT - 1))
                    last.then_inc(tile_done, 1)

            turn(0)
            with pe.Fori(0, NE - 1) as e:
                expert(e, False)
            expert(NE - 1, True)


def _chunks(w, cols):
    import numpy as np
    return np.stack([np.ascontiguousarray(w[:, c0:c0 + 256].reshape(8, 128, 256).transpose(1, 0, 2)).reshape(128, 2048)
                     for c0 in cols])


def _shape_constants():
    import numpy as np
    i = np.arange(128)
    ident = np.eye(128, dtype=np.float32)
    cum_f = (i[:, None] <= i[None, :]).astype(np.float32)
    cum_b = (i[:, None] >= i[None, :]).astype(np.float32)
    rot = np.zeros((128, 128), np.float32)
    cos = np.ones((128, 1024), np.float32)
    sin = np.zeros((128, 1024), np.float32)
    inv = np.power(np.float32(500000.0), -np.arange(8, dtype=np.float32) * np.float32(2.0) / np.float32(16))
    ang = np.arange(1024, dtype=np.float32)[None, :] * inv.astype(np.float32)[:, None]
    for half in (0, 64):
        for r in range(8):
            rot[half + 8 + r, half + r] = -1.0
            rot[half + r, half + 8 + r] = 1.0
        for q in (0, 8):
            cos[half + q:half + q + 8] = np.cos(ang)
            sin[half + q:half + q + 8] = np.sin(ang)
    big = np.float32(-1e30)
    consts = np.concatenate([ident, cum_f, cum_b, (1 - cum_f) * big, (1 - cum_b) * big, rot,
                             np.ones((128, 128), np.float32)], 1).astype(np.float32)
    return consts, np.stack([cos, sin])


def kernel(x_prompt, x_sample, norm1_g, w_in, lam_qk, attn_sub_g, conv_w, conv_b, dt_bias, a_log, d_skip, ssm_norm_g,
           w_out, norm2_g, w_router, w_gate, w_up, w_down, final_g):
    import numpy as np
    import concourse.bacc as _bacc
    from concourse import mybir as _mybir
    from concourse.bass_utils import run_bass_kernel_spmd as _run

    A = np.asarray
    x = np.concatenate([A(x_sample)[0], A(x_prompt)[0]], 0)
    wi = A(w_in)[0]
    in_cols = [2048 + 256 * i for i in range(4)] + [256 * i for i in range(8)] + [wi.shape[1] - 256]
    wg, wu, wd = A(w_gate)[0], A(w_up)[0], A(w_down)[0]
    cols = [0, 256, 512, 768]
    moe = np.empty((16 * 12, 128, 2048), wg.dtype)
    for e in range(16):
        moe[12 * e:12 * e + 8:2] = _chunks(wg[e], cols)
        moe[12 * e + 1:12 * e + 8:2] = _chunks(wu[e], cols)
        moe[12 * e + 8:12 * e + 12] = _chunks(wd[e], cols)
    row = lambda a: np.broadcast_to(A(a).reshape(1, -1), (128, A(a).size))
    part = lambda a: A(a).reshape(-1, 128).T
    params = np.concatenate([
        A(conv_w)[0].T.reshape(8, 128, 5).transpose(1, 0, 2).reshape(128, 40), part(conv_b),
        part(np.repeat(A(d_skip)[0], 64)), part(ssm_norm_g), part(attn_sub_g), row(dt_bias), row(a_log), row(lam_qk),
        A(w_router)[0].reshape(8, 128, 16).transpose(1, 0, 2).reshape(128, 128)], 1)
    gains = np.stack([np.broadcast_to(A(g).reshape(1, -1), (128, 1024)) for g in (norm1_g, norm2_g, final_g)])
    consts, rope = _shape_constants()
    arrays = {"x": x, "w_in_chunks": _chunks(wi, in_cols), "w_out_chunks": _chunks(A(w_out)[0], cols),
              "moe_chunks": moe, "params": params, "consts": consts, "rope": rope, "gains": gains}
    arrays = {k: np.ascontiguousarray(a) for k, a in arrays.items()}

    nc = _bacc.Bacc("TRN2", target_bir_lowering=False, num_devices=1)
    args = [nc.dram_tensor(k, a.shape, _mybir.dt.from_np(a.dtype), kind="ExternalInput").ap()
            for k, a in arrays.items()]
    args.append(nc.dram_tensor("y", x.shape, _mybir.dt.float32, kind="ExternalOutput").ap())
    hybrid_encoder(nc, *args)
    r = _run(nc, [arrays], core_ids=[0])
    y = r.results[0]["y"]
    return y[None, 1024:], y[None, :1024]
```

```python
from contextlib import ExitStack

import concourse.bass as bass
from concourse import mybir

ALU = mybir.AluOpType
ACT = mybir.ActivationFunctionType
AX = mybir.AxisListType
F32 = mybir.dt.float32
F32R = mybir.dt.float32r
BF16 = mybir.dt.bfloat16
U32 = mybir.dt.uint32

P = 128
D = 1024
KT = D // P
CW = 256
BLK = 512
TPB = BLK // P
EPS = 1e-6
LAM_INIT = 0.2
HEADS = 4
SH = 8
NE = 16
NM = 25
NCH = 13
NR = 13
SEQS = [(0, 8, (0, 1), 128), (8, 4, (2,), 64)]
NT = 12
FIRST_CHUNK = {0: 0, 1: 13, 2: 30}
FIRST_OUT_CHUNK = (26, 43)
MOE_CHUNK = 47
ECH = 12
TOK = 192

PAR = {}
_at = 0
for _name, _w in (("conv_w", 40), ("conv_b", 8), ("d_skip", 4), ("ssm_g", 4), ("sub_g", 1), ("dt_bias", 16),
                  ("a_log", 16), ("lam", 256), ("router", KT * NE)):
    PAR[_name] = (_at, _at + _w)
    _at += _w
NPAR = _at
CST = {n: (i * P, i * P + P) for i, n in enumerate(("ident", "cum_f", "cum_b", "neg_f", "neg_b", "rot", "ones"))}
NCST = P * len(CST)


class Order:

    def __init__(self, engine, sem):
        self.engine, self.sem, self.n = engine, sem, 0

    def step(self, ins):
        self.n += 1
        ins.then_inc(self.sem, 1)

    def wait(self):
        self.engine.wait_ge(self.sem, self.n)

    def link(self, ins):
        self.step(ins)
        self.wait()


def hybrid_encoder(nc, x, w_in, w_out, w_moe, params, consts, rope, gains, y):
    ctx = ExitStack()
    KB = 1024
    base = 16640

    def at(name, kb, shape, dt=F32):
        return nc.alloc_sbuf_tensor_at(name, shape, dt, offset=base + int(kb * KB) // 32 * 32)

    def sem(name):
        return ctx.enter_context(nc.semaphore(name))

    with ctx:
        wraw = at("wraw", 0, [P, 2, KT * CW])
        whi = at("whi", 16, [P, 2, KT, CW], F32R)
        wlo = at("wlo", 32, [P, 2, KT, CW], F32R)
        ht_hi = at("ht_hi", 48, [P, KT, BLK], F32R)
        ht_lo = at("ht_lo", 64, [P, KT, BLK], F32R)
        qT = at("qT", 80, [P, HEADS, 1024])
        kT = at("kT", 96, [P, HEADS, 1024])
        v = at("v", 112, [P, 8, 512])
        LX = 1028
        xbc = at("xbc", 128, [P, 8, LX])
        S0 = 160.25
        conv_acc = at("conv_acc", S0, [P, 1024])
        cos_t = at("cos_t", S0 + 4, [P, BLK])
        sin_t = at("sin_t", S0 + 6, [P, BLK])
        stage = at("stage", S0 + 8, [P, 2, BLK])
        tmp = at("tmp", S0 + 12, [P, 2, BLK])
        xin = at("xin", S0 + 16, [P, 2, D])
        khl = at("khl", 48, [P, 2, 2, 1024], F32R)
        qhl = at("qhl", 64, [P, 2, 4, BLK], F32R)
        prob = [[at(f"prob{s}{i}", 16 + 16 * i + 8 * (1 - FIRST_OUT_CHUNK[s] % 2), [P, 2, 1024]) for i in range(2)]
                for s in range(2)]
        wgtT = at("wgtT", S0 + 16, [P, 2, 1024])
        oatt = at("oatt", S0, [P, 8, 512])
        xf = at("xf", 48, [P, 8, 2, 512])
        state = [at("state_f", 96, [P, 8, 512]), at("state_b", 112, [P, 8, 512])]
        xs = at("xs", S0, [P, 2, 2, 512])
        btok = at("btok", S0 + 8, [P, 2, 256])
        scan_t = [at("scan_f", S0 + 10, [P, 512]), at("scan_b", S0 + 12, [P, 512])]
        er = at("er", S0, [P, 2, 512])
        dr = at("dr", S0 + 4, [P, 2, 512])
        lr = at("lr", S0 + 8, [P, 2, 512])
        mr = at("mr", S0 + 12, [P, 2, 512])
        cr = at("cr", S0 + 16, [P, 2, 512])
        zin = at("zin", S0 + 20, [P, 2, 512])
        sq = at("sq", S0, [P, 2, BLK])
        rs = at("rs", S0 + 4, [P, 2, BLK])
        mix_hi = at("mix_hi", 48, [P, KT, 1024], F32R)
        mix_lo = at("mix_lo", 96, [P, KT, 1024], F32R)
        x2 = at("x2", 128, [P, 8, D])
        h2 = at("h2", S0, [P, 2, D])
        h2T = at("h2T", S0 + 8, [P, 2, KT, P])
        aff = at("aff", 80, [P, P])
        aff2 = at("aff2", 80.5, [P, P])
        affT = at("affT", 120, [NE, 1024])
        xe_s = at("xe_s", 48, [P, D])
        xe_p = at("xe_p", 52, [64, D])
        xT = at("xT", 56, [P, KT, 2 * TOK], F32R)
        hid = at("hid", 68, [P, KT, 2 * TOK], F32R)
        gr = at("gr", 80, [P, 2, TOK])
        ur = at("ur", 82, [P, 2, TOK])
        sg = at("sg", 84, [P, 2, TOK])
        hm = at("hm", 86, [P, 2, TOK])
        ye_s = at("ye_s", 88, [P, D])
        ye_p = at("ye_p", 92, [64, D])
        tp = at("tp", 96, [64, 2, CW])
        wraw_x = at("wraw_x", 128, [P, 2, KT * CW])
        whi_x = at("whi_x", 144, [P, KT, CW], F32R)
        wlo_x = at("wlo_x", 152, [P, KT, CW], F32R)
        old = (MOE_CHUNK % 2, 1 - MOE_CHUNK % 2)
        moe_raw = [wraw[:, old[0], :], wraw[:, old[1], :], wraw_x[:, 0, :], wraw_x[:, 1, :]]
        moe_hi = [whi[:, old[0]], whi[:, old[1]], whi_x[:, :, :]]
        moe_lo = [wlo[:, old[0]], wlo[:, old[1]], wlo_x[:, :, :]]
        yin = at("yin", 100, [P, 2, D])
        yout = at("yout", 108, [P, 2, D])
        gain = at("gain", 184.5, [P, D])
        junk = at("junk", 188.5, [P, D], BF16)
        osq = at("osq", 188.5, [P, 512])
        cst = at("cst", 190.5, [P, NCST])
        par = at("par", 194, [P, NPAR])
        o = 194 + NPAR * 4 / KB + 0.1
        small = at("small", o, [P, 8, NT])
        dts = at("dts", o + 0.5, [P, 10, P])
        o += 5.6
        stat = at("stat", o, [P, 2, 16])
        ostat = at("ostat", o + 0.25, [P, 3, 32])
        lamt = at("lamt", o + 0.75, [P, 16])
        rsum = at("rsum", o + 0.81, [P, 16])
        topv = at("topv", o + 0.9, [NE, TOK])
        topi = at("topi", o + 1.65, [NE, TOK], U32)
        topf = at("topf", o + 2.4, [NE, TOK])
        o += 0.75
        gate_s = at("gate_s", o + 2.4, [P, NE])
        gate_p = at("gate_p", o + 2.5, [64, NE])
        idx_s = at("idx_s", o + 2.6, [P, NE], U32)
        idx_p = at("idx_p", o + 2.7, [64, NE], U32)
        gcur_s = at("gcur_s", o + 2.8, [P, 1])
        gcur_p = at("gcur_p", o + 2.85, [64, 1])
        gi_s = at("gi_s", o + 2.9, [P, 1], U32)
        gi_p = at("gi_p", o + 2.95, [64, 1], U32)
        si_s = at("si_s", o + 3.0, [P, 1], U32)
        si_p = at("si_p", o + 3.05, [64, 1], U32)
        pmark2 = at("pmark2", o + 3.3, [1, 8])
        pmark = at("pmark", o + 3.2, [1, 8])
        mark = at("mark", o + 3.1, [1, 16])
        psum = ctx.enter_context(nc.psum_tensor("psum", [P, 8 * 512], F32))
        pb = [psum[:, i * 512:(i + 1) * 512] for i in range(8)]

        z_dram = nc.dram_tensor("z_scratch", (3, P, 4, BLK), F32).ap()
        h2_dram = nc.dram_tensor("h2_scratch", (NT * P, D), F32).ap()
        acc_dram = nc.dram_tensor("acc_scratch", (NT * P, D), F32).ap()

        def c(name):
            a, b = CST[name]
            return cst[:, a:b]

        def p_(name, i=None, n=None):
            a, b = PAR[name]
            return par[:, a:b] if i is None else par[:, a + i:a + i + (n or 1)]

        ident = c("ident")

        cst_in, par_in = sem("cst_in"), sem("par_in")
        gain_in = sem("gain_in")
        rope_in = sem("rope_in")
        raw_in = [sem("raw_in0"), sem("raw_in1")]
        raw_x_in = [sem("raw_x_in0"), sem("raw_x_in1")]
        moe_raw_in = [(raw_in[old[0]], MOE_CHUNK // 2), (raw_in[old[1]], (MOE_CHUNK + 1) // 2),
                      (raw_x_in[0], 0), (raw_x_in[1], 0)]
        w_hi_done, w_lo_done = sem("w_hi_done"), sem("w_lo_done")
        xin_in = [sem("xin_in0"), sem("xin_in1")]
        ss_done, ms_done, rms_done, hn_done = sem("ss_done"), sem("ms_done"), sem("rms_done"), sem("hn_done")
        h_turned, ht_hi_done, ht_lo_done = sem("h_turned"), sem("ht_hi_done"), sem("ht_lo_done")
        col_done, col_out, turn_done, rot_out = sem("col_done"), sem("col_out"), sem("turn_done"), sem("rot_out")
        z_out = [sem("z_out0"), sem("z_out1")]
        conv_done, conv_act = sem("conv_done"), sem("conv_act")
        phase_act, phase_dve, phase_pool = sem("phase_act"), sem("phase_dve"), sem("phase_pool")
        sc_done, mx_done, exp_done = sem("sc_done"), sem("mx_done"), sem("exp_done")
        khi_done, klo_done, qhi_done, qlo_done = sem("khi_done"), sem("klo_done"), sem("qhi_done"), sem("qlo_done")
        o_scaled, o_squared, o_summed = sem("o_scaled"), sem("o_squared"), sem("o_summed")
        wg_done, wt_done, wt_out, av_done = sem("wg_done"), sem("wt_done"), sem("wt_out"), sem("av_done")
        osum_done, orms_done, on_done, ot_done, ot_out = (sem("osum_done"), sem("orms_done"), sem("on_done"),
                                                          sem("ot_done"), sem("ot_out"))
        dt_v, dt_a, cs_done = sem("dt_v"), sem("dt_a"), sem("cs_done")
        xt_done, bt_done, xf_done, bt_out, xs_done = (sem("xt_done"), sem("bt_done"), sem("xf_done"), sem("bt_out"),
                                                      sem("xs_done"))
        st_done, st_out = sem("st_done"), sem("st_out")
        cb_done, cb_used, row_done, e_done, d_done, l_done = (sem("cb_done"), sem("cb_used"), sem("row_done"),
                                                              sem("e_done"), sem("d_done"), sem("l_done"))
        m_done, c_done, yh_done, y_done, y_used = (sem("m_done"), sem("c_done"), sem("yh_done"), sem("y_done"),
                                                   sem("y_used"))
        z_in = [sem("z_in0"), sem("z_in1")]
        z_used = sem("z_used")
        sq_done, nsum_done, nms_done, nrms_done, nrm_done = (sem("sq_done"), sem("nsum_done"), sem("nms_done"),
                                                             sem("nrms_done"), sem("nrm_done"))
        mix_hi_done, mix_lo_done = sem("mix_hi_done"), sem("mix_lo_done")
        x2_in = sem("x2_in")
        op_done, op_out = sem("op_done"), sem("op_out")
        ss2_done, rms2_done, h2_done, h2_turned, h2T_out = (sem("ss2_done"), sem("rms2_done"), sem("h2_done"),
                                                            sem("h2_turned"), sem("h2T_out"))
        x2_out = sem("x2_out")
        h2_out = [sem("h2_out0"), sem("h2_out1")]
        lg_done = sem("lg_done")
        rt_v, rt_a, rt_p = sem("rt_v"), sem("rt_a"), sem("rt_p")
        own_dve, own_act, own_pool = sem("own_dve"), sem("own_act"), sem("own_pool")
        idx_ready, cur_ready = sem("idx_ready"), sem("cur_ready")
        xs_in, xp_in = sem("xs_in"), sem("xp_in")
        xturn, xhi_done, xlo_done = sem("xturn"), sem("xhi_done"), sem("xlo_done")
        tile_done, red_done, silu_done, hm_done = sem("tile_done"), sem("red_done"), sem("silu_done"), sem("hm_done")
        hhi_done, hlo_done = sem("hhi_done"), sem("hlo_done")
        ys_done, tp_done, yp_done = sem("ys_done"), sem("tp_done"), sem("yp_done")
        sc_s, sc_p = sem("sc_s"), sem("sc_p")
        y_in = [sem("y_in0"), sem("y_in1")]
        fss, fms, frms, fy = sem("fss"), sem("fms"), sem("frms"), sem("fy")
        y_out = [sem("y_out0"), sem("y_out1")]
        half_added, adds_done, scattered = sem("half_added"), sem("adds_done"), sem("scattered")

        block = ctx.enter_context(nc.Block())

        def block_tile(b):
            return {0: 0, 1: TPB, 2: 0}[b]

        def chunk_used(eng, g):
            if g < 0:
                return
            for s in (1, 0):
                if g >= FIRST_OUT_CHUNK[s] and (s == 1 or g < FIRST_CHUNK[2]):
                    nt = SEQS[s][1]
                    done = 4 * SEQS[0][1] if s else 0
                    eng.wait_ge(op_done, done + nt * (g - FIRST_OUT_CHUNK[s] + 1))
                    return
            b = max(b for b in range(3) if g >= FIRST_CHUNK[b])
            eng.wait_ge(col_done, NM * b + min(2 * (g - FIRST_CHUNK[b] + 1), NM))

        def row_bank(n):
            return pb[(2, 3, 6)[n % 3]]

        def phase(eng, n, but=None):
            for s in (phase_act, phase_dve, phase_pool):
                if s is not but:
                    eng.wait_ge(s, n)


        @block.sync
        def _(sp):
            sp.dma_start(cst[:, :], consts).then_inc(cst_in, 16)
            sp.dma_start(par[:, :], params).then_inc(par_in, 16)

            def load(g, src):
                if g >= 2:
                    sp.wait_ge(w_lo_done, g - 1)
                sp.dma_start(wraw[:, g % 2, :], src).then_inc(raw_in[g % 2], 16)

            for s, (_, _, blocks, _) in enumerate(SEQS):
                for b in blocks:
                    for j in range(NCH):
                        load(FIRST_CHUNK[b] + j, w_in[j])
                for j in range(4):
                    load(FIRST_OUT_CHUNK[s] + j, w_out[j])
            load(MOE_CHUNK, w_moe[0])
            load(MOE_CHUNK + 1, w_moe[1])
            phase(sp, 14)
            for i in (2, 3):
                sp.dma_start(moe_raw[i], w_moe[i]).then_inc(moe_raw_in[i][0], 16)

            def load_moe(e, j):
                sp.wait_ge(w_lo_done, e * ECH + (MOE_CHUNK + j + 1))
                sp.dma_start(moe_raw[j % 4], w_moe[bass.ds(e * ECH + j + 4, 1), :, :].rearrange("a p n -> (a p) n")
                             ).then_inc(moe_raw_in[j % 4][0], 16)

            with sp.Fori(0, NE - 1) as e:
                for j in range(ECH):
                    load_moe(e, j)
            for j in range(ECH - 4):
                sp.wait_ge(w_lo_done, (NE - 1) * ECH + MOE_CHUNK + j + 1)
                sp.dma_start(moe_raw[j % 4], w_moe[(NE - 1) * ECH + j + 4]).then_inc(moe_raw_in[j % 4][0], 16)
            sp.wait_ge(sc_s, 16 * NE)
            sp.wait_ge(sc_p, 16 * NE)
            for t in range(NT):
                if t >= 2:
                    sp.wait_ge(fy, t - 1)
                sp.dma_start(yin[:, t % 2, :], acc_dram[t * P:(t + 1) * P, :]).then_inc(y_in[t % 2], 16)
                if t >= 1:
                    sp.wait_ge(fy, t)
                    sp.dma_start(y[(t - 1) * P:t * P, :], yout[:, (t - 1) % 2, :]).then_inc(y_out[(t - 1) % 2], 16)
            sp.wait_ge(fy, NT)
            sp.dma_start(y[(NT - 1) * P:NT * P, :], yout[:, (NT - 1) % 2, :]).then_inc(y_out[(NT - 1) % 2], 16)
            for i in range(2):
                sp.wait_ge(y_out[i], 16 * (NT // 2))

        @block.gpsimd
        def _(pool):
            own = Order(pool, own_pool)
            for s, (t0, nt, blocks, cap) in enumerate(SEQS):
                ph = 7 * s
                if s:
                    phase(pool, ph, phase_pool)
                pool.dma_start(gain[:, :], gains[0]).then_inc(gain_in, 16)
                for b in blocks:
                    if b:
                        pool.wait_ge(rot_out, NR * b)
                    c0 = block_tile(b) * P
                    pool.dma_start(cos_t[:, :], rope[0][:, c0:c0 + BLK]).then_inc(rope_in, 16)
                    pool.dma_start(sin_t[:, :], rope[1][:, c0:c0 + BLK]).then_inc(rope_in, 16)
                    for j in range(TPB):
                        t = TPB * b + j
                        if t >= 2:
                            pool.wait_ge(h_turned, 2 * (t - 1))
                        pool.dma_start(xin[:, t % 2, :], x[t * P:(t + 1) * P, :]).then_inc(xin_in[t % 2], 16)
                    for j in range(4):
                        pool.wait_ge(col_out, NM * b + 21 + j)
                        pool.dma_start(z_dram[b][:, j, :], tmp[:, j % 2, :]).then_inc(z_out[j % 2], 16)
                for i in range(2):
                    pool.wait_ge(z_out[i], 16 * 2 * (blocks[-1] + 1))
                pool.memset(mark[0:1, 0:1], 0.0).then_inc(phase_pool, 1)
                pool.memset(mark[0:1, 1:2], 0.0).then_inc(phase_pool, 1)

                phase(pool, ph + 2, phase_pool)
                pool.wait_ge(dt_a, 3 * s + 3)
                for cc in range(nt):
                    k = 8 * s + cc
                    pool.wait_ge(xf_done, 2 * (k + 1))
                    if k >= 2:
                        pool.wait_ge(st_done, 4 * (k - 1))
                    for d in range(2):
                        ins = pool.tensor_tensor(
                            xs[:, cc % 2, d, :].rearrange("p (h q) -> p h q", h=SH),
                            xf[:, cc, d, :].rearrange("p (h q) -> p h q", h=SH),
                            dts[:, 9, cc * 16 + 8 * d:cc * 16 + 8 * d + 8].unsqueeze(2).to_broadcast([P, SH, 64]),
                            ALU.mult)
                        ins.then_inc(xs_done, 1)
                pool.wait_ge(st_out, 2 * (8 * s + nt))
                for cc in range(nt - 2, 0, -1):
                    own.link(pool.tensor_tensor(
                        scan_t[1][:, :].rearrange("p (h q) -> p h q", h=SH),
                        state[1][:, cc, :].rearrange("p (h q) -> p h q", h=SH),
                        dts[:, 8, cc * 16 + 8:cc * 16 + 16].unsqueeze(2).to_broadcast([P, SH, 64]), ALU.mult))
                    own.link(pool.tensor_tensor(state[1][:, cc - 1, :], state[1][:, cc - 1, :], scan_t[1][:, :],
                                                ALU.add))
                pool.memset(mark[0:1, 0:1], 0.0).then_inc(phase_pool, 1)

                phase(pool, ph + 3, phase_pool)
                for cc in range(nt):
                    k = 8 * s + cc
                    if cc >= 2:
                        pool.wait_ge(z_used, k - 1)
                    b = blocks[cc // TPB]
                    pool.dma_start(zin[:, k % 2, :].rearrange("p (j l) -> p j l", j=4),
                                   z_dram[b][:, :, (cc % TPB) * P:(cc % TPB + 1) * P]).then_inc(z_in[k % 2], 16)
                    for u in range(4):
                        g, d, n = u // 2, u % 2, 4 * k + u
                        pool.wait_ge(e_done, n + 1)
                        if n >= 2:
                            pool.wait_ge(yh_done, n - 1)
                        pool.tensor_tensor(
                            cr[:, n % 2, :].rearrange("p (h l) -> p h l", h=4),
                            er[:, n % 2, :].rearrange("p (h l) -> p h l", h=4),
                            xbc[:, 6 + g, 2 + cc * P:2 + cc * P + P].unsqueeze(1).to_broadcast([P, 4, P]),
                            ALU.mult).then_inc(c_done, 1)
                pool.memset(mark[0:1, 0:1], 0.0).then_inc(phase_pool, 1)
                pool.memset(mark[0:1, 1:2], 0.0).then_inc(phase_pool, 1)

                phase(pool, ph + 5, phase_pool)
                pool.dma_start(gain[:, :], gains[1]).then_inc(gain_in, 16)
                pool.dma_start(x2[:, 0:nt, :], x[t0 * P:(t0 + nt) * P, :].rearrange("(t p) d -> p t d", p=P)
                               ).then_inc(x2_in, 16)
                pool.wait_ge(op_out, 4 * (t0 + nt))
                pool.dma_start(acc_dram[t0 * P:(t0 + nt) * P, :].rearrange("(t p) d -> p t d", p=P), x2[:, 0:nt, :]
                               ).then_inc(x2_out, 16)
                for j in range(nt):
                    t = t0 + j
                    pool.wait_ge(h2_done, t + 1)
                    pool.dma_start(h2_dram[t * P:(t + 1) * P, :], h2[:, t % 2, :]).then_inc(h2_out[t % 2], 16)
                pool.wait_ge(x2_out, 16 * (s + 1))
                for i in range(2):
                    pool.wait_ge(h2_out[i], 16 * (t0 + nt) // 2)
                pool.memset(mark[0:1, 0:1], 0.0).then_inc(phase_pool, 1)
                pool.memset(mark[0:1, 1:2], 0.0).then_inc(phase_pool, 1)

            phase(pool, 14, phase_pool)
            pool.dma_start(gain[:, :], gains[2]).then_inc(gain_in, 16)

            def gather(e1, first=False):
                if not first:
                    pool.wait_ge(adds_done, e1 * 2 - 1)
                pool.wait_ge(idx_ready, e1 + 1)
                pool.tensor_tensor(pmark[:, 0:1], pmark[:, 1:2], pmark[:, 2:3], ALU.add).then_inc(adds_done, 1)
                pool.indirect_dma_start(out=xe_s[:, :], out_offset=None, in_=h2_dram,
                                        in_offset=bass.IndirectOffsetOnAxis(ap=gi_s[:, 0:1], axis=0)
                                        ).then_inc(xs_in, 16)
                pool.indirect_dma_start(out=xe_p[:, :], out_offset=None, in_=h2_dram,
                                        in_offset=bass.IndirectOffsetOnAxis(ap=gi_p[:, 0:1], axis=0)
                                        ).then_inc(xp_in, 16)

            def expert(e, last):
                if not last:
                    pool.wait_ge(xturn, (e + 1) * 4)
                    gather(e + 1)
                pool.wait_ge(cur_ready, e + 1)
                pool.wait_ge(ys_done, (e + 1) * 4)
                pool.wait_ge(yp_done, e * 4 + 6)
                pool.wait_ge(adds_done, e * 2 + (1 if last else 2))
                pool.tensor_tensor(pmark[:, 0:1], pmark[:, 1:2], pmark[:, 2:3], ALU.add).then_inc(adds_done, 1)
                pool.indirect_dma_start(out=acc_dram, in_=ye_s[:, :], in_offset=None, compute_op=ALU.add,
                                        out_offset=bass.IndirectOffsetOnAxis(ap=si_s[:, 0:1], axis=0)
                                        ).then_inc(sc_s, 16)
                pool.indirect_dma_start(out=acc_dram, in_=ye_p[:, :], in_offset=None, compute_op=ALU.add,
                                        out_offset=bass.IndirectOffsetOnAxis(ap=si_p[:, 0:1], axis=0)
                                        ).then_inc(sc_p, 16)
                pool.wait_ge(sc_s, e * 16 + 16)
                pool.wait_ge(sc_p, e * 16 + 16)
                pool.wait_ge(scattered, e + 1)
                pool.tensor_tensor(pmark[:, 3:4], pmark[:, 1:2], pmark[:, 2:3], ALU.add).then_inc(scattered, 1)

            pool.wait_ge(x2_out, 32)
            pool.memset(pmark[:, :], 0.0).then_inc(own_pool, 1)
            pool.memset(pmark2[:, :], 0.0).then_inc(scattered, 1)
            own.n += 1
            own.wait()
            gather(0, True)
            with pool.Fori(0, NE - 1) as e:
                expert(e, False)
            expert(NE - 1, True)

        @block.scalar
        def _(act):
            own = Order(act, own_act)

            def split(g):
                act.wait_ge(raw_in[g % 2], 16 * (g // 2 + 1))
                chunk_used(act, g - 2)
                act.activation(whi[:, g % 2, :, :], wraw[:, g % 2, :].rearrange("p (k n) -> p k n", k=KT), ACT.Copy
                               ).then_inc(w_hi_done, 1)

            def end():
                act.activation(mark[0:1, 4:5], mark[0:1, 5:6], ACT.Copy).then_inc(phase_act, 1)

            def squares(act, s, a):
                t0, nt = SEQS[s][0:2]
                h, i = (4 * a) // nt, (4 * a) % nt
                act.wait_ge(o_scaled, t0 + a + 1)
                if t0 + a:
                    act.wait_ge(o_summed, t0 + a)
                act.activation(osq[:, :].rearrange("p (t n) -> p t n", t=4), oatt[:, i:i + 4, h * P:(h + 1) * P],
                               ACT.Square).then_inc(o_squared, 1)

            act.wait_ge(cst_in, 16)
            act.wait_ge(par_in, 16)
            act.wait_ge(own_dve, 1)
            act.wait_ge(own_dve, 5)
            act.activation(lamt[:, 2:4], lamt[:, 0:2], ACT.Exp).then_inc(own_act, 1)
            act.activation(stat[:, 0, :], p_("a_log"), ACT.Exp).then_inc(own_act, 1)
            own.n = 2
            split(0)
            for s, (t0, nt, blocks, cap) in enumerate(SEQS):
                ph = 7 * s
                L = nt * P
                if s:
                    phase(act, ph, phase_act)
                for b in blocks:
                    for j in range(TPB):
                        t = TPB * b + j
                        act.wait_ge(xin_in[t % 2], 16 * (t // 2 + 1))
                        act.activation(junk[:, :], xin[:, t % 2, :], ACT.Square, accum_out=small[:, 0, t:t + 1]
                                       ).then_inc(ss_done, 1)
                        act.wait_ge(ms_done, t + 1)
                        act.activation(small[:, 2, t:t + 1], small[:, 1, t:t + 1], ACT.Sqrt).then_inc(rms_done, 1)
                        if b and j == 0:
                            act.wait_ge(col_done, NM * b)
                            if b == 2:
                                act.wait_ge(op_done, 4 * 8)
                        for q in range(2):
                            act.wait_ge(h_turned, 2 * t + q + 1)
                            act.activation(ht_hi[:, 4 * q:4 * q + 4, j * P:(j + 1) * P],
                                           pb[6 + q][:, :].rearrange("p (k n) -> p k n", k=4), ACT.Copy
                                           ).then_inc(ht_hi_done, 1)
                    for m in range(NM):
                        n = NM * b + m
                        if m % 2 == 0:
                            split(FIRST_CHUNK[b] + m // 2 + 1)
                        act.wait_ge(col_done, n + 1)
                        src = pb[m % 4][:, :]
                        tok = block_tile(b) * P
                        if m < 8:
                            ins = act.activation(xbc[:, m, 2 + tok:2 + tok + BLK], src, ACT.Copy)
                        elif m < 20 or m == 24:
                            r = NR * b + min(m - 8, 12)
                            if r >= 2:
                                act.wait_ge(rot_out, r - 1)
                            ins = act.activation(stage[:, r % 2, :], src, ACT.Copy, scale=0.125 if m < 12 else 1.0)
                        else:
                            act.wait_ge(rot_out, NR * b + 8)
                            if m >= 22:
                                act.wait_ge(z_out[m % 2], 16 * (2 * b + 1))
                            ins = act.activation(tmp[:, m % 2, :], src, ACT.Silu)
                        ins.then_inc(col_out, 1)
                        if b == blocks[-1] and 9 <= m < 17:
                            i = m - 9
                            act.wait_ge(conv_done, 8 * s + i + 1)
                            act.activation(xbc[:, i, 2:2 + L], conv_acc[:, 0:L], ACT.Silu, bias=p_("conv_b", i)
                                           ).then_inc(conv_act, 1)
                end()

                phase(act, ph + 1, phase_act)

                def k_hi(h):
                    H = HEADS * s + h
                    if h >= 2:
                        act.wait_ge(sc_done, 2 * (4 * t0 + nt * (h - 1)))
                    for c_ in range(2):
                        act.activation(khl[64 * c_:64 * c_ + 64, h % 2, c_, 0:L], kT[64 * c_:64 * c_ + 64, h, 0:L], ACT.Copy
                                       ).then_inc(khi_done, 1)

                def q_hi(a):
                    h, i = (4 * a) // nt, (4 * a) % nt
                    if a >= 2:
                        act.wait_ge(sc_done, 2 * (4 * t0 + 4 * (a - 1)))
                    for c_ in range(2):
                        for half in range(2):
                            act.activation(qhl[64 * half:64 * half + 64, a % 2, c_, :],
                                           qT[64 * c_:64 * c_ + 64, h, i * P:i * P + BLK], ACT.Copy
                                           ).then_inc(qhi_done, 1)

                k_hi(0)
                q_hi(0)
                for u in range(4 * nt + 1):
                    U = 4 * t0 + u
                    if u < 4 * nt:
                        sl = prob[s][u % 2]
                        for c_ in range(2):
                            act.wait_ge(mx_done, 2 * U + c_ + 1)
                            if u >= 2:
                                act.wait_ge(wt_done, U - 1)
                            act.activation(sl[:, c_, 0:L], psum[:, 1024 * c_:1024 * c_ + L], ACT.Exp,
                                           bias=ostat[:, 0, 2 * (u % 2) + c_:2 * (u % 2) + c_ + 1],
                                           accum_out=ostat[:, 1, 2 * (u % 2) + c_:2 * (u % 2) + c_ + 1]
                                           ).then_inc(exp_done, 1)
                    if u % 4 == 1 and u // 4 + 1 < nt:
                        q_hi(u // 4 + 1)
                    if u % nt == 2 and u // nt + 1 < HEADS:
                        k_hi(u // nt + 1)
                    if u >= 1:
                        w = u - 1
                        W = 4 * t0 + w
                        act.wait_ge(wt_done, W + 1)
                        if w >= 2:
                            act.wait_ge(av_done, W - 1)
                        act.activation(wgtT[:, w % 2, 0:L], psum[:, 2048:2048 + L], ACT.Copy).then_inc(wt_out, 1)
                    if u % 4 == 3 and u >= 7:
                        squares(act, s, u // 4 - 1)
                squares(act, s, nt - 1)
                act.wait_ge(osum_done, s + 1)
                act.activation(dts[:, 2, 0:4 * nt], dts[:, 1, 0:4 * nt], ACT.Sqrt).then_inc(orms_done, 1)
                for i in range(nt):
                    act.wait_ge(ot_done, t0 + i + 1)
                    act.activation(qT[:, :, i * P:(i + 1) * P], pb[i % 2][:, :].rearrange("p (h n) -> p h n", h=4),
                                   ACT.Copy, scale=lamt[:, 8:9]).then_inc(ot_out, 1)
                end()

                phase(act, ph + 2, phase_act)
                act.wait_ge(dt_v, 4 * s + 1)
                act.activation(dts[:, 2, 0:16 * nt], dts[:, 1, 0:16 * nt], ACT.Exp).then_inc(dt_a, 1)
                act.wait_ge(dt_v, 4 * s + 2)
                act.activation(dts[:, 4, 0:16 * nt], dts[:, 3, 0:16 * nt], ACT.Ln).then_inc(dt_a, 1)
                act.wait_ge(dt_v, 4 * s + 4)
                act.activation(dts[:, 8, 0:16 * nt], dts[:, 3, 0:16 * nt], ACT.Exp).then_inc(own_act, 1)
                act.activation(dts[:, 9, 0:16 * nt], dts[:, 4, 0:16 * nt], ACT.Exp).then_inc(dt_a, 1)
                own.n += 1
                for cc in range(nt):
                    k = 8 * s + cc
                    act.wait_ge(bt_done, k + 1)
                    if k >= 2:
                        act.wait_ge(st_done, 4 * (k - 1))
                    act.activation(btok[:, cc % 2, :], pb[1 if cc % 2 == 0 else 3][:, 0:256], ACT.Copy
                                   ).then_inc(bt_out, 1)
                    for d in range(2):
                        act.wait_ge(st_done, 4 * k + 2 * d + 2)
                        to = cc + 1 if d == 0 else cc - 1
                        if 0 <= to < nt:
                            ins = act.activation(state[d][:, to, :], pb[4 + d][:, :], ACT.Copy)
                        else:
                            ins = act.activation(mark[0:1, 6:7], mark[0:1, 5:6], ACT.Copy)
                        ins.then_inc(st_out, 1)
                end()

                phase(act, ph + 3, phase_act)
                def row_exp(n4):
                    n = 32 * s + n4
                    act.wait_ge(row_done, n + 1)
                    if n >= 2:
                        act.wait_ge(c_done, n - 1)
                    act.activation(er[:, n % 2, :], row_bank(n), ACT.Exp).then_inc(e_done, 1)

                row_exp(0)
                for n4 in range(4 * nt):
                    n = 32 * s + n4
                    cc, g, d = n4 // 4, (n4 // 2) % 2, n4 % 2
                    if n4 + 1 < 4 * nt:
                        row_exp(n4 + 1)
                    act.wait_ge(d_done, n + 1)
                    if n >= 2:
                        act.wait_ge(m_done, n - 1)
                    for hh in range(4):
                        col = cc * 16 + 8 * d + 4 * g + hh
                        ins = act.activation(lr[:, n % 2, hh * P:(hh + 1) * P], dr[:, n % 2, hh * P:(hh + 1) * P],
                                             ACT.Exp, bias=dts[:, 7, col:col + 1])
                    ins.then_inc(l_done, 1)
                end()

                phase(act, ph + 4, phase_act)
                for q in range(2 * (L // BLK)):
                    N = (4 if s else 0) + q
                    hf, g = q // 2, q % 2
                    for i in range(2):
                        if q >= 1:
                            act.wait_ge(nsum_done, N)
                        act.activation(sq[:, i, :], xbc[:, 2 * g + i, 2 + hf * BLK:2 + (hf + 1) * BLK], ACT.Square
                                       ).then_inc(sq_done, 1)
                    act.wait_ge(nms_done, N + 1)
                    act.activation(rs[:, 0, :], rs[:, 1, :], ACT.Sqrt).then_inc(nrms_done, 1)
                for k in range(KT):
                    src = qT[:, k, 0:L] if k < 4 else xbc[:, k - 4, 2:2 + L]
                    if k == 4:
                        act.wait_ge(nrm_done, 2 * ((4 if s else 0) + 2 * (L // BLK)))
                    act.activation(mix_hi[:, k, 0:L], src, ACT.Copy).then_inc(mix_hi_done, 1)
                end()

                phase(act, ph + 5, phase_act)
                for jo in range(4):
                    g = FIRST_OUT_CHUNK[s] + jo + 1
                    if g < MOE_CHUNK:
                        split(g)
                    else:
                        act.wait_ge(raw_in[g % 2], 16 * (g // 2 + 1))
                        chunk_used(act, g - 2)
                        act.activation(whi[:, g % 2, :, :], wraw[:, g % 2, :].rearrange("p (k n) -> p k n", k=KT),
                                       ACT.Copy).then_inc(w_hi_done, 1)
                for i in range(nt):
                    act.wait_ge(op_out, 4 * t0 + 3 * nt + i + 1)
                    ins = act.activation(junk[:, :], x2[:, i, :], ACT.Square, accum_out=small[:, 0, i:i + 1])
                    ins.then_inc(ss2_done, 1)
                    act.wait_ge(ss2_done, t0 + i + 1)
                act.wait_ge(rms2_done, 2 * s + 1)
                act.activation(small[:, 2, 0:nt], small[:, 1, 0:nt], ACT.Sqrt).then_inc(rms2_done, 1)
                for i in range(nt):
                    t = t0 + i
                    for q in range(2):
                        act.wait_ge(h2_turned, 2 * t + q + 1)
                        if t >= 2:
                            act.wait_ge(lg_done, t - 1)
                        act.activation(h2T[:, t % 2, 4 * q:4 * q + 4, :],
                                       pb[6 + q][:, :].rearrange("p (k n) -> p k n", k=4), ACT.Copy
                                       ).then_inc(h2T_out, 1)
                end()

                phase(act, ph + 6, phase_act)
                act.wait_ge(rt_v, 2 * s + 1)
                act.activation(aff[:, 0:16 * nt], aff[:, 0:16 * nt], ACT.Exp).then_inc(rt_a, 1)
                end()

            phase(act, 14, phase_act)

            def turned_out(n):
                for kk in range(4):
                    act.wait_ge(xturn, n * 4 + kk + 1)
                    act.activation(xT[:, 2 * kk:2 * kk + 2, 0:TOK],
                                   pb[6 + kk % 2][:, 0:2 * TOK].rearrange("p (k n) -> p k n", k=2), ACT.Copy
                                   ).then_inc(xhi_done, 1)

            def expert(e, last):
                for j in range(ECH):
                    if not (last and j >= ECH - 2):
                        i = j + 2
                        landed, before = moe_raw_in[i % 4]
                        act.wait_ge(landed, e * (16 * ECH // 4) + 16 * (before + i // 4 + 1))
                        act.wait_ge(tile_done, e * 24 + 2 * j + 2)
                        act.activation(moe_hi[i % 3], moe_raw[i % 4].rearrange("p (k n) -> p k n", k=KT), ACT.Copy
                                       ).then_inc(w_hi_done, 1)
                    if j < 8 and j % 2:
                        for ft in range(2):
                            act.wait_ge(red_done, e * 16 + 4 + 2 * (j - 1) + ft + 1)
                            act.wait_ge(hm_done, e * 8 + 2 + j - 1)
                            act.activation(sg[:, ft, :], gr[:, ft, :], ACT.Silu).then_inc(silu_done, 1)
                    if j in (2, 4, 6, 7):
                        f0 = j - 2 if j < 7 else 6
                        for ft in range(2):
                            act.wait_ge(hm_done, e * 8 + 2 + f0 + ft + 1)
                            act.activation(hid[:, f0 + ft, 0:TOK], hm[:, ft, :], ACT.Copy).then_inc(hhi_done, 1)
                    if j == 7 and not last:
                        turned_out(e + 1)
                    if j >= 8:
                        dc = j - 8
                        bank = pb[4 + dc % 2]
                        act.wait_ge(tile_done, e * 24 + 2 + 2 * j + 2)
                        if dc == 0:
                            act.wait_ge(cur_ready, e + 1)
                        act.wait_ge(yp_done, e * 4 + dc + 1 - 0)
                        act.activation(tp[:, dc % 2, :], bank[64:P, CW:2 * CW], ACT.Copy).then_inc(tp_done, 1)
                        act.activation(ye_s[:, dc * CW:(dc + 1) * CW], bank[:, 0:CW], ACT.Copy,
                                       scale=gcur_s[:, 0:1]).then_inc(ys_done, 1)

            split(MOE_CHUNK + 1)
            turned_out(0)
            with act.Fori(0, NE - 1) as e:
                expert(e, False)
            expert(NE - 1, True)

            for t in range(NT):
                act.wait_ge(y_in[t % 2], 16 * (t // 2 + 1))
                act.activation(junk[:, :], yin[:, t % 2, :], ACT.Square, accum_out=small[:, 0, t:t + 1]
                               ).then_inc(fss, 1)
                act.wait_ge(fms, t + 1)
                act.activation(small[:, 2, t:t + 1], small[:, 1, t:t + 1], ACT.Sqrt).then_inc(frms, 1)

        @block.vector
        def _(dve):
            own = Order(dve, own_dve)
            tt, ts, stt = dve.tensor_tensor, dve.tensor_scalar, dve.scalar_tensor_tensor

            def split(g):
                dve.wait_ge(w_hi_done, g + 1)
                tt(wlo[:, g % 2, :, :], wraw[:, g % 2, :].rearrange("p (k n) -> p k n", k=KT),
                   whi[:, g % 2, :, :].bitcast(F32), ALU.subtract).then_inc(w_lo_done, 1)

            def end():
                dve.memset(mark[0:1, 8:9], 0.0).then_inc(phase_dve, 1)

            def choose(s, n):
                L, o_ = SEQS[s][1] * P, 128 * s + 8 * n
                tv, ti = topv[:, o_:o_ + 8], topi[:, o_:o_ + 8]
                own.link(dve.max(tv, affT[:, 0:L]))
                own.link(dve.max_index(ti, tv, affT[:, 0:L]))
                own.link(dve.match_replace(affT[:, 0:L], tv, affT[:, 0:L], -1.0))

            def chosen(s):
                cols = slice(128 * s, 128 * s + SEQS[s][3])
                own.link(dve.tensor_copy(topf[:, cols], topi[:, cols]))
                own.link(ts(topf[:, cols], topf[:, cols], float(SEQS[s][0] * P), None, ALU.add))

            own.link(dve.memset(mark[0:1, :], 0.0))
            dve.wait_ge(par_in, 16)
            lam4 = p_("lam").rearrange("p (i j) -> p i j", i=4)
            own.link(tt(conv_acc[:, 0:64], lam4[:, 0, :], lam4[:, 1, :], ALU.mult))
            own.link(tt(conv_acc[:, 64:128], lam4[:, 2, :], lam4[:, 3, :], ALU.mult))
            own.link(dve.tensor_reduce(lamt[:, 0:2], conv_acc[:, 0:128].rearrange("p (i j) -> p i j", i=2), AX.X,
                                       ALU.add))
            own.link(ts(lamt[:, 8:9], p_("sub_g"), 1.0 - LAM_INIT, None, ALU.mult))
            dve.wait_ge(own_act, 2)
            own.link(tt(lamt[:, 4:5], lamt[:, 2:3], lamt[:, 3:4], ALU.subtract))
            own.link(ts(lamt[:, 6:7], lamt[:, 4:5], LAM_INIT, -1.0, ALU.add, ALU.mult))
            own.link(ts(stat[:, 1, :], stat[:, 0, :], -1.0, None, ALU.mult))
            split(0)
            for s, (t0, nt, blocks, cap) in enumerate(SEQS):
                ph = 7 * s
                L = nt * P
                if s:
                    phase(dve, ph, phase_dve)
                own.step(dve.memset(xbc[:, :, 0:2], 0.0))
                own.link(dve.memset(xbc[:, :, 2 + L:4 + L], 0.0))
                dve.wait_ge(gain_in, 16 * (2 * s + 1))
                for b in blocks:
                    for j in range(TPB):
                        t = TPB * b + j
                        dve.wait_ge(ss_done, t + 1)
                        ts(small[:, 1, t:t + 1], small[:, 0, t:t + 1], 1.0 / D, EPS, ALU.mult, ALU.add
                           ).then_inc(ms_done, 1)
                        dve.wait_ge(rms_done, t + 1)
                        own.link(dve.reciprocal(small[:, 3, t:t + 1], small[:, 2, t:t + 1]))
                        stt(out=xin[:, t % 2, :], in0=xin[:, t % 2, :], scalar=small[:, 3, t:t + 1], in1=gain[:, :],
                            op0=ALU.mult, op1=ALU.mult).then_inc(hn_done, 1)
                        for q in range(2):
                            dve.wait_ge(ht_hi_done, 2 * t + q + 1)
                            sl = (slice(None), slice(4 * q, 4 * q + 4), slice(j * P, (j + 1) * P))
                            tt(ht_lo[sl], pb[6 + q][:, :].rearrange("p (k n) -> p k n", k=4),
                               ht_hi[sl].bitcast(F32), ALU.subtract).then_inc(ht_lo_done, 1)
                    tok = block_tile(b) * P
                    dve.wait_ge(rope_in, 32 * (b + 1))

                    def second_step(m):
                        r = NR * b + min(m - 8, 12)
                        st = stage[:, r % 2, :]
                        bank = pb[4 + r % 2]
                        if m < 16:
                            if r % NR == 0 and b:
                                for i in range(2):
                                    dve.wait_ge(z_out[i], 16 * 2 * b)
                            if r:
                                dve.wait_ge(rot_out, r)
                            dve.wait_ge(col_out, NM * b + m + 1)
                            own.step(tt(tmp[:, 0, :], st, cos_t[:, :], ALU.mult))
                            dve.wait_ge(turn_done, r + 1)
                            own.link(tt(tmp[:, 1, :], bank[:, :], sin_t[:, :], ALU.mult))
                            dst = (qT if m < 12 else kT)[:, (m - 8) % 4, tok:tok + BLK]
                            tt(dst, tmp[:, 0, :], tmp[:, 1, :], ALU.add).then_inc(rot_out, 1)
                        elif m < 20:
                            dve.wait_ge(turn_done, r + 1)
                            h = m - 16
                            dve.tensor_copy(v[:, block_tile(b):block_tile(b) + TPB, h * P:(h + 1) * P],
                                            bank[:, :].rearrange("p (t n) -> p t n", t=TPB)).then_inc(rot_out, 1)
                        else:
                            dve.wait_ge(turn_done, r + 1)
                            i = block_tile(b)
                            dve.tensor_copy(
                                dts[:, 6, 16 * i:16 * (i + TPB)].rearrange("p (t n) -> p t n", t=TPB),
                                bank[:, :].rearrange("p (t n) -> p t n", t=TPB)[:, :, 112:128]).then_inc(rot_out, 1)

                    for m in range(NM):
                        if m % 2 == 0:
                            split(FIRST_CHUNK[b] + m // 2 + 1)
                        if 9 <= m < 21:
                            second_step(m - 1)
                        if s == 1 and m % 16 < 8:
                            choose(0, m % 16 + m // 16 * 8)
                        if b == blocks[-1] and 8 <= m < 16:
                            i = m - 8
                            if i == 0:
                                dve.wait_ge(col_out, NM * b + 8)
                            else:
                                dve.wait_ge(conv_act, 8 * s + i)
                            own.link(ts(conv_acc[:, 0:L], xbc[:, i, 0:L], p_("conv_w", 5 * i), None, ALU.mult))
                            for w in range(1, 5):
                                ins = stt(out=conv_acc[:, 0:L], in0=xbc[:, i, w:w + L], scalar=p_("conv_w", 5 * i + w),
                                          in1=conv_acc[:, 0:L], op0=ALU.mult, op1=ALU.add)
                                if w < 4:
                                    own.link(ins)
                                else:
                                    ins.then_inc(conv_done, 1)
                    second_step(24)
                if s == 1:
                    chosen(0)
                end()

                phase(dve, ph + 1, phase_dve)

                def k_lo(h):
                    H = HEADS * s + h
                    for c_ in range(2):
                        dve.wait_ge(khi_done, 2 * H + c_ + 1)
                        rows, other = slice(64 * c_, 64 * c_ + 64), slice(64 * (1 - c_), 64 * (1 - c_) + 64)
                        tt(khl[other, h % 2, c_, 0:L], kT[rows, h, 0:L],
                           khl[rows, h % 2, c_, 0:L].bitcast(F32), ALU.subtract).then_inc(klo_done, 1)

                def q_lo(a):
                    h, i = (4 * a) // nt, (4 * a) % nt
                    for c_ in range(2):
                        dve.wait_ge(qhi_done, 4 * (t0 + a) + 2 * c_ + 2)
                        rows = slice(64 * c_, 64 * c_ + 64)
                        for half in range(2):
                            tt(qhl[64 * half:64 * half + 64, a % 2, 2 + c_, :], qT[rows, h, i * P:i * P + BLK],
                               qhl[rows, a % 2, c_, :].bitcast(F32), ALU.subtract).then_inc(qlo_done, 1)

                def weights(w):
                    W = 4 * t0 + w
                    sl, o2 = prob[s][w % 2], 2 * (w % 2)
                    dve.wait_ge(exp_done, 2 * W + 2)
                    own.link(dve.reciprocal(rsum[:, 2 * (w % 8):2 * (w % 8) + 2], ostat[:, 1, o2:o2 + 2]))
                    own.link(stt(out=ostat[:, 2, o2:o2 + 1], in0=ostat[:, 1, o2:o2 + 1],
                                 scalar=rsum[:, 2 * (w % 8) + 1:2 * (w % 8) + 2], in1=lamt[:, 6:7],
                                 op0=ALU.mult, op1=ALU.mult))
                    stt(out=sl[:, 0, 0:L], in0=sl[:, 1, 0:L], scalar=ostat[:, 2, o2:o2 + 1], in1=sl[:, 0, 0:L],
                        op0=ALU.mult, op1=ALU.add).then_inc(wg_done, 1)

                def scaled(a):
                    h, i = (4 * a) // nt, (4 * a) % nt
                    dve.wait_ge(av_done, 4 * (t0 + a) + 4)
                    tt(oatt[:, i:i + 4, h * P:(h + 1) * P], pb[6 + a % 2].rearrange("p (t n) -> p t n", t=4),
                       rsum[:, 8 * (a % 2):8 * (a % 2) + 8:2].unsqueeze(2).to_broadcast([P, 4, P]), ALU.mult
                       ).then_inc(o_scaled, 1)

                def summed(a):
                    h, i = (4 * a) // nt, (4 * a) % nt
                    dve.wait_ge(o_squared, t0 + a + 1)
                    dve.tensor_reduce(dts[:, 0, 0:4 * nt].rearrange("p (t h) -> p t h", h=4)[:, i:i + 4, h],
                                      osq[:, :].rearrange("p (t n) -> p t n", t=4), AX.X, ALU.add
                                      ).then_inc(o_summed, 1)

                k_lo(0)
                q_lo(0)
                for u in range(4 * nt + 1):
                    U = 4 * t0 + u
                    if u >= 1:
                        weights(u - 1)
                    for c_ in range(2):
                        if u < 4 * nt:
                            dve.wait_ge(sc_done, 2 * U + c_ + 1)
                            dve.tensor_reduce(ostat[:, 0, 2 * (u % 2) + c_:2 * (u % 2) + c_ + 1],
                                              psum[:, 1024 * c_:1024 * c_ + L], AX.X, ALU.max, negate=True
                                              ).then_inc(mx_done, 1)
                    if u % 4 == 1 and u // 4 + 1 < nt:
                        q_lo(u // 4 + 1)
                    if u % nt == 2 and u // nt + 1 < HEADS:
                        k_lo(u // nt + 1)
                    if u % 4 == 2 and u >= 6:
                        scaled(u // 4 - 1)
                    if u % 4 == 0 and u >= 8:
                        summed(u // 4 - 2)
                scaled(nt - 1)
                summed(nt - 1)
                dve.wait_ge(o_summed, t0 + nt)
                ts(dts[:, 1, 0:4 * nt], dts[:, 0, 0:4 * nt], 1.0 / P, EPS, ALU.mult, ALU.add).then_inc(osum_done, 1)
                dve.wait_ge(orms_done, s + 1)
                own.link(dve.reciprocal(dts[:, 3, 0:4 * nt], dts[:, 2, 0:4 * nt]))
                for i in range(nt):
                    tt(oatt[:, i, :].rearrange("p (h n) -> p h n", h=4),
                       oatt[:, i, :].rearrange("p (h n) -> p h n", h=4),
                       dts[:, 3, 4 * i:4 * i + 4].unsqueeze(2).to_broadcast([P, 4, P]), ALU.mult
                       ).then_inc(on_done, 1)
                end()

                phase(dve, ph + 2, phase_dve)
                W = 16 * nt
                sl = slice(0, W)

                def rep(ap):
                    return ap.unsqueeze(1).to_broadcast([P, nt, 16])

                def grid(i):
                    return dts[:, i, sl].rearrange("p (t n) -> p t n", n=16)

                own.link(tt(grid(5), grid(6), rep(p_("dt_bias")), ALU.add))
                own.link(ts(dts[:, 1, sl], dts[:, 5, sl], -1.0, None, ALU.mult))
                tt(dts[:, 1, sl], dts[:, 5, sl], dts[:, 1, sl], ALU.min).then_inc(dt_v, 1)
                dve.wait_ge(dt_a, 3 * s + 1)
                ts(dts[:, 3, sl], dts[:, 2, sl], 1.0, None, ALU.add).then_inc(dt_v, 1)
                dve.wait_ge(dt_v, 4 * s + 2)
                own.step(ts(dts[:, 8, sl], dts[:, 3, sl], -1.0, None, ALU.add))
                own.link(dve.reciprocal(dts[:, 9, sl], dts[:, 3, sl]))
                own.link(tt(dts[:, 8, sl], dts[:, 2, sl], dts[:, 8, sl], ALU.subtract))
                own.link(tt(dts[:, 8, sl], dts[:, 8, sl], dts[:, 9, sl], ALU.mult))
                dve.wait_ge(dt_a, 3 * s + 2)
                own.link(tt(dts[:, 8, sl], dts[:, 8, sl], dts[:, 4, sl], ALU.add))
                own.link(ts(dts[:, 5, sl], dts[:, 5, sl], 0.0, None, ALU.max))
                own.link(tt(dts[:, 5, sl], dts[:, 5, sl], dts[:, 8, sl], ALU.add))
                tt(grid(6), grid(5), rep(stat[:, 1, :]), ALU.mult).then_inc(dt_v, 1)
                dve.wait_ge(cs_done, s + 1)
                cs = pb[7]
                own.step(ts(grid(7)[:, :, 0:8], cs[:, 0:8 * nt].rearrange("p (t n) -> p t n", n=8), -1.0, None,
                            ALU.mult))
                own.step(ts(grid(7)[:, :, 8:16], cs[:, 64:64 + 8 * nt].rearrange("p (t n) -> p t n", n=8), -1.0, None,
                            ALU.mult))
                own.link(dve.tensor_copy(dts[:, 3, sl], cs[:, 128:128 + W]))
                tt(dts[:, 4, sl], dts[:, 3, sl], dts[:, 7, sl], ALU.add).then_inc(dt_v, 1)
                for cc in range(nt):
                    k = 8 * s + cc
                    dve.wait_ge(xt_done, k + 1)
                    for d in range(2):
                        tt(xf[:, cc, d, :].rearrange("p (h q) -> p h q", h=SH),
                           pb[0 if cc % 2 == 0 else 2][:, :].rearrange("p (h q) -> p h q", h=SH),
                           dts[:, 5, cc * 16 + 8 * d:cc * 16 + 8 * d + 8].unsqueeze(2).to_broadcast([P, SH, 64]),
                           ALU.mult).then_inc(xf_done, 1)
                dve.wait_ge(st_out, 2 * (8 * s + nt))
                dve.wait_ge(dt_a, 3 * s + 3)
                for cc in range(1, nt - 1):
                    own.link(tt(scan_t[0][:, :].rearrange("p (h q) -> p h q", h=SH),
                                state[0][:, cc, :].rearrange("p (h q) -> p h q", h=SH),
                                dts[:, 8, cc * 16:cc * 16 + 8].unsqueeze(2).to_broadcast([P, SH, 64]), ALU.mult))
                    own.link(tt(state[0][:, cc + 1, :], state[0][:, cc + 1, :], scan_t[0][:, :], ALU.add))
                end()

                phase(dve, ph + 3, phase_dve)
                def masked(n4):
                    n, d = 32 * s + n4, n4 % 2
                    dve.wait_ge(e_done, n + 1)
                    if n >= 2:
                        dve.wait_ge(l_done, n - 1)
                    tt(dr[:, n % 2, :].rearrange("p (h l) -> p h l", h=4),
                       row_bank(n).rearrange("p (h l) -> p h l", h=4),
                       c("neg_b" if d else "neg_f").unsqueeze(1).to_broadcast([P, 4, P]), ALU.add
                       ).then_inc(d_done, 1)

                masked(0)
                for n4 in range(4 * nt):
                    n = 32 * s + n4
                    cc, g, d = n4 // 4, (n4 // 2) % 2, n4 % 2
                    k = 8 * s + cc
                    if n4 + 1 < 4 * nt:
                        masked(n4 + 1)
                    dve.wait_ge(l_done, n + 1)
                    dve.wait_ge(cb_done, k + 1)
                    if n >= 2:
                        dve.wait_ge(yh_done, n - 1)
                    tt(mr[:, n % 2, :].rearrange("p (h l) -> p h l", h=4),
                       lr[:, n % 2, :].rearrange("p (h l) -> p h l", h=4),
                       pb[cc % 2][:, g * P:(g + 1) * P].unsqueeze(1).to_broadcast([P, 4, P]), ALU.mult
                       ).then_inc(m_done, 1)
                    if n4 % 4 == 3:
                        tk = slice(2 + cc * P, 2 + (cc + 1) * P)
                        dve.wait_ge(yh_done, n + 1)
                        for jj in range(4):
                            own.step(stt(out=xbc[:, jj, tk], in0=xbc[:, jj, tk], scalar=p_("d_skip", jj),
                                         in1=pb[4 + cc % 2][:, jj * P:(jj + 1) * P], op0=ALU.mult, op1=ALU.add))
                        own.wait()
                        dve.wait_ge(z_in[k % 2], 16 * (k // 2 + 1))
                        tt(xbc[:, 0:4, tk], xbc[:, 0:4, tk],
                           zin[:, k % 2, :].rearrange("p (j l) -> p j l", j=4), ALU.mult).then_inc(z_used, 1)
                end()

                phase(dve, ph + 4, phase_dve)
                for q in range(2 * (L // BLK)):
                    N = (4 if s else 0) + q
                    hf, g = q // 2, q % 2
                    dve.wait_ge(nsum_done, N + 1)
                    if q:
                        dve.wait_ge(nrms_done, N)
                    ts(rs[:, 1, :], pb[6 + q % 2][:, :], 1.0 / 256, EPS, ALU.mult, ALU.add).then_inc(nms_done, 1)
                    dve.wait_ge(nrms_done, N + 1)
                    own.link(dve.reciprocal(rs[:, 0, :], rs[:, 0, :]))
                    for i in range(2):
                        a = xbc[:, 2 * g + i, 2 + hf * BLK:2 + (hf + 1) * BLK]
                        stt(out=a, in0=a, scalar=p_("ssm_g", 2 * g + i), in1=rs[:, 0, :], op0=ALU.mult, op1=ALU.mult
                            ).then_inc(nrm_done, 1)
                for k in range(KT):
                    src = qT[:, k, 0:L] if k < 4 else xbc[:, k - 4, 2:2 + L]
                    dve.wait_ge(mix_hi_done, KT * s + k + 1)
                    tt(mix_lo[:, k, 0:L], src, mix_hi[:, k, 0:L].bitcast(F32), ALU.subtract
                       ).then_inc(mix_lo_done, 1)
                end()

                phase(dve, ph + 5, phase_dve)
                dve.wait_ge(x2_in, 16 * (s + 1))
                for jo in range(4):
                    split(FIRST_OUT_CHUNK[s] + jo + 1)
                    for i in range(nt):
                        u = nt * jo + i
                        dve.wait_ge(op_done, 4 * t0 + u + 1)
                        a = x2[:, i, jo * CW:(jo + 1) * CW]
                        tt(a, a, pb[u % 4][:, 0:CW], ALU.add).then_inc(op_out, 1)
                dve.wait_ge(ss2_done, t0 + nt)
                ts(small[:, 1, 0:nt], small[:, 0, 0:nt], 1.0 / D, EPS, ALU.mult, ALU.add).then_inc(rms2_done, 1)
                dve.wait_ge(rms2_done, 2 * s + 2)
                own.link(dve.reciprocal(small[:, 3, 0:nt], small[:, 2, 0:nt]))
                dve.wait_ge(gain_in, 16 * (2 * s + 2))
                for i in range(nt):
                    t = t0 + i
                    if t >= 2:
                        dve.wait_ge(h2_out[t % 2], 16 * (t // 2))
                        dve.wait_ge(h2_turned, 2 * (t - 1))
                    stt(out=h2[:, t % 2, :], in0=x2[:, i, :], scalar=small[:, 3, i:i + 1], in1=gain[:, :],
                        op0=ALU.mult, op1=ALU.mult).then_inc(h2_done, 1)
                dve.wait_ge(lg_done, t0 + nt)
                end()

                phase(dve, ph + 6, phase_dve)
                lg = pb[5][:, sl].rearrange("p (t n) -> p t n", n=NE)
                af = aff[:, sl].rearrange("p (t n) -> p t n", n=NE)
                own.link(dve.tensor_reduce(aff2[:, 0:nt], lg, AX.X, ALU.max))
                tt(af, lg, aff2[:, 0:nt].unsqueeze(2).to_broadcast([P, nt, NE]), ALU.subtract).then_inc(rt_v, 1)
                dve.wait_ge(rt_a, s + 1)
                own.link(dve.tensor_reduce(aff2[:, 16:16 + nt], af, AX.X, ALU.add))
                own.link(dve.reciprocal(aff2[:, 32:32 + nt], aff2[:, 16:16 + nt]))
                tt(af, af, aff2[:, 32:32 + nt].unsqueeze(2).to_broadcast([P, nt, NE]), ALU.mult).then_inc(rt_v, 1)
                dve.wait_ge(rt_p, s + 1)
                for q in range(L // 512):
                    own.step(dve.tensor_copy(affT[:, q * 512:(q + 1) * 512], pb[6 + q][0:NE, :]))
                own.wait()
                if s == 0:
                    end()
                    continue
                for n in range(cap // 8):
                    choose(s, n)
                chosen(s)
                dve.memset(mark[0:1, 9:10], 0.0).then_inc(rt_v, 1)
                dve.wait_ge(rt_p, 3)
                for i, (gate, idx) in enumerate(((gate_s, idx_s), (gate_p, idx_p))):
                    n = SEQS[i][3]
                    own.step(dve.tensor_copy(gate[:, :], pb[4 + i][0:n, 0:NE]))
                    own.link(dve.tensor_copy(idx[:, :], pb[4 + i][0:n, 16:16 + NE]))
                end()

            phase(dve, 14, phase_dve)
            dve.memset(mark[0:1, 10:11], 0.0).then_inc(tile_done, 2)
            dve.memset(mark[0:1, 11:12], 0.0).then_inc(red_done, 4)
            dve.memset(mark[0:1, 12:13], 0.0).then_inc(hm_done, 2)
            dve.memset(mark[0:1, 13:14], 0.0).then_inc(yp_done, 2)

            def next_indices(e1):
                dve.tensor_copy(gi_s[:, :], idx_s[:, bass.ds(e1, 1)])
                dve.tensor_copy(gi_p[:, :], idx_p[:, bass.ds(e1, 1)]).then_inc(idx_ready, 1)

            def turned_out(n):
                for kk in range(4):
                    dve.wait_ge(xhi_done, n * 4 + kk + 1)
                    tt(xT[:, 2 * kk:2 * kk + 2, TOK:2 * TOK],
                       pb[6 + kk % 2][:, 0:2 * TOK].rearrange("p (k n) -> p k n", k=2),
                       xT[:, 2 * kk:2 * kk + 2, 0:TOK].bitcast(F32), ALU.subtract).then_inc(xlo_done, 1)

            def expert(e, last):
                for j in range(ECH):
                    if j == 0 and not last:
                        dve.wait_ge(xs_in, e * 16 + 16)
                        dve.wait_ge(xp_in, e * 16 + 16)
                        next_indices(e + 1)
                    if j == 1:
                        dve.wait_ge(scattered, e + 1)
                        dve.tensor_copy(gcur_s[:, :], gate_s[:, bass.ds(e, 1)])
                        dve.tensor_copy(gcur_p[:, :], gate_p[:, bass.ds(e, 1)])
                        dve.tensor_copy(si_s[:, :], idx_s[:, bass.ds(e, 1)])
                        dve.tensor_copy(si_p[:, :], idx_p[:, bass.ds(e, 1)]).then_inc(cur_ready, 1)
                    if not (last and j >= ECH - 2):
                        i = j + 2
                        dve.wait_ge(w_hi_done, e * ECH + MOE_CHUNK + i + 1)
                        tt(moe_lo[i % 3], moe_raw[i % 4].rearrange("p (k n) -> p k n", k=KT),
                           moe_hi[i % 3].bitcast(F32), ALU.subtract).then_inc(w_lo_done, 1)
                    if j < 8:
                        for ft in range(2):
                            dve.wait_ge(tile_done, e * 24 + 2 + 2 * j + ft + 1)
                            dve.tensor_reduce((ur if j % 2 else gr)[:, ft, :],
                                              pb[2 * (j % 2) + ft][:, 0:2 * TOK].rearrange("p (a n) -> p n a", a=2),
                                              AX.X, ALU.add).then_inc(red_done, 1)
                    if j < 8 and j % 2:
                        for ft in range(2):
                            dve.wait_ge(silu_done, e * 8 + (j - 1) + ft + 1)
                            dve.wait_ge(red_done, e * 16 + 4 + 2 * j + ft + 1)
                            if j > 1:
                                dve.wait_ge(hlo_done, e * 8 + (j - 3) + ft + 1)
                            tt(hm[:, ft, :], sg[:, ft, :], ur[:, ft, :], ALU.mult).then_inc(hm_done, 1)
                    if j in (2, 4, 6, 7):
                        for ft in range(2):
                            f = (j - 2 if j < 7 else 6) + ft
                            dve.wait_ge(hhi_done, e * 8 + f + 1)
                            tt(hid[:, f, 256:384], hm[:, ft, 0:P], hid[:, f, 0:P].bitcast(F32), ALU.subtract)
                            tt(hid[:, f, 192:256], hm[:, ft, P:TOK], hid[:, f, P:TOK].bitcast(F32), ALU.subtract
                               ).then_inc(hlo_done, 1)
                    if j == 7 and not last:
                        turned_out(e + 1)
                    if j >= 8:
                        dc = j - 8
                        bank = pb[4 + dc % 2]
                        dve.wait_ge(tp_done, e * 4 + dc + 1)
                        dve.wait_ge(ys_done, e * 4 + dc + 1)
                        a = ye_p[:, dc * CW:(dc + 1) * CW]
                        own_tp = tt(a, bank[0:64, CW:2 * CW], tp[:, dc % 2, :], ALU.add)
                        own_tp.then_inc(half_added, 1)
                        dve.wait_ge(half_added, e * 4 + dc + 1)
                        ts(a, a, gcur_p[:, 0:1], None, ALU.mult).then_inc(yp_done, 1)

            next_indices(0)
            split(MOE_CHUNK + 1)
            turned_out(0)
            with dve.Fori(0, NE - 1) as e:
                expert(e, False)
            expert(NE - 1, True)

            dve.wait_ge(gain_in, 16 * 5)
            for t in range(NT):
                dve.wait_ge(fss, t + 1)
                ts(small[:, 1, t:t + 1], small[:, 0, t:t + 1], 1.0 / D, EPS, ALU.mult, ALU.add).then_inc(fms, 1)
                dve.wait_ge(frms, t + 1)
                own.link(dve.reciprocal(small[:, 3, t:t + 1], small[:, 2, t:t + 1]))
                if t >= 2:
                    dve.wait_ge(y_out[t % 2], 16 * (t // 2))
                stt(out=yout[:, t % 2, :], in0=yin[:, t % 2, :], scalar=small[:, 3, t:t + 1], in1=gain[:, :],
                    op0=ALU.mult, op1=ALU.mult).then_inc(fy, 1)

        @block.tensor
        def _(pe):
            mm = pe.matmul
            pe.wait_ge(cst_in, 16)
            pe.wait_ge(par_in, 16)

            def split3(out, wh, wl, xh, xl, first, final, **kw):
                mm(out, wh, xh, start=first, stop=False, **kw)
                mm(out, wh, xl, start=False, stop=False, **kw)
                return mm(out, wl, xh, start=False, stop=final, **kw)

            for s, (t0, nt, blocks, cap) in enumerate(SEQS):
                ph = 7 * s
                L = nt * P
                if s:
                    phase(pe, ph)
                for b in blocks:
                    for j in range(TPB):
                        t = TPB * b + j
                        pe.wait_ge(hn_done, t + 1)
                        if t:
                            pe.wait_ge(ht_lo_done, 2 * t)
                        for q in range(2):
                            for i in range(4):
                                k = 4 * q + i
                                last = pe.transpose(pb[6 + q][:, i * P:(i + 1) * P],
                                                    xin[:, t % 2, k * P:(k + 1) * P], ident)
                            last.then_inc(h_turned, 1)
                    pe.wait_ge(ht_lo_done, 2 * TPB * (b + 1))

                    def second_step(m):
                        r = NR * b + min(m - 8, 12)
                        pe.wait_ge(col_out, NM * b + m + 1)
                        if r >= 2:
                            pe.wait_ge(rot_out, r - 1)
                        bank = pb[4 + r % 2]
                        if m < 16:
                            mm(bank[:, :], c("rot"), stage[:, r % 2, :], start=True, stop=True
                               ).then_inc(turn_done, 1)
                        else:
                            for i in range(TPB):
                                last = pe.transpose(bank[:, i * P:(i + 1) * P], stage[:, r % 2, i * P:(i + 1) * P],
                                                    ident)
                            last.then_inc(turn_done, 1)

                    for m in range(NM):
                        n = NM * b + m
                        g = FIRST_CHUNK[b] + m // 2
                        if m % 2 == 0:
                            pe.wait_ge(w_lo_done, g + 1)
                        if n >= 4:
                            pe.wait_ge(col_out, n - (3 if m >= 4 else m))
                        cols = slice(P, 2 * P) if (m % 2 or m == 24) else slice(0, P)
                        for k in range(KT):
                            last = split3(pb[m % 4][:, :], whi[:, g % 2, k, cols], wlo[:, g % 2, k, cols],
                                          ht_hi[:, k, :], ht_lo[:, k, :], k == 0, k == KT - 1)
                        last.then_inc(col_done, 1)
                        if 9 <= m < 21:
                            second_step(m - 1)
                    second_step(24)

                phase(pe, ph + 1)
                for u in range(4 * nt + 2):
                    U = 4 * t0 + u
                    if u < 4 * nt:
                        h, i = u // nt, u % nt
                        if i == 0:
                            pe.wait_ge(klo_done, 2 * (HEADS * s + h) + 2)
                        if u % 4 == 0:
                            pe.wait_ge(qlo_done, 4 * (t0 + u // 4) + 4)
                        for c_ in range(2):
                            if u:
                                pe.wait_ge(exp_done, 2 * (U - 1) + c_ + 1)
                            for q in range(L // BLK):
                                kk = khl[:, h % 2, c_, q * BLK:(q + 1) * BLK]
                                sl = qhl[:, (u // 4) % 2, :, (u % 4) * P:(u % 4 + 1) * P]
                                mm(pb[2 * c_ + q], sl[:, c_, :], kk, start=True, stop=False)
                                last = mm(pb[2 * c_ + q], sl[:, 2 + c_, :], kk, start=False, stop=True)
                            last.then_inc(sc_done, 1)
                    if 1 <= u <= 4 * nt:
                        w, W = u - 1, U - 1
                        pe.wait_ge(wg_done, W + 1)
                        if w:
                            pe.wait_ge(wt_out, W)
                        for kk in range(nt):
                            last = pe.transpose(psum[:, 2048 + kk * P:2048 + (kk + 1) * P],
                                                prob[s][w % 2][:, 0, kk * P:(kk + 1) * P], ident)
                        last.then_inc(wt_done, 1)
                    if u >= 2:
                        w, W = u - 2, U - 2
                        h = w // nt
                        pe.wait_ge(wt_out, W + 1)
                        if w % 4 == 0 and w >= 8:
                            pe.wait_ge(o_scaled, t0 + w // 4 - 1)
                        for kk in range(nt):
                            last = mm(pb[6 + (w // 4) % 2][:, (w % 4) * P:(w % 4 + 1) * P],
                                      wgtT[:, w % 2, kk * P:(kk + 1) * P], v[:, kk, h * P:(h + 1) * P],
                                      start=(kk == 0), stop=(kk == nt - 1))
                        last.then_inc(av_done, 1)
                for i in range(nt):
                    pe.wait_ge(on_done, t0 + i + 1)
                    if i >= 2:
                        pe.wait_ge(ot_out, t0 + i - 1)
                    for h in range(4):
                        last = pe.transpose(pb[i % 2][:, h * P:(h + 1) * P], oatt[:, i, h * P:(h + 1) * P], ident)
                    last.then_inc(ot_done, 1)

                phase(pe, ph + 2)
                a3 = dts[:, 6, 0:16 * nt].rearrange("p (t n) -> p t n", n=16)
                pe.wait_ge(dt_v, 4 * s + 3)
                mm(pb[7][:, 0:8 * nt], c("cum_f"), a3[:, :, 0:8], start=True, stop=True)
                mm(pb[7][:, 64:64 + 8 * nt], c("cum_b"), a3[:, :, 8:16], start=True, stop=True)
                mm(pb[7][:, 128:128 + 16 * nt], c("ones"), dts[:, 6, 0:16 * nt], start=True, stop=True
                   ).then_inc(cs_done, 1)
                for cc in range(nt + 1):
                    k = 8 * s + cc
                    if cc < nt:
                        tk = slice(2 + cc * P, 2 + (cc + 1) * P)
                        if cc >= 2:
                            pe.wait_ge(xf_done, 2 * (k - 1))
                            pe.wait_ge(bt_out, k - 1)
                        for i in range(4):
                            last = pe.transpose(pb[0 if cc % 2 == 0 else 2][:, i * P:(i + 1) * P], xbc[:, i, tk], ident)
                        last.then_inc(xt_done, 1)
                        for i in range(2):
                            last = pe.transpose(pb[1 if cc % 2 == 0 else 3][:, i * P:(i + 1) * P], xbc[:, 4 + i, tk],
                                                ident)
                        last.then_inc(bt_done, 1)
                    if cc >= 1:
                        k -= 1
                        c1 = cc - 1
                        pe.wait_ge(bt_out, k + 1)
                        for d in range(2):
                            pe.wait_ge(xs_done, 2 * k + d + 1)
                            if c1:
                                pe.wait_ge(st_out, 2 * k + d - 1)
                            for g in range(2):
                                mm(pb[4 + d][:, g * 256:(g + 1) * 256], btok[:, c1 % 2, g * P:(g + 1) * P],
                                   xs[:, c1 % 2, d, g * 256:(g + 1) * 256], start=True, stop=True
                                   ).then_inc(st_done, 1)

                phase(pe, ph + 3)

                def rows_of(n4):
                    n = 32 * s + n4
                    cc, g, d = n4 // 4, (n4 // 2) % 2, n4 % 2
                    if n4 >= 3:
                        pe.wait_ge(d_done, n - 2)
                    for hh in range(4):
                        col = cc * 16 + 8 * d + 4 * g + hh
                        last = mm(row_bank(n)[:, hh * P:(hh + 1) * P],
                                  dts[:, 6, col:col + 1].to_broadcast([P, P]), c("cum_b" if d else "cum_f"),
                                  start=True, stop=True)
                    last.then_inc(row_done, 1)

                rows_of(0)
                rows_of(1)
                for n4 in range(4 * nt):
                    n = 32 * s + n4
                    cc, g, d = n4 // 4, (n4 // 2) % 2, n4 % 2
                    k = 8 * s + cc
                    if n4 % 4 == 0:
                        tk = slice(2 + cc * P, 2 + (cc + 1) * P)
                        if cc >= 2:
                            pe.wait_ge(m_done, n - 4)
                        for gg in range(2):
                            last = mm(pb[cc % 2][:, gg * P:(gg + 1) * P], xbc[:, 4 + gg, tk], xbc[:, 6 + gg, tk],
                                      start=True, stop=True)
                        last.then_inc(cb_done, 1)
                        if cc >= 2:
                            pe.wait_ge(z_used, k - 1)
                    if n4 + 2 < 4 * nt:
                        rows_of(n4 + 2)
                    pe.wait_ge(m_done, n + 1)
                    pe.wait_ge(c_done, n + 1)
                    ybank = pb[4 + cc % 2]
                    for hh in range(4):
                        h = 4 * g + hh
                        out = ybank[64 * (h % 2):64 * (h % 2) + 64, (h // 2) * P:(h // 2 + 1) * P]
                        last = mm(out, xf[:, cc, d, h * 64:(h + 1) * 64], mr[:, n % 2, hh * P:(hh + 1) * P],
                                  start=(g == 0 and d == 0 and hh < 2), stop=(d == 1), skip_group_check=True)
                        if cc > 0 if d == 0 else cc < nt - 1:
                            last = mm(out, state[d][:, cc, h * 64:(h + 1) * 64], cr[:, n % 2, hh * P:(hh + 1) * P],
                                      start=False, stop=(d == 1), skip_group_check=True)
                    last.then_inc(yh_done, 1)

                phase(pe, ph + 4)
                for q in range(2 * (L // BLK)):
                    N = (4 if s else 0) + q
                    pe.wait_ge(sq_done, 2 * (N + 1))
                    if q >= 2:
                        pe.wait_ge(nms_done, N - 1)
                    for i in range(2):
                        last = mm(pb[6 + q % 2][:, :], c("ones"), sq[:, i, :], start=(i == 0), stop=(i == 1))
                    last.then_inc(nsum_done, 1)

                phase(pe, ph + 5)
                for jo in range(4):
                    g = FIRST_OUT_CHUNK[s] + jo
                    pe.wait_ge(w_lo_done, g + 1)
                    for i in range(nt):
                        u = nt * jo + i
                        if u >= 4:
                            pe.wait_ge(op_out, 4 * t0 + u - 3)
                        for k in range(KT):
                            last = split3(pb[u % 4][:, 0:CW], mix_hi[:, k, i * P:(i + 1) * P],
                                          mix_lo[:, k, i * P:(i + 1) * P], whi[:, g % 2, k, :], wlo[:, g % 2, k, :],
                                          k == 0, k == KT - 1)
                        last.then_inc(op_done, 1)
                for i in range(nt + 1):
                    t = t0 + i
                    if i < nt:
                        pe.wait_ge(h2_done, t + 1)
                        if i:
                            pe.wait_ge(h2T_out, 2 * t)
                        for q in range(2):
                            for kk in range(4):
                                k = 4 * q + kk
                                last = pe.transpose(pb[6 + q][:, kk * P:(kk + 1) * P], h2[:, t % 2, k * P:(k + 1) * P],
                                                    ident)
                            last.then_inc(h2_turned, 1)
                    if i >= 1:
                        pe.wait_ge(h2T_out, 2 * t)
                        for k in range(KT):
                            last = mm(pb[5][:, (i - 1) * NE:i * NE], h2T[:, (t - 1) % 2, k, :],
                                      p_("router", k * NE, NE), start=(k == 0), stop=(k == KT - 1))
                        last.then_inc(lg_done, 1)

                phase(pe, ph + 6)
                pe.wait_ge(rt_v, 2 * s + 2)
                for i in range(nt):
                    last = pe.transpose(pb[6 + i // 4][0:NE, (i % 4) * P:(i % 4 + 1) * P], aff[:, i * NE:(i + 1) * NE],
                                        ident)
                last.then_inc(rt_p, 1)
            pe.wait_ge(rt_v, 5)
            for i in range(2):
                n = SEQS[i][3]
                cols = slice(128 * i, 128 * i + n)
                pe.transpose(pb[4 + i][0:n, 0:NE], topv[:, cols], ident[0:NE, 0:NE])
                last = pe.transpose(pb[4 + i][0:n, 16:16 + NE], topf[:, cols], ident[0:NE, 0:NE])
            last.then_inc(rt_p, 1)

            phase(pe, 14)
            pe.wait_ge(hm_done, 2)

            def turn(n):
                pe.wait_ge(xs_in, n * 16 + 16)
                pe.wait_ge(xp_in, n * 16 + 16)
                for kk in range(4):
                    if kk >= 2:
                        pe.wait_ge(xlo_done, n * 4 + kk - 1)
                    for i in range(2):
                        k = 2 * kk + i
                        bank = pb[6 + kk % 2]
                        pe.transpose(bank[:, i * TOK:i * TOK + P], xe_s[:, k * P:(k + 1) * P], ident)
                        last = pe.transpose(bank[:, i * TOK + P:(i + 1) * TOK], xe_p[:, k * P:(k + 1) * P],
                                            ident[0:64, 0:64])
                    last.then_inc(xturn, 1)

            def expert(e, last_one):
                pe.wait_ge(xlo_done, e * 4 + 4)
                for j in range(8):
                    hi, lo = moe_hi[j % 3], moe_lo[j % 3]
                    pe.wait_ge(w_lo_done, e * ECH + MOE_CHUNK + j + 1)
                    for ft in range(2):
                        q = 2 * j + ft
                        pe.wait_ge(red_done, e * 16 + q + 1)
                        bank = pb[2 * (j % 2) + ft]
                        cols = slice(ft * P, (ft + 1) * P)
                        for k in range(KT):
                            mm(bank[:, 0:2 * TOK], hi[:, k, cols], xT[:, k, :], start=(k == 0), stop=False)
                            last = mm(bank[:, 0:TOK], lo[:, k, cols], xT[:, k, 0:TOK], start=False,
                                      stop=(k == KT - 1))
                        last.then_inc(tile_done, 1)
                if not last_one:
                    turn(e + 1)
                pe.wait_ge(hlo_done, e * 8 + 8)
                for j in range(8, ECH):
                    hi, lo = moe_hi[j % 3], moe_lo[j % 3]
                    dc = j - 8
                    pe.wait_ge(w_lo_done, e * ECH + MOE_CHUNK + j + 1)
                    pe.wait_ge(yp_done, e * 4 + dc + 1)
                    bank = pb[4 + dc % 2]
                    for k in range(KT):
                        last = split3(bank[:, 0:CW], hid[:, k, 0:P], hid[:, k, 256:384], hi[:, k, :],
                                      lo[:, k, :], k == 0, k == KT - 1)
                    last.then_inc(tile_done, 1)
                    for k in range(KT):
                        mm(bank[:, CW:2 * CW], hid[:, k, P:256], hi[:, k, :], start=(k == 0), stop=False)
                        last = mm(bank[:, CW:2 * CW], hid[:, k, P:256], lo[:, k, :], start=False,
                                  stop=(k == KT - 1))
                    last.then_inc(tile_done, 1)

            turn(0)
            with pe.Fori(0, NE - 1) as e:
                expert(e, False)
            expert(NE - 1, True)


def _chunks(w, cols):
    import numpy as np
    return np.stack([np.ascontiguousarray(w[:, c0:c0 + 256].reshape(8, 128, 256).transpose(1, 0, 2)).reshape(128, 2048)
                     for c0 in cols])


def _shape_constants():
    import numpy as np
    i = np.arange(128)
    ident = np.eye(128, dtype=np.float32)
    cum_f = (i[:, None] <= i[None, :]).astype(np.float32)
    cum_b = (i[:, None] >= i[None, :]).astype(np.float32)
    rot = np.zeros((128, 128), np.float32)
    cos = np.ones((128, 1024), np.float32)
    sin = np.zeros((128, 1024), np.float32)
    inv = np.power(np.float32(500000.0), -np.arange(8, dtype=np.float32) * np.float32(2.0) / np.float32(16))
    ang = np.arange(1024, dtype=np.float32)[None, :] * inv.astype(np.float32)[:, None]
    for half in (0, 64):
        for r in range(8):
            rot[half + 8 + r, half + r] = -1.0
            rot[half + r, half + 8 + r] = 1.0
        for q in (0, 8):
            cos[half + q:half + q + 8] = np.cos(ang)
            sin[half + q:half + q + 8] = np.sin(ang)
    big = np.float32(-1e30)
    consts = np.concatenate([ident, cum_f, cum_b, (1 - cum_f) * big, (1 - cum_b) * big, rot,
                             np.ones((128, 128), np.float32)], 1).astype(np.float32)
    return consts, np.stack([cos, sin])


def kernel(x_prompt, x_sample, norm1_g, w_in, lam_qk, attn_sub_g, conv_w, conv_b, dt_bias, a_log, d_skip, ssm_norm_g,
           w_out, norm2_g, w_router, w_gate, w_up, w_down, final_g):
    import numpy as np
    import concourse.bacc as _bacc
    from concourse import mybir as _mybir
    from concourse.bass_utils import run_bass_kernel_spmd as _run

    A = np.asarray
    x = np.concatenate([A(x_sample)[0], A(x_prompt)[0]], 0)
    wi = A(w_in)[0]
    in_cols = [2048 + 256 * i for i in range(4)] + [256 * i for i in range(8)] + [wi.shape[1] - 256]
    wg, wu, wd = A(w_gate)[0], A(w_up)[0], A(w_down)[0]
    cols = [0, 256, 512, 768]
    moe = np.empty((16 * 12, 128, 2048), wg.dtype)
    for e in range(16):
        moe[12 * e:12 * e + 8:2] = _chunks(wg[e], cols)
        moe[12 * e + 1:12 * e + 8:2] = _chunks(wu[e], cols)
        moe[12 * e + 8:12 * e + 12] = _chunks(wd[e], cols)
    row = lambda a: np.broadcast_to(A(a).reshape(1, -1), (128, A(a).size))
    part = lambda a: A(a).reshape(-1, 128).T
    params = np.concatenate([
        A(conv_w)[0].T.reshape(8, 128, 5).transpose(1, 0, 2).reshape(128, 40), part(conv_b),
        part(np.repeat(A(d_skip)[0], 64)), part(ssm_norm_g), part(attn_sub_g), row(dt_bias), row(a_log), row(lam_qk),
        A(w_router)[0].reshape(8, 128, 16).transpose(1, 0, 2).reshape(128, 128)], 1)
    gains = np.stack([np.broadcast_to(A(g).reshape(1, -1), (128, 1024)) for g in (norm1_g, norm2_g, final_g)])
    consts, rope = _shape_constants()
    arrays = {"x": x, "w_in_chunks": _chunks(wi, in_cols), "w_out_chunks": _chunks(A(w_out)[0], cols),
              "moe_chunks": moe, "params": params, "consts": consts, "rope": rope, "gains": gains}
    arrays = {k: np.ascontiguousarray(a) for k, a in arrays.items()}

    nc = _bacc.Bacc("TRN2", target_bir_lowering=False, num_devices=1)
    args = [nc.dram_tensor(k, a.shape, _mybir.dt.from_np(a.dtype), kind="ExternalInput").ap()
            for k, a in arrays.items()]
    args.append(nc.dram_tensor("y", x.shape, _mybir.dt.float32, kind="ExternalOutput").ap())
    hybrid_encoder(nc, *args)
    r = _run(nc, [arrays], core_ids=[0])
    y = r.results[0]["y"]
    return y[None, 1024:], y[None, :1024]
```

```python
from contextlib import ExitStack

import concourse.bass as bass
from concourse import mybir

ALU = mybir.AluOpType
ACT = mybir.ActivationFunctionType
AX = mybir.AxisListType
F32 = mybir.dt.float32
F32R = mybir.dt.float32r
BF16 = mybir.dt.bfloat16
U32 = mybir.dt.uint32

P = 128
D = 1024
KT = D // P
CW = 256
BLK = 512
TPB = BLK // P
EPS = 1e-6
LAM_INIT = 0.2
HEADS = 4
SH = 8
NE = 16
NM = 25
NCH = 13
NR = 13
SEQS = [(0, 8, (0, 1), 128), (8, 4, (2,), 64)]
NT = 12
FIRST_CHUNK = {0: 0, 1: 13, 2: 30}
FIRST_OUT_CHUNK = (26, 43)
MOE_CHUNK = 47
ECH = 12
TOK = 192

PAR = {}
_at = 0
for _name, _w in (("conv_w", 40), ("conv_b", 8), ("d_skip", 4), ("ssm_g", 4), ("sub_g", 1), ("dt_bias", 16),
                  ("a_log", 16), ("lam", 256), ("router", KT * NE)):
    PAR[_name] = (_at, _at + _w)
    _at += _w
NPAR = _at
CST = {n: (i * P, i * P + P) for i, n in enumerate(("ident", "cum_f", "cum_b", "neg_f", "neg_b", "rot", "ones"))}
NCST = P * len(CST)


class Order:

    def __init__(self, engine, sem):
        self.engine, self.sem, self.n = engine, sem, 0

    def step(self, ins):
        self.n += 1
        ins.then_inc(self.sem, 1)

    def wait(self):
        self.engine.wait_ge(self.sem, self.n)

    def link(self, ins):
        self.step(ins)
        self.wait()


def hybrid_encoder(nc, x, w_in, w_out, w_moe, params, consts, rope, gains, y):
    ctx = ExitStack()
    KB = 1024
    base = 16640

    def at(name, kb, shape, dt=F32):
        return nc.alloc_sbuf_tensor_at(name, shape, dt, offset=base + int(kb * KB) // 32 * 32)

    def sem(name):
        return ctx.enter_context(nc.semaphore(name))

    with ctx:
        wraw = at("wraw", 0, [P, 2, KT * CW])
        whi = at("whi", 16, [P, 2, KT, CW], F32R)
        wlo = at("wlo", 32, [P, 2, KT, CW], F32R)
        ht_hi = at("ht_hi", 48, [P, KT, BLK], F32R)
        ht_lo = at("ht_lo", 64, [P, KT, BLK], F32R)
        qT = at("qT", 80, [P, HEADS, 1024])
        kT = at("kT", 96, [P, HEADS, 1024])
        v = at("v", 112, [P, 8, 512])
        LX = 1028
        xbc = at("xbc", 128, [P, 8, LX])
        S0 = 160.25
        conv_acc = at("conv_acc", S0, [P, 1024])
        cos_t = at("cos_t", S0 + 4, [P, BLK])
        sin_t = at("sin_t", S0 + 6, [P, BLK])
        stage = at("stage", S0 + 8, [P, 2, BLK])
        tmp = at("tmp", S0 + 12, [P, 2, BLK])
        xin = at("xin", S0 + 16, [P, 2, D])
        khl = at("khl", 48, [P, 2, 2, 1024], F32R)
        qhl = at("qhl", 64, [P, 2, 4, BLK], F32R)
        prob = [[at(f"prob{s}{i}", 16 + 16 * i + 8 * (1 - FIRST_OUT_CHUNK[s] % 2), [P, 2, 1024]) for i in range(2)]
                for s in range(2)]
        wgtT = at("wgtT", S0 + 16, [P, 2, 1024])
        oatt = at("oatt", S0, [P, 8, 512])
        xf = at("xf", 48, [P, 8, 2, 512])
        state = [at("state_f", 96, [P, 8, 512]), at("state_b", 112, [P, 8, 512])]
        xs = at("xs", S0, [P, 2, 2, 512])
        btok = at("btok", S0 + 8, [P, 2, 256])
        scan_t = [at("scan_f", S0 + 10, [P, 512]), at("scan_b", 188.5, [P, 512])]
        er = at("er", S0, [P, 2, 512])
        dr = at("dr", S0 + 4, [P, 2, 512])
        lr = at("lr", S0 + 8, [P, 2, 512])
        mr = at("mr", S0 + 12, [P, 2, 512])
        cr = at("cr", S0 + 16, [P, 2, 512])
        zin = at("zin", S0 + 20, [P, 2, 512])
        sq = at("sq", S0, [P, 8, BLK])
        mix_hi = at("mix_hi", 48, [P, KT, 1024], F32R)
        mix_lo = at("mix_lo", 96, [P, KT, 1024], F32R)
        x2 = at("x2", 128, [P, 8, D])
        h2 = at("h2", S0, [P, 4, D])
        h2T = at("h2T", 84, [P, 2, KT, P])
        gain2 = at("gain2", 92, [P, D])
        aff = at("aff", 80, [P, P])
        aff2 = at("aff2", 80.5, [P, P])
        lgT = at("lgT", 124, [NE, 1024])
        affT = at("affT", 120, [NE, 1024])
        xe_s = at("xe_s", 48, [P, D])
        xe_p = at("xe_p", 52, [64, D])
        xT = at("xT", 56, [P, KT, 2 * TOK], F32R)
        hid = at("hid", 68, [P, KT, 2 * TOK], F32R)
        gr = at("gr", 80, [P, 2, TOK])
        ur = at("ur", 82, [P, 2, TOK])
        sg = at("sg", 84, [P, 2, TOK])
        hm = at("hm", 86, [P, 2, TOK])
        ye_s = at("ye_s", 88, [P, D])
        ye_p = at("ye_p", 92, [64, D])
        tp = at("tp", 96, [64, 2, CW])
        wraw_x = at("wraw_x", 128, [P, 2, KT * CW])
        whi_x = at("whi_x", 144, [P, KT, CW], F32R)
        wlo_x = at("wlo_x", 152, [P, KT, CW], F32R)
        old = (MOE_CHUNK % 2, 1 - MOE_CHUNK % 2)
        moe_raw = [wraw[:, old[0], :], wraw[:, old[1], :], wraw_x[:, 0, :], wraw_x[:, 1, :]]
        moe_hi = [whi[:, old[0]], whi[:, old[1]], whi_x[:, :, :]]
        moe_lo = [wlo[:, old[0]], wlo[:, old[1]], wlo_x[:, :, :]]
        yin = at("yin", 100, [P, 4, D])
        yout = at("yout", 116, [P, 3, D])
        gain = at("gain", 184.5, [P, D])
        junk = at("junk", 188.5, [P, D], BF16)
        osq = at("osq", 188.5, [P, 512])
        cst = at("cst", 190.5, [P, NCST])
        par = at("par", 194, [P, NPAR])
        o = 194 + NPAR * 4 / KB + 0.1
        small = at("small", o, [P, 8, NT])
        dts = at("dts", o + 0.5, [P, 10, P])
        o += 5.6
        stat = at("stat", o, [P, 2, 16])
        ostat = at("ostat", o + 0.25, [P, 3, 32])
        lamt = at("lamt", o + 0.75, [P, 16])
        asum = at("asum", o + 4.1, [P, 4, 32])
        rsum = at("rsum", o + 0.81, [P, 16])
        topv = at("topv", o + 0.9, [NE, TOK])
        topi = at("topi", o + 1.65, [NE, TOK], U32)
        topf = at("topf", o + 2.4, [NE, TOK])
        o += 0.75
        gate_s = at("gate_s", o + 2.4, [P, NE])
        gate_p = at("gate_p", o + 2.5, [64, NE])
        idx_s = at("idx_s", o + 2.6, [P, NE], U32)
        idx_p = at("idx_p", o + 2.7, [64, NE], U32)
        gcur_s = at("gcur_s", o + 2.8, [P, 1])
        gcur_p = at("gcur_p", o + 2.85, [64, 1])
        gi_s = at("gi_s", o + 2.9, [P, 1], U32)
        gi_p = at("gi_p", o + 2.95, [64, 1], U32)
        si_s = at("si_s", o + 3.0, [P, 1], U32)
        si_p = at("si_p", o + 3.05, [64, 1], U32)
        pmark2 = at("pmark2", o + 3.3, [1, 8])
        pmark = at("pmark", o + 3.2, [1, 8])
        mark = at("mark", o + 3.1, [1, 16])
        psum = ctx.enter_context(nc.psum_tensor("psum", [P, 8 * 512], F32))
        pb = [psum[:, i * 512:(i + 1) * 512] for i in range(8)]

        z_dram = nc.dram_tensor("z_scratch", (3, P, 4, BLK), F32).ap()
        h2_dram = nc.dram_tensor("h2_scratch", (NT * P, D), F32).ap()
        acc_dram = nc.dram_tensor("acc_scratch", (NT * P, D), F32).ap()

        def c(name):
            a, b = CST[name]
            return cst[:, a:b]

        def p_(name, i=None, n=None):
            a, b = PAR[name]
            return par[:, a:b] if i is None else par[:, a + i:a + i + (n or 1)]

        ident = c("ident")

        cst_in, par_in = sem("cst_in"), sem("par_in")
        gain_in = sem("gain_in")
        rope_in = sem("rope_in")
        raw_in = [sem("raw_in0"), sem("raw_in1")]
        raw_x_in = [sem("raw_x_in0"), sem("raw_x_in1")]
        moe_raw_in = [(raw_in[old[0]], MOE_CHUNK // 2), (raw_in[old[1]], (MOE_CHUNK + 1) // 2),
                      (raw_x_in[0], 0), (raw_x_in[1], 0)]
        w_hi_done, w_lo_done = sem("w_hi_done"), sem("w_lo_done")
        xin_in = [sem("xin_in0"), sem("xin_in1")]
        ss_done, ms_done, rms_done, hn_done = sem("ss_done"), sem("ms_done"), sem("rms_done"), sem("hn_done")
        h_turned, ht_hi_done, ht_lo_done = sem("h_turned"), sem("ht_hi_done"), sem("ht_lo_done")
        col_done, col_out, turn_done, rot_out = sem("col_done"), sem("col_out"), sem("turn_done"), sem("rot_out")
        z_out = [sem("z_out0"), sem("z_out1")]
        conv_done, conv_act = sem("conv_done"), sem("conv_act")
        phase_act, phase_dve, phase_pool = sem("phase_act"), sem("phase_dve"), sem("phase_pool")
        sc_done, mx_done, exp_done = sem("sc_done"), sem("mx_done"), sem("exp_done")
        khi_done, klo_done, qhi_done, qlo_done = sem("khi_done"), sem("klo_done"), sem("qhi_done"), sem("qlo_done")
        o_scaled, o_squared, o_summed = sem("o_scaled"), sem("o_squared"), sem("o_summed")
        wg_done, wt_done, wt_out, av_done = sem("wg_done"), sem("wt_done"), sem("wt_out"), sem("av_done")
        osum_done, orms_done, on_done, ot_done, ot_out = (sem("osum_done"), sem("orms_done"), sem("on_done"),
                                                          sem("ot_done"), sem("ot_out"))
        dt_v, dt_a, cs_done = sem("dt_v"), sem("dt_a"), sem("cs_done")
        xt_done, bt_done, xf_done, bt_out, xs_done = (sem("xt_done"), sem("bt_done"), sem("xf_done"), sem("bt_out"),
                                                      sem("xs_done"))
        st_done, st_out, scan_b_done = sem("st_done"), sem("st_out"), sem("scan_b_done")
        cb_done, cb_used, row_done, e_done, d_done, l_done = (sem("cb_done"), sem("cb_used"), sem("row_done"),
                                                              sem("e_done"), sem("d_done"), sem("l_done"))
        m_done, c_done, yh_done, y_done, y_used = (sem("m_done"), sem("c_done"), sem("yh_done"), sem("y_done"),
                                                   sem("y_used"))
        z_in = [sem("z_in0"), sem("z_in1")]
        z_used = sem("z_used")
        sq_done, nsum_done, nms_done, nrms_done, nrm_done = (sem("sq_done"), sem("nsum_done"), sem("nms_done"),
                                                             sem("nrms_done"), sem("nrm_done"))
        ninv_done, nrow_done = sem("ninv_done"), sem("nrow_done")
        mix_hi_done = sem("mix_hi_done")
        x2_in = [sem(f"x2_in{i}") for i in range(4)]
        op_done, op_out = sem("op_done"), sem("op_out")
        ms2_done = sem("ms2_done")
        ss2_done, rms2_done, h2_done, h2_turned, h2T_out = (sem("ss2_done"), sem("rms2_done"), sem("h2_done"),
                                                            sem("h2_turned"), sem("h2T_out"))
        x2_out = [sem(f"x2_out{i}") for i in range(4)]
        h2_out = [sem(f"h2_out{i}") for i in range(4)]
        lg_done = sem("lg_done")
        rt_v, rt_a, rt_p = sem("rt_v"), sem("rt_a"), sem("rt_p")
        own_dve, own_act, own_pool = sem("own_dve"), sem("own_act"), sem("own_pool")
        idx_ready, cur_ready = sem("idx_ready"), sem("cur_ready")
        xs_in, xp_in = sem("xs_in"), sem("xp_in")
        xturn, xhi_done, xlo_done = sem("xturn"), sem("xhi_done"), sem("xlo_done")
        tile_done, red_done, silu_done, hm_done = sem("tile_done"), sem("red_done"), sem("silu_done"), sem("hm_done")
        hhi_done, hlo_done = sem("hhi_done"), sem("hlo_done")
        ys_done, tp_done, yp_done = sem("ys_done"), sem("tp_done"), sem("yp_done")
        sc_s, sc_p = sem("sc_s"), sem("sc_p")
        y_in = [sem(f"y_in{i}") for i in range(4)]
        fss, fms, frms, fy = sem("fss"), sem("fms"), sem("frms"), sem("fy")
        y_out = [sem(f"y_out{i}") for i in range(3)]
        half_added, adds_done, scattered = sem("half_added"), sem("adds_done"), sem("scattered")

        block = ctx.enter_context(nc.Block())

        def block_tile(b):
            return {0: 0, 1: TPB, 2: 0}[b]

        def chunk_used(eng, g):
            if g < 0:
                return
            for s in (1, 0):
                if g >= FIRST_OUT_CHUNK[s] and (s == 1 or g < FIRST_CHUNK[2]):
                    nt = SEQS[s][1]
                    done = 4 * SEQS[0][1] if s else 0
                    eng.wait_ge(op_done, done + nt * (g - FIRST_OUT_CHUNK[s] + 1))
                    return
            b = max(b for b in range(3) if g >= FIRST_CHUNK[b])
            eng.wait_ge(col_done, NM * b + min(2 * (g - FIRST_CHUNK[b] + 1), NM))

        def turn_bank(t, q):
            return pb[(6, 4)[t % 2] + q]

        def row_bank(n):
            return pb[(2, 3, 6)[n % 3]]

        Q_PIECES = ((0, 0), (0, 1), (1, 1), (1, 0))

        def q_pieces(u):
            return (Q_PIECES[0:1], Q_PIECES[1:2], Q_PIECES[2:4], ())[u % 4]

        def k_pieces(u, nt):
            return [c_ for c_ in range(2) if u % nt == nt - 3 + c_]

        def phase(eng, n, but=None):
            for s in (phase_act, phase_dve, phase_pool):
                if s is not but:
                    eng.wait_ge(s, n)


        @block.sync
        def _(sp):
            sp.dma_start(cst[:, :], consts).then_inc(cst_in, 16)
            sp.dma_start(par[:, :], params).then_inc(par_in, 16)

            def load(g, src):
                if g >= 2:
                    sp.wait_ge(w_lo_done, g - 1)
                sp.dma_start(wraw[:, g % 2, :], src).then_inc(raw_in[g % 2], 16)

            for s, (_, _, blocks, _) in enumerate(SEQS):
                for b in blocks:
                    for j in range(NCH):
                        load(FIRST_CHUNK[b] + j, w_in[j])
                for j in range(4):
                    load(FIRST_OUT_CHUNK[s] + j, w_out[j])
            load(MOE_CHUNK, w_moe[0])
            load(MOE_CHUNK + 1, w_moe[1])
            phase(sp, 13)
            for i in (2, 3):
                sp.dma_start(moe_raw[i], w_moe[i]).then_inc(moe_raw_in[i][0], 16)

            def load_moe(e, j):
                sp.wait_ge(w_lo_done, e * ECH + (MOE_CHUNK + j + 1))
                sp.dma_start(moe_raw[j % 4], w_moe[bass.ds(e * ECH + j + 4, 1), :, :].rearrange("a p n -> (a p) n")
                             ).then_inc(moe_raw_in[j % 4][0], 16)

            with sp.Fori(0, NE - 1) as e:
                for j in range(ECH):
                    load_moe(e, j)
            for j in range(ECH - 4):
                sp.wait_ge(w_lo_done, (NE - 1) * ECH + MOE_CHUNK + j + 1)
                sp.dma_start(moe_raw[j % 4], w_moe[(NE - 1) * ECH + j + 4]).then_inc(moe_raw_in[j % 4][0], 16)
            sp.wait_ge(sc_s, 16 * NE)
            sp.wait_ge(sc_p, 16 * NE)
            for t in range(NT + 3):
                if t < NT:
                    if t >= 4:
                        sp.wait_ge(fy, t - 3)
                    sp.dma_start(yin[:, t % 4, :], acc_dram[t * P:(t + 1) * P, :]).then_inc(y_in[t % 4], 16)
                if t >= 3:
                    i = t - 3
                    sp.wait_ge(fy, i + 1)
                    sp.dma_start(y[i * P:(i + 1) * P, :], yout[:, i % 3, :]).then_inc(y_out[i % 3], 16)
            for i in range(3):
                sp.wait_ge(y_out[i], 16 * (NT // 3))

        @block.gpsimd
        def _(pool):
            own = Order(pool, own_pool)

            def load_tile(t):
                if t >= 2:
                    pool.wait_ge(h_turned, 2 * (t - 1))
                pool.dma_start(xin[:, t % 2, :], x[t * P:(t + 1) * P, :]).then_inc(xin_in[t % 2], 16)

            load_tile(0)
            load_tile(1)
            pool.dma_start(gain[:, :], gains[0]).then_inc(gain_in, 16)
            for s, (t0, nt, blocks, cap) in enumerate(SEQS):
                ph = 7 * s
                L = nt * P
                if s:
                    phase(pool, ph, phase_pool)
                for b in blocks:
                    if b:
                        pool.wait_ge(rot_out, NR * b)
                    c0 = block_tile(b) * P
                    for t in (TPB * b + 2, TPB * b + 3):
                        load_tile(t)
                    pool.dma_start(cos_t[:, :], rope[0][:, c0:c0 + BLK]).then_inc(rope_in, 16)
                    pool.dma_start(sin_t[:, :], rope[1][:, c0:c0 + BLK]).then_inc(rope_in, 16)
                    if b == 0:
                        for t in (TPB, TPB + 1):
                            load_tile(t)
                    for m in range(NM):
                        if m % 2 == 0:
                            g = FIRST_CHUNK[b] + m // 2 + 1
                            pool.wait_ge(w_hi_done, g + 1)
                            pool.tensor_tensor(wlo[:, g % 2, :, :],
                                               wraw[:, g % 2, :].rearrange("p (k n) -> p k n", k=KT),
                                               whi[:, g % 2, :, :].bitcast(F32), ALU.subtract
                                               ).then_inc(w_lo_done, 1)
                        if 20 <= m < 24:
                            j = m - 20
                            pool.wait_ge(col_out, NM * b + 21 + j)
                            pool.dma_start(z_dram[b][:, j, :], tmp[:, j % 2, :]).then_inc(z_out[j % 2], 16)
                for i in range(2):
                    pool.wait_ge(z_out[i], 16 * 2 * (blocks[-1] + 1))
                pool.memset(mark[0:1, 0:1], 0.0).then_inc(phase_pool, 1)

                phase(pool, ph + 1, phase_pool)

                def k_lo(h, halves):
                    for c_ in halves:
                        pool.wait_ge(khi_done, 2 * (HEADS * s + h) + c_ + 1)
                        rows, other = slice(64 * c_, 64 * c_ + 64), slice(64 * (1 - c_), 64 * (1 - c_) + 64)
                        pool.tensor_tensor(khl[other, h % 2, c_, 0:L], kT[rows, h, 0:L],
                                           khl[rows, h % 2, c_, 0:L].bitcast(F32), ALU.subtract
                                           ).then_inc(klo_done, 1)

                def q_lo(a, pieces):
                    h, i = (4 * a) // nt, (4 * a) % nt
                    for c_, half in pieces:
                        pool.wait_ge(qhi_done, 4 * (t0 + a) + Q_PIECES.index((c_, half)) + 1)
                        rows = slice(64 * c_, 64 * c_ + 64)
                        pool.tensor_tensor(qhl[64 * half:64 * half + 64, a % 2, 2 + c_, :],
                                           qT[rows, h, i * P:i * P + BLK],
                                           qhl[rows, a % 2, c_, :].bitcast(F32), ALU.subtract).then_inc(qlo_done, 1)

                q_lo(0, Q_PIECES)
                for u in range(4 * nt):
                    if u // 4 + 1 < nt:
                        q_lo(u // 4 + 1, q_pieces(u))
                    if u // nt + 1 < HEADS:
                        k_lo(u // nt + 1, k_pieces(u, nt))
                pool.memset(mark[0:1, 1:2], 0.0).then_inc(phase_pool, 1)

                phase(pool, ph + 2, phase_pool)
                pool.wait_ge(dt_a, 3 * s + 3)
                for cc in range(nt):
                    k = 8 * s + cc
                    pool.wait_ge(xf_done, 2 * (k + 1))
                    if k >= 2:
                        pool.wait_ge(st_done, 4 * (k - 1))
                    for d in range(2):
                        ins = pool.tensor_tensor(
                            xs[:, cc % 2, d, :].rearrange("p (h q) -> p h q", h=SH),
                            xf[:, cc, d, :].rearrange("p (h q) -> p h q", h=SH),
                            dts[:, 9, cc * 16 + 8 * d:cc * 16 + 8 * d + 8].unsqueeze(2).to_broadcast([P, SH, 64]),
                            ALU.mult)
                        ins.then_inc(xs_done, 1)
                pool.memset(mark[0:1, 0:1], 0.0).then_inc(phase_pool, 1)

                phase(pool, ph + 3, phase_pool)
                for cc in range(nt):
                    k = 8 * s + cc
                    ch = nt - 1 - cc
                    if cc >= 2:
                        pool.wait_ge(z_used, k - 1)
                    b = blocks[ch // TPB]
                    pool.dma_start(zin[:, k % 2, :].rearrange("p (j l) -> p j l", j=4),
                                   z_dram[b][:, :, (ch % TPB) * P:(ch % TPB + 1) * P]).then_inc(z_in[k % 2], 16)
                    if 1 <= ch - 1 <= nt - 2:
                        own.link(pool.tensor_tensor(
                            scan_t[1][:, :].rearrange("p (h q) -> p h q", h=SH),
                            state[1][:, ch - 1, :].rearrange("p (h q) -> p h q", h=SH),
                            dts[:, 8, (ch - 1) * 16 + 8:(ch - 1) * 16 + 16].unsqueeze(2).to_broadcast([P, SH, 64]),
                            ALU.mult))
                        pool.tensor_tensor(state[1][:, ch - 2, :], state[1][:, ch - 2, :], scan_t[1][:, :],
                                           ALU.add).then_inc(scan_b_done, 1)
                        pool.wait_ge(scan_b_done, 6 * s + cc + 1)
                    for u in range(4):
                        g, d, n = u // 2, u % 2, 4 * k + u
                        pool.wait_ge(e_done, n + 1)
                        if n >= 2:
                            pool.wait_ge(yh_done, n - 1)
                        pool.tensor_tensor(
                            cr[:, n % 2, :].rearrange("p (h l) -> p h l", h=4),
                            er[:, n % 2, :].rearrange("p (h l) -> p h l", h=4),
                            xbc[:, 6 + g, 2 + ch * P:2 + ch * P + P].unsqueeze(1).to_broadcast([P, 4, P]),
                            ALU.mult).then_inc(c_done, 1)
                pool.memset(mark[0:1, 0:1], 0.0).then_inc(phase_pool, 1)

                phase(pool, ph + 4, phase_pool)
                for k in range(6):
                    pool.wait_ge(mix_hi_done, KT * s + k + 1)
                    src = qT[:, k, 0:L] if k < 4 else xbc[:, k - 4, 2:2 + L]
                    pool.tensor_tensor(mix_lo[:, k, 0:L], src, mix_hi[:, k, 0:L].bitcast(F32), ALU.subtract)
                pool.memset(mark[0:1, 1:2], 0.0).then_inc(phase_pool, 1)

                phase(pool, ph + 5)
                for i in range(nt // 2):
                    pool.dma_start(x2[:, 2 * i:2 * i + 2, :],
                                   x[(t0 + 2 * i) * P:(t0 + 2 * i + 2) * P, :].rearrange("(t p) d -> p t d", p=P)
                                   ).then_inc(x2_in[i], 16)
                pool.dma_start(gain2[:, :], gains[1]).then_inc(gain_in, 16)
                if s == 0:
                    load_tile(8)
                    load_tile(9)
                for j in range(nt):
                    t = t0 + j
                    pool.wait_ge(h2_done, t + 1)
                    if t >= 4:
                        pool.wait_ge(x2_out[t % 4], 16 * (t // 4))
                    pool.dma_start(acc_dram[t * P:(t + 1) * P, :], x2[:, j, :]).then_inc(x2_out[t % 4], 16)
                    pool.dma_start(h2_dram[t * P:(t + 1) * P, :], h2[:, t % 4, :]).then_inc(h2_out[t % 4], 16)
                for i in range(4):
                    pool.wait_ge(x2_out[i], 16 * (t0 + nt) // 4)
                    pool.wait_ge(h2_out[i], 16 * (t0 + nt) // 4)
                pool.memset(mark[0:1, 0:1], 0.0).then_inc(phase_pool, 1)
                pool.memset(mark[0:1, 1:2], 0.0).then_inc(phase_pool, 1)

            phase(pool, 14, phase_pool)

            def gather(e1, first=False):
                if not first:
                    pool.wait_ge(adds_done, e1 * 2 - 1)
                pool.wait_ge(idx_ready, e1 + 1)
                pool.tensor_tensor(pmark[:, 0:1], pmark[:, 1:2], pmark[:, 2:3], ALU.add).then_inc(adds_done, 1)
                pool.indirect_dma_start(out=xe_s[:, :], out_offset=None, in_=h2_dram,
                                        in_offset=bass.IndirectOffsetOnAxis(ap=gi_s[:, 0:1], axis=0)
                                        ).then_inc(xs_in, 16)
                pool.indirect_dma_start(out=xe_p[:, :], out_offset=None, in_=h2_dram,
                                        in_offset=bass.IndirectOffsetOnAxis(ap=gi_p[:, 0:1], axis=0)
                                        ).then_inc(xp_in, 16)

            def expert(e, last):
                if not last:
                    pool.wait_ge(xturn, (e + 1) * 4)
                    gather(e + 1)
                pool.wait_ge(cur_ready, e + 1)
                pool.wait_ge(ys_done, (e + 1) * 4)
                pool.wait_ge(yp_done, e * 4 + 6)
                pool.wait_ge(adds_done, e * 2 + (1 if last else 2))
                pool.tensor_tensor(pmark[:, 0:1], pmark[:, 1:2], pmark[:, 2:3], ALU.add).then_inc(adds_done, 1)
                pool.indirect_dma_start(out=acc_dram, in_=ye_s[:, :], in_offset=None, compute_op=ALU.add,
                                        out_offset=bass.IndirectOffsetOnAxis(ap=si_s[:, 0:1], axis=0)
                                        ).then_inc(sc_s, 16)
                pool.indirect_dma_start(out=acc_dram, in_=ye_p[:, :], in_offset=None, compute_op=ALU.add,
                                        out_offset=bass.IndirectOffsetOnAxis(ap=si_p[:, 0:1], axis=0)
                                        ).then_inc(sc_p, 16)
                pool.wait_ge(sc_s, e * 16 + 16)
                pool.wait_ge(sc_p, e * 16 + 16)
                pool.wait_ge(scattered, e + 1)
                pool.tensor_tensor(pmark[:, 3:4], pmark[:, 1:2], pmark[:, 2:3], ALU.add).then_inc(scattered, 1)

            pool.memset(pmark[:, :], 0.0).then_inc(own_pool, 1)
            pool.memset(pmark2[:, :], 0.0).then_inc(scattered, 1)
            own.n += 1
            own.wait()
            gather(0, True)
            pool.dma_start(gain[:, :], gains[2]).then_inc(gain_in, 16)
            with pool.Fori(0, NE - 1) as e:
                expert(e, False)
            expert(NE - 1, True)

        @block.scalar
        def _(act):
            own = Order(act, own_act)

            def split(g):
                act.wait_ge(raw_in[g % 2], 16 * (g // 2 + 1))
                chunk_used(act, g - 2)
                act.activation(whi[:, g % 2, :, :], wraw[:, g % 2, :].rearrange("p (k n) -> p k n", k=KT), ACT.Copy
                               ).then_inc(w_hi_done, 1)

            def rms(t):
                act.wait_ge(xin_in[t % 2], 16 * (t // 2 + 1))
                act.activation(junk[:, :], xin[:, t % 2, :], ACT.Square, accum_out=small[:, 0, t:t + 1]
                               ).then_inc(ss_done, 1)
                act.wait_ge(ms_done, t + 1)
                act.activation(small[:, 2, t:t + 1], small[:, 1, t:t + 1], ACT.Sqrt).then_inc(rms_done, 1)

            def end():
                act.activation(mark[0:1, 4:5], mark[0:1, 5:6], ACT.Copy).then_inc(phase_act, 1)

            def squares(act, s, a):
                t0, nt = SEQS[s][0:2]
                h, i = (4 * a) // nt, (4 * a) % nt
                act.wait_ge(o_scaled, t0 + a + 1)
                if t0 + a:
                    act.wait_ge(o_summed, t0 + a)
                act.activation(osq[:, :].rearrange("p (t n) -> p t n", t=4), oatt[:, i:i + 4, h * P:(h + 1) * P],
                               ACT.Square).then_inc(o_squared, 1)

            act.wait_ge(cst_in, 16)
            act.wait_ge(par_in, 16)
            act.wait_ge(own_dve, 1)
            act.wait_ge(own_dve, 5)
            act.activation(lamt[:, 2:4], lamt[:, 0:2], ACT.Exp).then_inc(own_act, 1)
            act.activation(stat[:, 0, :], p_("a_log"), ACT.Exp).then_inc(own_act, 1)
            own.n = 2
            rms(0)
            rms(1)
            split(0)
            for s, (t0, nt, blocks, cap) in enumerate(SEQS):
                ph = 7 * s
                L = nt * P
                if s:
                    phase(act, ph, phase_act)
                for b in blocks:
                    for j in range(TPB):
                        t = TPB * b + j
                        if b and j == 0:
                            act.wait_ge(col_done, NM * b)
                            if b == 2:
                                act.wait_ge(op_done, 4 * 8)
                        for q in range(2):
                            act.wait_ge(h_turned, 2 * t + q + 1)
                            act.activation(ht_hi[:, 4 * q:4 * q + 4, j * P:(j + 1) * P],
                                           turn_bank(t, q).rearrange("p (k n) -> p k n", k=4), ACT.Copy
                                           ).then_inc(ht_hi_done, 1)
                        if j < 2:
                            rms(t + 2)
                    for m in range(NM):
                        n = NM * b + m
                        if m % 2 == 0:
                            split(FIRST_CHUNK[b] + m // 2 + 1)
                        if b == 0 and m == 18:
                            rms(TPB)
                            rms(TPB + 1)
                        act.wait_ge(col_done, n + 1)
                        src = pb[m % 4][:, :]
                        tok = block_tile(b) * P
                        if m < 8:
                            ins = act.activation(xbc[:, m, 2 + tok:2 + tok + BLK], src, ACT.Copy)
                        elif m < 20 or m == 24:
                            r = NR * b + min(m - 8, 12)
                            if r >= 2:
                                act.wait_ge(rot_out, r - 1)
                            ins = act.activation(stage[:, r % 2, :], src, ACT.Copy, scale=0.125 if m < 12 else 1.0)
                        else:
                            act.wait_ge(rot_out, NR * b + 8)
                            if m >= 22:
                                act.wait_ge(z_out[m % 2], 16 * (2 * b + 1))
                            ins = act.activation(tmp[:, m % 2, :], src, ACT.Silu)
                        ins.then_inc(col_out, 1)
                        if b == blocks[-1] and 9 <= m < 17:
                            i = m - 9
                            act.wait_ge(conv_done, 8 * s + i + 1)
                            act.activation(xbc[:, i, 2:2 + L], conv_acc[:, 0:L], ACT.Silu, bias=p_("conv_b", i)
                                           ).then_inc(conv_act, 1)
                end()

                phase(act, ph + 1, phase_act)

                def k_hi(h, halves):
                    if h >= 2:
                        act.wait_ge(sc_done, 2 * (4 * t0 + nt * (h - 1)))
                    for c_ in halves:
                        act.activation(khl[64 * c_:64 * c_ + 64, h % 2, c_, 0:L], kT[64 * c_:64 * c_ + 64, h, 0:L], ACT.Copy
                                       ).then_inc(khi_done, 1)

                def q_hi(a, pieces):
                    h, i = (4 * a) // nt, (4 * a) % nt
                    if a >= 2:
                        act.wait_ge(sc_done, 2 * (4 * t0 + 4 * (a - 1)))
                    for c_, half in pieces:
                        act.activation(qhl[64 * half:64 * half + 64, a % 2, c_, :],
                                       qT[64 * c_:64 * c_ + 64, h, i * P:i * P + BLK], ACT.Copy
                                       ).then_inc(qhi_done, 1)

                q_hi(0, Q_PIECES)
                k_hi(0, (0, 1))
                for u in range(4 * nt + 2):
                    U = 4 * t0 + u
                    if u < 4 * nt:
                        sl = prob[s][u % 2]
                        for c_ in range(2):
                            act.wait_ge(mx_done, 2 * U + c_ + 1)
                            if u >= 2:
                                act.wait_ge(wt_done, U - 1)
                            act.activation(sl[:, c_, 0:L], psum[:, 1024 * c_:1024 * c_ + L], ACT.Exp,
                                           bias=ostat[:, 0, 2 * (u % 2) + c_:2 * (u % 2) + c_ + 1],
                                           accum_out=ostat[:, 1, 2 * (u % 2) + c_:2 * (u % 2) + c_ + 1]
                                           ).then_inc(exp_done, 1)
                    if u >= 2:
                        w = u - 2
                        W = 4 * t0 + w
                        act.wait_ge(wt_done, W + 1)
                        if w >= 2:
                            act.wait_ge(av_done, W - 1)
                        act.activation(wgtT[:, w % 2, 0:L], psum[:, 2048:2048 + L], ACT.Copy).then_inc(wt_out, 1)
                    if u == 2:
                        act.wait_ge(dt_v, 4 * s + 1)
                        act.activation(dts[:, 2, 0:16 * nt], dts[:, 1, 0:16 * nt], ACT.Exp).then_inc(dt_a, 1)
                    if u == 3:
                        act.wait_ge(dt_v, 4 * s + 2)
                        act.activation(dts[:, 4, 0:16 * nt], dts[:, 3, 0:16 * nt], ACT.Ln).then_inc(dt_a, 1)
                    if u // 4 + 1 < nt:
                        q_hi(u // 4 + 1, q_pieces(u))
                    if u // nt + 1 < HEADS:
                        k_hi(u // nt + 1, k_pieces(u, nt))
                    if u % 4 == 0 and u >= 8:
                        squares(act, s, u // 4 - 2)
                squares(act, s, nt - 1)
                act.wait_ge(osum_done, s + 1)
                act.activation(asum[:, 2, 0:4 * nt], asum[:, 1, 0:4 * nt], ACT.Sqrt).then_inc(orms_done, 1)
                for i in range(nt):
                    act.wait_ge(ot_done, t0 + i + 1)
                    act.activation(qT[:, :, i * P:(i + 1) * P], pb[i % 2][:, :].rearrange("p (h n) -> p h n", h=4),
                                   ACT.Copy, scale=lamt[:, 8:9]).then_inc(ot_out, 1)
                end()

                phase(act, ph + 2, phase_act)
                act.wait_ge(dt_v, 4 * s + 4)
                act.activation(dts[:, 8, 0:16 * nt], dts[:, 3, 0:16 * nt], ACT.Exp).then_inc(own_act, 1)
                act.activation(dts[:, 9, 0:16 * nt], dts[:, 4, 0:16 * nt], ACT.Exp).then_inc(dt_a, 1)
                own.n += 1
                for cc in range(nt):
                    k = 8 * s + cc
                    act.wait_ge(bt_done, k + 1)
                    if k >= 2:
                        act.wait_ge(st_done, 4 * (k - 1))
                    act.activation(btok[:, cc % 2, :], pb[1 if cc % 2 == 0 else 3][:, 0:256], ACT.Copy
                                   ).then_inc(bt_out, 1)
                    for d in range(2):
                        act.wait_ge(st_done, 4 * k + 2 * d + 2)
                        to = cc + 1 if d == 0 else cc - 1
                        if 0 <= to < nt:
                            ins = act.activation(state[d][:, to, :], pb[4 + d][:, :], ACT.Copy)
                        else:
                            ins = act.activation(mark[0:1, 6:7], mark[0:1, 5:6], ACT.Copy)
                        ins.then_inc(st_out, 1)
                end()

                phase(act, ph + 3, phase_act)
                def row_exp(n4):
                    n = 32 * s + n4
                    act.wait_ge(row_done, n + 1)
                    if n >= 2:
                        act.wait_ge(c_done, n - 1)
                    act.activation(er[:, n % 2, :], row_bank(n), ACT.Exp).then_inc(e_done, 1)

                row_exp(0)
                for n4 in range(4 * nt):
                    n = 32 * s + n4
                    cc, g, d = n4 // 4, (n4 // 2) % 2, n4 % 2
                    if n4 + 1 < 4 * nt:
                        row_exp(n4 + 1)
                    act.wait_ge(d_done, n + 1)
                    if n >= 2:
                        act.wait_ge(m_done, n - 1)
                    for hh in range(4):
                        col = (nt - 1 - cc) * 16 + 8 * d + 4 * g + hh
                        ins = act.activation(lr[:, n % 2, hh * P:(hh + 1) * P], dr[:, n % 2, hh * P:(hh + 1) * P],
                                             ACT.Exp, bias=dts[:, 7, col:col + 1])
                    ins.then_inc(l_done, 1)
                end()

                phase(act, ph + 4, phase_act)
                nh = L // BLK
                for q in range(2 * nh):
                    g, hf = q // nh, q % nh
                    for i in range(2):
                        act.activation(sq[:, 2 * q + i, :], xbc[:, 2 * g + i, 2 + hf * BLK:2 + (hf + 1) * BLK],
                                       ACT.Square).then_inc(sq_done, 1)
                for k in range(4):
                    act.activation(mix_hi[:, k, 0:L], qT[:, k, 0:L], ACT.Copy).then_inc(mix_hi_done, 1)
                act.wait_ge(nms_done, s + 1)
                act.activation(dts[:, 1, 0:2 * nt], dts[:, 0, 0:2 * nt], ACT.Sqrt).then_inc(nrms_done, 1)
                for k in range(4, KT):
                    act.wait_ge(nrm_done, (8 if s else 0) + 2 * nh * ((k - 4) // 2 + 1))
                    act.activation(mix_hi[:, k, 0:L], xbc[:, k - 4, 2:2 + L], ACT.Copy).then_inc(mix_hi_done, 1)
                end()

                phase(act, ph + 5, phase_act)
                for jo in range(4):
                    g = FIRST_OUT_CHUNK[s] + jo + 1
                    if g < MOE_CHUNK:
                        split(g)
                    else:
                        act.wait_ge(raw_in[g % 2], 16 * (g // 2 + 1))
                        chunk_used(act, g - 2)
                        act.activation(whi[:, g % 2, :, :], wraw[:, g % 2, :].rearrange("p (k n) -> p k n", k=KT),
                                       ACT.Copy).then_inc(w_hi_done, 1)
                for i in range(nt + 4):
                    if i < nt:
                        act.wait_ge(op_out, 4 * t0 + 3 * nt + i + 1)
                        if t0 + i:
                            act.wait_ge(ss2_done, t0 + i)
                        act.activation(junk[:, :], x2[:, i, :], ACT.Square, accum_out=small[:, 0, i:i + 1]
                                       ).then_inc(ss2_done, 1)
                    if 1 <= i <= nt:
                        act.wait_ge(ms2_done, t0 + i)
                        act.activation(small[:, 2, i - 1:i], small[:, 1, i - 1:i], ACT.Sqrt).then_inc(rms2_done, 1)
                    if 3 <= i < nt + 3:
                        t = t0 + i - 3
                        for q in range(2):
                            act.wait_ge(h2_turned, 2 * t + q + 1)
                            if t >= 2:
                                act.wait_ge(lg_done, t - 1)
                            act.activation(h2T[:, t % 2, 4 * q:4 * q + 4, :],
                                           pb[6 + q][:, :].rearrange("p (k n) -> p k n", k=4), ACT.Copy
                                           ).then_inc(h2T_out, 1)
                end()

                phase(act, ph + 6, phase_act)
                act.wait_ge(rt_v, 3 * s + 2)
                act.activation(aff[:, 0:16 * nt], aff[:, 0:16 * nt], ACT.Exp).then_inc(rt_a, 1)
                if s == 0:
                    rms(8)
                    rms(9)
                end()

            phase(act, 14, phase_act)

            def turned_out(n, pairs):
                for kk in pairs:
                    act.wait_ge(xturn, n * 4 + kk + 1)
                    act.activation(xT[:, 2 * kk:2 * kk + 2, 0:TOK],
                                   pb[6 + kk % 2][:, 0:2 * TOK].rearrange("p (k n) -> p k n", k=2), ACT.Copy
                                   ).then_inc(xhi_done, 1)

            def expert(e, last):
                for j in range(ECH):
                    if not (last and j >= ECH - 2):
                        i = j + 2
                        landed, before = moe_raw_in[i % 4]
                        act.wait_ge(landed, e * (16 * ECH // 4) + 16 * (before + i // 4 + 1))
                        act.wait_ge(tile_done, e * 24 + 2 * j + 2)
                        act.activation(moe_hi[i % 3], moe_raw[i % 4].rearrange("p (k n) -> p k n", k=KT), ACT.Copy
                                       ).then_inc(w_hi_done, 1)
                    if j < 8 and j % 2:
                        for ft in range(2):
                            act.wait_ge(red_done, e * 16 + 4 + 2 * (j - 1) + ft + 1)
                            act.wait_ge(hm_done, e * 8 + 2 + j - 1)
                            act.activation(sg[:, ft, :], gr[:, ft, :], ACT.Silu).then_inc(silu_done, 1)
                    if j in (2, 4, 6, 7):
                        f0 = j - 2 if j < 7 else 6
                        for ft in range(2):
                            act.wait_ge(hm_done, e * 8 + 2 + f0 + ft + 1)
                            act.activation(hid[:, f0 + ft, 0:TOK], hm[:, ft, :], ACT.Copy).then_inc(hhi_done, 1)
                    if j == 7 and not last:
                        turned_out(e + 1, (0, 1))
                    if j >= 8:
                        dc = j - 8
                        bank = pb[4 + dc % 2]
                        act.wait_ge(tile_done, e * 24 + 2 + 2 * j + 2)
                        if dc == 0:
                            act.wait_ge(cur_ready, e + 1)
                        act.wait_ge(yp_done, e * 4 + dc + 1 - 0)
                        act.activation(tp[:, dc % 2, :], bank[64:P, CW:2 * CW], ACT.Copy).then_inc(tp_done, 1)
                        act.activation(ye_s[:, dc * CW:(dc + 1) * CW], bank[:, 0:CW], ACT.Copy,
                                       scale=gcur_s[:, 0:1]).then_inc(ys_done, 1)
                    if j == 8 and not last:
                        turned_out(e + 1, (2, 3))

            split(MOE_CHUNK + 1)
            turned_out(0, range(4))
            with act.Fori(0, NE - 1) as e:
                expert(e, False)
            expert(NE - 1, True)

            for t in range(NT + 1):
                if t < NT:
                    act.wait_ge(y_in[t % 4], 16 * (t // 4 + 1))
                    if t:
                        act.wait_ge(fss, t)
                    act.activation(junk[:, :], yin[:, t % 4, :], ACT.Square, accum_out=small[:, 0, t:t + 1]
                                   ).then_inc(fss, 1)
                if t >= 1:
                    act.wait_ge(fms, t)
                    act.activation(small[:, 2, t - 1:t], small[:, 1, t - 1:t], ACT.Sqrt).then_inc(frms, 1)

        @block.vector
        def _(dve):
            own = Order(dve, own_dve)
            tt, ts, stt = dve.tensor_tensor, dve.tensor_scalar, dve.scalar_tensor_tensor

            def split(g):
                dve.wait_ge(w_hi_done, g + 1)
                tt(wlo[:, g % 2, :, :], wraw[:, g % 2, :].rearrange("p (k n) -> p k n", k=KT),
                   whi[:, g % 2, :, :].bitcast(F32), ALU.subtract).then_inc(w_lo_done, 1)

            def end():
                dve.memset(mark[0:1, 8:9], 0.0).then_inc(phase_dve, 1)

            def normed(t):
                dve.wait_ge(ss_done, t + 1)
                ts(small[:, 1, t:t + 1], small[:, 0, t:t + 1], 1.0 / D, EPS, ALU.mult, ALU.add).then_inc(ms_done, 1)
                dve.wait_ge(rms_done, t + 1)
                own.link(dve.reciprocal(small[:, 3, t:t + 1], small[:, 2, t:t + 1]))
                stt(out=xin[:, t % 2, :], in0=xin[:, t % 2, :], scalar=small[:, 3, t:t + 1], in1=gain[:, :],
                    op0=ALU.mult, op1=ALU.mult).then_inc(hn_done, 1)

            def choose(s, n):
                L, o_ = SEQS[s][1] * P, 128 * s + 8 * n
                tv, ti = topv[:, o_:o_ + 8], topi[:, o_:o_ + 8]
                own.link(dve.max(tv, affT[:, 0:L]))
                own.link(dve.max_index(ti, tv, affT[:, 0:L]))
                own.link(dve.match_replace(affT[:, 0:L], tv, affT[:, 0:L], -1.0))

            def chosen(s):
                cols = slice(128 * s, 128 * s + SEQS[s][3])
                own.link(dve.tensor_copy(topf[:, cols], topi[:, cols]))
                own.link(ts(topf[:, cols], topf[:, cols], float(SEQS[s][0] * P), None, ALU.add))

            own.link(dve.memset(mark[0:1, :], 0.0))
            dve.wait_ge(par_in, 16)
            lam4 = p_("lam").rearrange("p (i j) -> p i j", i=4)
            own.link(tt(conv_acc[:, 0:64], lam4[:, 0, :], lam4[:, 1, :], ALU.mult))
            own.link(tt(conv_acc[:, 64:128], lam4[:, 2, :], lam4[:, 3, :], ALU.mult))
            own.link(dve.tensor_reduce(lamt[:, 0:2], conv_acc[:, 0:128].rearrange("p (i j) -> p i j", i=2), AX.X,
                                       ALU.add))
            own.link(ts(lamt[:, 8:9], p_("sub_g"), 1.0 - LAM_INIT, None, ALU.mult))
            dve.wait_ge(own_act, 2)
            own.link(tt(lamt[:, 4:5], lamt[:, 2:3], lamt[:, 3:4], ALU.subtract))
            own.link(ts(lamt[:, 6:7], lamt[:, 4:5], LAM_INIT, -1.0, ALU.add, ALU.mult))
            own.link(ts(stat[:, 1, :], stat[:, 0, :], -1.0, None, ALU.mult))
            dve.wait_ge(gain_in, 16)
            normed(0)
            normed(1)
            split(0)
            for s, (t0, nt, blocks, cap) in enumerate(SEQS):
                ph = 7 * s
                L = nt * P
                if s:
                    phase(dve, ph, phase_dve)
                own.step(dve.memset(xbc[:, :, 0:2], 0.0))
                own.link(dve.memset(xbc[:, :, 2 + L:4 + L], 0.0))
                for b in blocks:
                    for j in range(TPB):
                        t = TPB * b + j
                        for q in range(2):
                            dve.wait_ge(ht_hi_done, 2 * t + q + 1)
                            sl = (slice(None), slice(4 * q, 4 * q + 4), slice(j * P, (j + 1) * P))
                            tt(ht_lo[sl], turn_bank(t, q).rearrange("p (k n) -> p k n", k=4),
                               ht_hi[sl].bitcast(F32), ALU.subtract).then_inc(ht_lo_done, 1)
                        if j < 2:
                            normed(t + 2)
                    tok = block_tile(b) * P
                    dve.wait_ge(rope_in, 32 * (b + 1))

                    def second_step(m):
                        r = NR * b + min(m - 8, 12)
                        st = stage[:, r % 2, :]
                        bank = pb[4 + r % 2]
                        if m < 16:
                            if r % NR == 0 and b:
                                for i in range(2):
                                    dve.wait_ge(z_out[i], 16 * 2 * b)
                            if r:
                                dve.wait_ge(rot_out, r)
                            dve.wait_ge(col_out, NM * b + m + 1)
                            own.step(tt(tmp[:, 0, :], st, cos_t[:, :], ALU.mult))
                            dve.wait_ge(turn_done, r + 1)
                            own.link(tt(tmp[:, 1, :], bank[:, :], sin_t[:, :], ALU.mult))
                            dst = (qT if m < 12 else kT)[:, (m - 8) % 4, tok:tok + BLK]
                            tt(dst, tmp[:, 0, :], tmp[:, 1, :], ALU.add).then_inc(rot_out, 1)
                        elif m < 20:
                            dve.wait_ge(turn_done, r + 1)
                            h = m - 16
                            dve.tensor_copy(v[:, block_tile(b):block_tile(b) + TPB, h * P:(h + 1) * P],
                                            bank[:, :].rearrange("p (t n) -> p t n", t=TPB)).then_inc(rot_out, 1)
                        else:
                            dve.wait_ge(turn_done, r + 1)
                            i = block_tile(b)
                            dve.tensor_copy(
                                dts[:, 6, 16 * i:16 * (i + TPB)].rearrange("p (t n) -> p t n", t=TPB),
                                bank[:, :].rearrange("p (t n) -> p t n", t=TPB)[:, :, 112:128]).then_inc(rot_out, 1)

                    for m in range(NM):
                        if 9 <= m < 21:
                            second_step(m - 1)
                        if b == 0 and m == 18:
                            normed(TPB)
                            normed(TPB + 1)
                        if s == 1 and m % 16 < 8:
                            choose(0, m % 16 + m // 16 * 8)
                        if b == blocks[-1] and 8 <= m < 16:
                            i = m - 8
                            if i == 0:
                                dve.wait_ge(col_out, NM * b + 8)
                            else:
                                dve.wait_ge(conv_act, 8 * s + i)
                            own.link(ts(conv_acc[:, 0:L], xbc[:, i, 0:L], p_("conv_w", 5 * i), None, ALU.mult))
                            for w in range(1, 5):
                                ins = stt(out=conv_acc[:, 0:L], in0=xbc[:, i, w:w + L], scalar=p_("conv_w", 5 * i + w),
                                          in1=conv_acc[:, 0:L], op0=ALU.mult, op1=ALU.add)
                                if w < 4:
                                    own.link(ins)
                                else:
                                    ins.then_inc(conv_done, 1)
                    second_step(24)
                if s == 1:
                    chosen(0)
                end()

                phase(dve, ph + 1, phase_dve)
                W = 16 * nt
                sl = slice(0, W)

                def rep(ap):
                    return ap.unsqueeze(1).to_broadcast([P, nt, 16])

                def grid(i):
                    return dts[:, i, sl].rearrange("p (t n) -> p t n", n=16)

                def dt_step(i):
                    if i == 0:
                        own.link(tt(grid(5), grid(6), rep(p_("dt_bias")), ALU.add))
                        own.link(ts(dts[:, 1, sl], dts[:, 5, sl], -1.0, None, ALU.mult))
                        tt(dts[:, 1, sl], dts[:, 5, sl], dts[:, 1, sl], ALU.min).then_inc(dt_v, 1)
                    elif i == 1:
                        dve.wait_ge(dt_a, 3 * s + 1)
                        ts(dts[:, 3, sl], dts[:, 2, sl], 1.0, None, ALU.add).then_inc(dt_v, 1)
                    else:
                        dve.wait_ge(dt_v, 4 * s + 2)
                        own.step(ts(dts[:, 8, sl], dts[:, 3, sl], -1.0, None, ALU.add))
                        own.link(dve.reciprocal(dts[:, 9, sl], dts[:, 3, sl]))
                        own.link(tt(dts[:, 8, sl], dts[:, 2, sl], dts[:, 8, sl], ALU.subtract))
                        own.link(tt(dts[:, 8, sl], dts[:, 8, sl], dts[:, 9, sl], ALU.mult))
                        dve.wait_ge(dt_a, 3 * s + 2)
                        own.link(tt(dts[:, 8, sl], dts[:, 8, sl], dts[:, 4, sl], ALU.add))
                        own.link(ts(dts[:, 5, sl], dts[:, 5, sl], 0.0, None, ALU.max))
                        own.link(tt(dts[:, 5, sl], dts[:, 5, sl], dts[:, 8, sl], ALU.add))
                        tt(grid(6), grid(5), rep(stat[:, 1, :]), ALU.mult).then_inc(dt_v, 1)

                def weights(w):
                    W = 4 * t0 + w
                    sl, o2 = prob[s][w % 2], 2 * (w % 2)
                    dve.wait_ge(exp_done, 2 * W + 2)
                    own.link(dve.reciprocal(rsum[:, 2 * (w % 8):2 * (w % 8) + 2], ostat[:, 1, o2:o2 + 2]))
                    own.link(stt(out=ostat[:, 2, o2:o2 + 1], in0=ostat[:, 1, o2:o2 + 1],
                                 scalar=rsum[:, 2 * (w % 8) + 1:2 * (w % 8) + 2], in1=lamt[:, 6:7],
                                 op0=ALU.mult, op1=ALU.mult))
                    stt(out=sl[:, 0, 0:L], in0=sl[:, 1, 0:L], scalar=ostat[:, 2, o2:o2 + 1], in1=sl[:, 0, 0:L],
                        op0=ALU.mult, op1=ALU.add).then_inc(wg_done, 1)

                def scaled(a):
                    h, i = (4 * a) // nt, (4 * a) % nt
                    dve.wait_ge(av_done, 4 * (t0 + a) + 4)
                    tt(oatt[:, i:i + 4, h * P:(h + 1) * P], pb[6 + a % 2].rearrange("p (t n) -> p t n", t=4),
                       rsum[:, 8 * (a % 2):8 * (a % 2) + 8:2].unsqueeze(2).to_broadcast([P, 4, P]), ALU.mult
                       ).then_inc(o_scaled, 1)

                def summed(a):
                    h, i = (4 * a) // nt, (4 * a) % nt
                    dve.wait_ge(o_squared, t0 + a + 1)
                    dve.tensor_reduce(asum[:, 0, 0:4 * nt].rearrange("p (t h) -> p t h", h=4)[:, i:i + 4, h],
                                      osq[:, :].rearrange("p (t n) -> p t n", t=4), AX.X, ALU.add
                                      ).then_inc(o_summed, 1)

                for c_ in range(2):
                    dve.wait_ge(khi_done, 2 * HEADS * s + c_ + 1)
                    rows, other = slice(64 * c_, 64 * c_ + 64), slice(64 * (1 - c_), 64 * (1 - c_) + 64)
                    tt(khl[other, 0, c_, 0:L], kT[rows, 0, 0:L], khl[rows, 0, c_, 0:L].bitcast(F32), ALU.subtract
                       ).then_inc(klo_done, 1)
                for u in range(4 * nt + 2):
                    U = 4 * t0 + u
                    for c_ in range(2):
                        if u < 4 * nt:
                            dve.wait_ge(sc_done, 2 * U + c_ + 1)
                            dve.tensor_reduce(ostat[:, 0, 2 * (u % 2) + c_:2 * (u % 2) + c_ + 1],
                                              psum[:, 1024 * c_:1024 * c_ + L], AX.X, ALU.max, negate=True
                                              ).then_inc(mx_done, 1)
                    if 1 <= u <= 4 * nt:
                        weights(u - 1)
                    if u in (1, 2, 4):
                        dt_step(u // 2)
                    if u % 4 == 3 and 7 <= u < 4 * nt:
                        scaled(u // 4 - 1)
                    if u % 4 == 1 and u >= 9:
                        summed(u // 4 - 2)
                scaled(nt - 1)
                summed(nt - 1)
                dve.wait_ge(o_summed, t0 + nt)
                ts(asum[:, 1, 0:4 * nt], asum[:, 0, 0:4 * nt], 1.0 / P, EPS, ALU.mult, ALU.add).then_inc(osum_done, 1)
                dve.wait_ge(orms_done, s + 1)
                own.link(dve.reciprocal(asum[:, 3, 0:4 * nt], asum[:, 2, 0:4 * nt]))
                for i in range(nt):
                    tt(oatt[:, i, :].rearrange("p (h n) -> p h n", h=4),
                       oatt[:, i, :].rearrange("p (h n) -> p h n", h=4),
                       asum[:, 3, 4 * i:4 * i + 4].unsqueeze(2).to_broadcast([P, 4, P]), ALU.mult
                       ).then_inc(on_done, 1)
                end()

                phase(dve, ph + 2, phase_dve)
                dve.wait_ge(cs_done, s + 1)
                cs = pb[7]
                own.step(ts(grid(7)[:, :, 0:8], cs[:, 0:8 * nt].rearrange("p (t n) -> p t n", n=8), -1.0, None,
                            ALU.mult))
                own.step(ts(grid(7)[:, :, 8:16], cs[:, 64:64 + 8 * nt].rearrange("p (t n) -> p t n", n=8), -1.0, None,
                            ALU.mult))
                own.link(dve.tensor_copy(dts[:, 3, sl], cs[:, 128:128 + W]))
                tt(dts[:, 4, sl], dts[:, 3, sl], dts[:, 7, sl], ALU.add).then_inc(dt_v, 1)
                dve.wait_ge(dt_a, 3 * s + 3)
                for cc in range(nt + 1):
                    k = 8 * s + cc
                    if cc < nt:
                        dve.wait_ge(xt_done, k + 1)
                        for d in range(2):
                            tt(xf[:, cc, d, :].rearrange("p (h q) -> p h q", h=SH),
                               pb[0 if cc % 2 == 0 else 2][:, :].rearrange("p (h q) -> p h q", h=SH),
                               dts[:, 5, cc * 16 + 8 * d:cc * 16 + 8 * d + 8].unsqueeze(2).to_broadcast([P, SH, 64]),
                               ALU.mult).then_inc(xf_done, 1)
                    ch = cc - 2
                    if ch >= 1:
                        dve.wait_ge(st_out, 2 * (8 * s + ch) + 1)
                        own.link(tt(scan_t[0][:, :].rearrange("p (h q) -> p h q", h=SH),
                                    state[0][:, ch, :].rearrange("p (h q) -> p h q", h=SH),
                                    dts[:, 8, ch * 16:ch * 16 + 8].unsqueeze(2).to_broadcast([P, SH, 64]), ALU.mult))
                        own.link(tt(state[0][:, ch + 1, :], state[0][:, ch + 1, :], scan_t[0][:, :], ALU.add))
                end()

                phase(dve, ph + 3, phase_dve)
                def masked(n4):
                    n, d = 32 * s + n4, n4 % 2
                    dve.wait_ge(e_done, n + 1)
                    if n >= 2:
                        dve.wait_ge(l_done, n - 1)
                    tt(dr[:, n % 2, :].rearrange("p (h l) -> p h l", h=4),
                       row_bank(n).rearrange("p (h l) -> p h l", h=4),
                       c("neg_b" if d else "neg_f").unsqueeze(1).to_broadcast([P, 4, P]), ALU.add
                       ).then_inc(d_done, 1)

                masked(0)
                for n4 in range(4 * nt):
                    n = 32 * s + n4
                    cc, g, d = n4 // 4, (n4 // 2) % 2, n4 % 2
                    k = 8 * s + cc
                    if n4 + 1 < 4 * nt:
                        masked(n4 + 1)
                    dve.wait_ge(l_done, n + 1)
                    dve.wait_ge(cb_done, k + 1)
                    if n >= 2:
                        dve.wait_ge(yh_done, n - 1)
                    tt(mr[:, n % 2, :].rearrange("p (h l) -> p h l", h=4),
                       lr[:, n % 2, :].rearrange("p (h l) -> p h l", h=4),
                       pb[cc % 2][:, g * P:(g + 1) * P].unsqueeze(1).to_broadcast([P, 4, P]), ALU.mult
                       ).then_inc(m_done, 1)
                    if n4 % 4 == 3:
                        tk = slice(2 + (nt - 1 - cc) * P, 2 + (nt - cc) * P)
                        dve.wait_ge(yh_done, n + 1)
                        for jj in range(4):
                            own.step(stt(out=xbc[:, jj, tk], in0=xbc[:, jj, tk], scalar=p_("d_skip", jj),
                                         in1=pb[4 + cc % 2][:, jj * P:(jj + 1) * P], op0=ALU.mult, op1=ALU.add))
                        own.wait()
                        dve.wait_ge(z_in[k % 2], 16 * (k // 2 + 1))
                        tt(xbc[:, 0:4, tk], xbc[:, 0:4, tk],
                           zin[:, k % 2, :].rearrange("p (j l) -> p j l", j=4), ALU.mult).then_inc(z_used, 1)
                end()

                phase(dve, ph + 4, phase_dve)
                nh = L // BLK
                dve.wait_ge(nsum_done, s + 1)
                ts(dts[:, 0, 0:2 * nt], pb[0][:, 0:2 * nt], 1.0 / 256, EPS, ALU.mult, ALU.add).then_inc(nms_done, 1)
                dve.wait_ge(nrms_done, s + 1)
                dve.reciprocal(dts[:, 2, 0:2 * nt], dts[:, 1, 0:2 * nt]).then_inc(ninv_done, 1)
                for q in range(2 * nh):
                    g, hf = q // nh, q % nh
                    dve.wait_ge(nrow_done, (4 if s else 0) + q + 1)
                    for i in range(2):
                        a = xbc[:, 2 * g + i, 2 + hf * BLK:2 + (hf + 1) * BLK]
                        stt(out=a, in0=a, scalar=p_("ssm_g", 2 * g + i), in1=pb[1 + q][:, :], op0=ALU.mult,
                            op1=ALU.mult).then_inc(nrm_done, 1)
                for k in (6, 7):
                    dve.wait_ge(mix_hi_done, KT * s + k + 1)
                    tt(mix_lo[:, k, 0:L], xbc[:, k - 4, 2:2 + L], mix_hi[:, k, 0:L].bitcast(F32), ALU.subtract)
                end()

                phase(dve, ph + 5, phase_dve)
                def residual(jo, i):
                    u = nt * jo + i
                    dve.wait_ge(op_done, 4 * t0 + u + 1)
                    if jo == 0 and i % 2 == 0:
                        dve.wait_ge(x2_in[i // 2], 16 * (s + 1))
                    a = x2[:, i, jo * CW:(jo + 1) * CW]
                    tt(a, a, pb[u % 4][:, 0:CW], ALU.add).then_inc(op_out, 1)

                for jo in range(3):
                    split(FIRST_OUT_CHUNK[s] + jo + 1)
                    for i in range(nt):
                        residual(jo, i)
                split(FIRST_OUT_CHUNK[s] + 4)
                dve.wait_ge(gain_in, 16 * (s + 2))
                for i in range(nt + 2):
                    if i >= 2:
                        j = i - 2
                        t = t0 + j
                        dve.wait_ge(rms2_done, t + 1)
                        own.link(dve.reciprocal(small[:, 3, j:j + 1], small[:, 2, j:j + 1]))
                        if t >= 4:
                            dve.wait_ge(h2_out[t % 4], 16 * (t // 4))
                            dve.wait_ge(h2_turned, 2 * (t - 3))
                        stt(out=h2[:, t % 4, :], in0=x2[:, j, :], scalar=small[:, 3, j:j + 1], in1=gain2[:, :],
                            op0=ALU.mult, op1=ALU.mult).then_inc(h2_done, 1)
                    if i < nt:
                        residual(3, i)
                    if 1 <= i <= nt:
                        dve.wait_ge(ss2_done, t0 + i)
                        ts(small[:, 1, i - 1:i], small[:, 0, i - 1:i], 1.0 / D, EPS, ALU.mult, ALU.add
                           ).then_inc(ms2_done, 1)
                dve.wait_ge(lg_done, t0 + nt)
                end()

                phase(dve, ph + 6, phase_dve)
                dve.tensor_copy(lgT[:, 0:L], psum[0:NE, 2048:2048 + L]).then_inc(rt_v, 1)
                dve.wait_ge(rt_p, 2 * s + 1)
                lg = pb[0][:, sl].rearrange("p (t n) -> p t n", n=NE)
                af = aff[:, sl].rearrange("p (t n) -> p t n", n=NE)
                own.link(dve.tensor_reduce(aff2[:, 0:nt], lg, AX.X, ALU.max))
                tt(af, lg, aff2[:, 0:nt].unsqueeze(2).to_broadcast([P, nt, NE]), ALU.subtract).then_inc(rt_v, 1)
                dve.wait_ge(rt_a, s + 1)
                own.link(dve.tensor_reduce(aff2[:, 16:16 + nt], af, AX.X, ALU.add))
                own.link(dve.reciprocal(aff2[:, 32:32 + nt], aff2[:, 16:16 + nt]))
                tt(af, af, aff2[:, 32:32 + nt].unsqueeze(2).to_broadcast([P, nt, NE]), ALU.mult).then_inc(rt_v, 1)
                dve.wait_ge(rt_p, 2 * s + 2)
                for q in range(L // 512):
                    own.step(dve.tensor_copy(affT[:, q * 512:(q + 1) * 512], pb[6 + q][0:NE, :]))
                own.wait()
                if s == 0:
                    normed(8)
                    normed(9)
                    end()
                    continue
                for n in range(cap // 8):
                    choose(s, n)
                chosen(s)
                dve.memset(mark[0:1, 9:10], 0.0).then_inc(rt_v, 1)
                dve.wait_ge(rt_p, 5)
                for i, (gate, idx) in enumerate(((gate_s, idx_s), (gate_p, idx_p))):
                    n = SEQS[i][3]
                    own.step(dve.tensor_copy(gate[:, :], pb[4 + i][0:n, 0:NE]))
                    own.link(dve.tensor_copy(idx[:, :], pb[4 + i][0:n, 16:16 + NE]))
                end()

            phase(dve, 14, phase_dve)
            dve.memset(mark[0:1, 10:11], 0.0).then_inc(tile_done, 2)
            dve.memset(mark[0:1, 11:12], 0.0).then_inc(red_done, 4)
            dve.memset(mark[0:1, 12:13], 0.0).then_inc(hm_done, 2)
            dve.memset(mark[0:1, 13:14], 0.0).then_inc(yp_done, 2)

            def next_indices(e1):
                dve.tensor_copy(gi_s[:, :], idx_s[:, bass.ds(e1, 1)])
                dve.tensor_copy(gi_p[:, :], idx_p[:, bass.ds(e1, 1)]).then_inc(idx_ready, 1)

            def turned_out(n, pairs):
                for kk in pairs:
                    dve.wait_ge(xhi_done, n * 4 + kk + 1)
                    tt(xT[:, 2 * kk:2 * kk + 2, TOK:2 * TOK],
                       pb[6 + kk % 2][:, 0:2 * TOK].rearrange("p (k n) -> p k n", k=2),
                       xT[:, 2 * kk:2 * kk + 2, 0:TOK].bitcast(F32), ALU.subtract).then_inc(xlo_done, 1)

            def expert(e, last):
                for j in range(ECH):
                    if j == 0 and not last:
                        dve.wait_ge(xs_in, e * 16 + 16)
                        dve.wait_ge(xp_in, e * 16 + 16)
                        next_indices(e + 1)
                    if j == 1:
                        dve.wait_ge(scattered, e + 1)
                        dve.tensor_copy(gcur_s[:, :], gate_s[:, bass.ds(e, 1)])
                        dve.tensor_copy(gcur_p[:, :], gate_p[:, bass.ds(e, 1)])
                        dve.tensor_copy(si_s[:, :], idx_s[:, bass.ds(e, 1)])
                        dve.tensor_copy(si_p[:, :], idx_p[:, bass.ds(e, 1)]).then_inc(cur_ready, 1)
                    if not (last and j >= ECH - 2):
                        i = j + 2
                        dve.wait_ge(w_hi_done, e * ECH + MOE_CHUNK + i + 1)
                        tt(moe_lo[i % 3], moe_raw[i % 4].rearrange("p (k n) -> p k n", k=KT),
                           moe_hi[i % 3].bitcast(F32), ALU.subtract).then_inc(w_lo_done, 1)
                    if j < 8:
                        for ft in range(2):
                            dve.wait_ge(tile_done, e * 24 + 2 + 2 * j + ft + 1)
                            dve.tensor_reduce((ur if j % 2 else gr)[:, ft, :],
                                              pb[2 * (j % 2) + ft][:, 0:2 * TOK].rearrange("p (a n) -> p n a", a=2),
                                              AX.X, ALU.add).then_inc(red_done, 1)
                    if j < 8 and j % 2:
                        for ft in range(2):
                            dve.wait_ge(silu_done, e * 8 + (j - 1) + ft + 1)
                            dve.wait_ge(red_done, e * 16 + 4 + 2 * j + ft + 1)
                            if j > 1:
                                dve.wait_ge(hlo_done, e * 8 + (j - 3) + ft + 1)
                            tt(hm[:, ft, :], sg[:, ft, :], ur[:, ft, :], ALU.mult).then_inc(hm_done, 1)
                    if j in (2, 4, 6, 7):
                        for ft in range(2):
                            f = (j - 2 if j < 7 else 6) + ft
                            dve.wait_ge(hhi_done, e * 8 + f + 1)
                            tt(hid[:, f, 256:384], hm[:, ft, 0:P], hid[:, f, 0:P].bitcast(F32), ALU.subtract)
                            tt(hid[:, f, 192:256], hm[:, ft, P:TOK], hid[:, f, P:TOK].bitcast(F32), ALU.subtract
                               ).then_inc(hlo_done, 1)
                    if j == 7 and not last:
                        turned_out(e + 1, (0, 1))
                    if j >= 8:
                        dc = j - 8
                        bank = pb[4 + dc % 2]
                        dve.wait_ge(tp_done, e * 4 + dc + 1)
                        dve.wait_ge(ys_done, e * 4 + dc + 1)
                        a = ye_p[:, dc * CW:(dc + 1) * CW]
                        own_tp = tt(a, bank[0:64, CW:2 * CW], tp[:, dc % 2, :], ALU.add)
                        own_tp.then_inc(half_added, 1)
                        dve.wait_ge(half_added, e * 4 + dc + 1)
                        ts(a, a, gcur_p[:, 0:1], None, ALU.mult).then_inc(yp_done, 1)
                    if j == 8 and not last:
                        turned_out(e + 1, (2, 3))

            next_indices(0)
            split(MOE_CHUNK + 1)
            turned_out(0, range(4))
            with dve.Fori(0, NE - 1) as e:
                expert(e, False)
            expert(NE - 1, True)

            dve.wait_ge(gain_in, 16 * 4)
            for i in range(NT + 1):
                if i < NT:
                    dve.wait_ge(fss, i + 1)
                    ts(small[:, 1, i:i + 1], small[:, 0, i:i + 1], 1.0 / D, EPS, ALU.mult, ALU.add).then_inc(fms, 1)
                if i >= 1:
                    t = i - 1
                    dve.wait_ge(frms, t + 1)
                    own.link(dve.reciprocal(small[:, 3, t:t + 1], small[:, 2, t:t + 1]))
                    if t >= 3:
                        dve.wait_ge(y_out[t % 3], 16 * (t // 3))
                    stt(out=yout[:, t % 3, :], in0=yin[:, t % 4, :], scalar=small[:, 3, t:t + 1], in1=gain[:, :],
                        op0=ALU.mult, op1=ALU.mult).then_inc(fy, 1)

        @block.tensor
        def _(pe):
            mm = pe.matmul
            pe.wait_ge(cst_in, 16)
            pe.wait_ge(par_in, 16)

            def split3(out, wh, wl, xh, xl, first, final, **kw):
                mm(out, wh, xh, start=first, stop=False, **kw)
                mm(out, wh, xl, start=False, stop=False, **kw)
                return mm(out, wl, xh, start=False, stop=final, **kw)

            for s, (t0, nt, blocks, cap) in enumerate(SEQS):
                ph = 7 * s
                L = nt * P
                if s:
                    phase(pe, ph)
                for b in blocks:
                    for j in range(TPB):
                        t = TPB * b + j
                        pe.wait_ge(hn_done, t + 1)
                        if t >= 2:
                            pe.wait_ge(ht_lo_done, 2 * (t - 1))
                        if b and j == 1:
                            pe.wait_ge(rot_out, NR * b)
                        for q in range(2):
                            for i in range(4):
                                k = 4 * q + i
                                last = pe.transpose(turn_bank(t, q)[:, i * P:(i + 1) * P],
                                                    xin[:, t % 2, k * P:(k + 1) * P], ident)
                            last.then_inc(h_turned, 1)
                    pe.wait_ge(ht_lo_done, 2 * TPB * (b + 1))

                    def second_step(m):
                        r = NR * b + min(m - 8, 12)
                        pe.wait_ge(col_out, NM * b + m + 1)
                        if r >= 2:
                            pe.wait_ge(rot_out, r - 1)
                        bank = pb[4 + r % 2]
                        if m < 16:
                            mm(bank[:, :], c("rot"), stage[:, r % 2, :], start=True, stop=True
                               ).then_inc(turn_done, 1)
                        else:
                            for i in range(TPB):
                                last = pe.transpose(bank[:, i * P:(i + 1) * P], stage[:, r % 2, i * P:(i + 1) * P],
                                                    ident)
                            last.then_inc(turn_done, 1)

                    for m in range(NM):
                        n = NM * b + m
                        g = FIRST_CHUNK[b] + m // 2
                        if m % 2 == 0:
                            pe.wait_ge(w_lo_done, g + 1)
                        if n >= 4:
                            pe.wait_ge(col_out, n - (3 if m >= 4 else m))
                        cols = slice(P, 2 * P) if (m % 2 or m == 24) else slice(0, P)
                        for k in range(KT):
                            last = split3(pb[m % 4][:, :], whi[:, g % 2, k, cols], wlo[:, g % 2, k, cols],
                                          ht_hi[:, k, :], ht_lo[:, k, :], k == 0, k == KT - 1)
                        last.then_inc(col_done, 1)
                        if 9 <= m < 21:
                            second_step(m - 1)
                    second_step(24)

                phase(pe, ph + 1)
                for u in range(4 * nt + 3):
                    U = 4 * t0 + u
                    if u < 4 * nt:
                        h, i = u // nt, u % nt
                        if i == 0:
                            pe.wait_ge(klo_done, 2 * (HEADS * s + h) + 2)
                        if u % 4 == 0:
                            pe.wait_ge(qlo_done, 4 * (t0 + u // 4) + 4)
                        for c_ in range(2):
                            if u:
                                pe.wait_ge(exp_done, 2 * (U - 1) + c_ + 1)
                            for q in range(L // BLK):
                                kk = khl[:, h % 2, c_, q * BLK:(q + 1) * BLK]
                                sl = qhl[:, (u // 4) % 2, :, (u % 4) * P:(u % 4 + 1) * P]
                                mm(pb[2 * c_ + q], sl[:, c_, :], kk, start=True, stop=False)
                                last = mm(pb[2 * c_ + q], sl[:, 2 + c_, :], kk, start=False, stop=True)
                            last.then_inc(sc_done, 1)
                    if 2 <= u <= 4 * nt + 1:
                        w, W = u - 2, U - 2
                        pe.wait_ge(wg_done, W + 1)
                        if w:
                            pe.wait_ge(wt_out, W)
                        for kk in range(nt):
                            last = pe.transpose(psum[:, 2048 + kk * P:2048 + (kk + 1) * P],
                                                prob[s][w % 2][:, 0, kk * P:(kk + 1) * P], ident)
                        last.then_inc(wt_done, 1)
                    if u >= 3:
                        w, W = u - 3, U - 3
                        h = w // nt
                        pe.wait_ge(wt_out, W + 1)
                        if w % 4 == 0 and w >= 8:
                            pe.wait_ge(o_scaled, t0 + w // 4 - 1)
                        for kk in range(nt):
                            last = mm(pb[6 + (w // 4) % 2][:, (w % 4) * P:(w % 4 + 1) * P],
                                      wgtT[:, w % 2, kk * P:(kk + 1) * P], v[:, kk, h * P:(h + 1) * P],
                                      start=(kk == 0), stop=(kk == nt - 1))
                        last.then_inc(av_done, 1)
                for i in range(nt):
                    pe.wait_ge(on_done, t0 + i + 1)
                    if i >= 2:
                        pe.wait_ge(ot_out, t0 + i - 1)
                    for h in range(4):
                        last = pe.transpose(pb[i % 2][:, h * P:(h + 1) * P], oatt[:, i, h * P:(h + 1) * P], ident)
                    last.then_inc(ot_done, 1)

                phase(pe, ph + 2)
                a3 = dts[:, 6, 0:16 * nt].rearrange("p (t n) -> p t n", n=16)
                pe.wait_ge(dt_v, 4 * s + 3)
                mm(pb[7][:, 0:8 * nt], c("cum_f"), a3[:, :, 0:8], start=True, stop=True)
                mm(pb[7][:, 64:64 + 8 * nt], c("cum_b"), a3[:, :, 8:16], start=True, stop=True)
                mm(pb[7][:, 128:128 + 16 * nt], c("ones"), dts[:, 6, 0:16 * nt], start=True, stop=True
                   ).then_inc(cs_done, 1)
                for cc in range(nt + 1):
                    k = 8 * s + cc
                    if cc < nt:
                        tk = slice(2 + cc * P, 2 + (cc + 1) * P)
                        if cc >= 2:
                            pe.wait_ge(xf_done, 2 * (k - 1))
                            pe.wait_ge(bt_out, k - 1)
                        for i in range(4):
                            last = pe.transpose(pb[0 if cc % 2 == 0 else 2][:, i * P:(i + 1) * P], xbc[:, i, tk], ident)
                        last.then_inc(xt_done, 1)
                        for i in range(2):
                            last = pe.transpose(pb[1 if cc % 2 == 0 else 3][:, i * P:(i + 1) * P], xbc[:, 4 + i, tk],
                                                ident)
                        last.then_inc(bt_done, 1)
                    if cc >= 1:
                        k -= 1
                        c1 = cc - 1
                        pe.wait_ge(bt_out, k + 1)
                        for d in range(2):
                            pe.wait_ge(xs_done, 2 * k + d + 1)
                            if c1:
                                pe.wait_ge(st_out, 2 * k + d - 1)
                            for g in range(2):
                                mm(pb[4 + d][:, g * 256:(g + 1) * 256], btok[:, c1 % 2, g * P:(g + 1) * P],
                                   xs[:, c1 % 2, d, g * 256:(g + 1) * 256], start=True, stop=True
                                   ).then_inc(st_done, 1)

                phase(pe, ph + 3)

                def rows_of(n4):
                    n = 32 * s + n4
                    cc, g, d = n4 // 4, (n4 // 2) % 2, n4 % 2
                    if n4 >= 3:
                        pe.wait_ge(d_done, n - 2)
                    for hh in range(4):
                        col = (nt - 1 - cc) * 16 + 8 * d + 4 * g + hh
                        last = mm(row_bank(n)[:, hh * P:(hh + 1) * P],
                                  dts[:, 6, col:col + 1].to_broadcast([P, P]), c("cum_b" if d else "cum_f"),
                                  start=True, stop=True)
                    last.then_inc(row_done, 1)

                rows_of(0)
                rows_of(1)
                for n4 in range(4 * nt):
                    n = 32 * s + n4
                    cc, g, d = n4 // 4, (n4 // 2) % 2, n4 % 2
                    k = 8 * s + cc
                    ch = nt - 1 - cc
                    if n4 % 4 == 0:
                        tk = slice(2 + ch * P, 2 + (ch + 1) * P)
                        if cc >= 2:
                            pe.wait_ge(m_done, n - 4)
                        for gg in range(2):
                            last = mm(pb[cc % 2][:, gg * P:(gg + 1) * P], xbc[:, 4 + gg, tk], xbc[:, 6 + gg, tk],
                                      start=True, stop=True)
                        last.then_inc(cb_done, 1)
                        if cc >= 2:
                            pe.wait_ge(z_used, k - 1)
                    if n4 + 2 < 4 * nt:
                        rows_of(n4 + 2)
                    pe.wait_ge(m_done, n + 1)
                    pe.wait_ge(c_done, n + 1)
                    if d == 1 and ch <= nt - 3:
                        pe.wait_ge(scan_b_done, 6 * s + nt - 2 - ch)
                    ybank = pb[4 + cc % 2]
                    for hh in range(4):
                        h = 4 * g + hh
                        out = ybank[64 * (h % 2):64 * (h % 2) + 64, (h // 2) * P:(h // 2 + 1) * P]
                        last = mm(out, xf[:, ch, d, h * 64:(h + 1) * 64], mr[:, n % 2, hh * P:(hh + 1) * P],
                                  start=(g == 0 and d == 0 and hh < 2), stop=(d == 1), skip_group_check=True)
                        if ch > 0 if d == 0 else ch < nt - 1:
                            last = mm(out, state[d][:, ch, h * 64:(h + 1) * 64], cr[:, n % 2, hh * P:(hh + 1) * P],
                                      start=False, stop=(d == 1), skip_group_check=True)
                    last.then_inc(yh_done, 1)

                phase(pe, ph + 4)
                nh = L // BLK
                for q in range(2 * nh):
                    g, hf = q // nh, q % nh
                    pe.wait_ge(sq_done, 2 * ((4 if s else 0) + q + 1))
                    for j in range(TPB):
                        col = 2 * (TPB * hf + j) + g
                        for i in range(2):
                            last = mm(pb[0][:, col:col + 1], sq[:, 2 * q + i, j * P:(j + 1) * P], c("ones")[:, 0:1],
                                      start=(i == 0), stop=(i == 1))
                last.then_inc(nsum_done, 1)
                pe.wait_ge(ninv_done, s + 1)
                for q in range(2 * nh):
                    g, hf = q // nh, q % nh
                    for j in range(TPB):
                        col = 2 * (TPB * hf + j) + g
                        last = mm(pb[1 + q][:, j * P:(j + 1) * P], dts[:, 2, col:col + 1].to_broadcast([P, P]),
                                  ident, start=True, stop=True)
                    last.then_inc(nrow_done, 1)

                phase(pe, ph + 5)
                def project(jo, i):
                    g, u = FIRST_OUT_CHUNK[s] + jo, nt * jo + i
                    if u >= 4:
                        pe.wait_ge(op_out, 4 * t0 + u - 3)
                    for k in range(KT):
                        last = split3(pb[u % 4][:, 0:CW], mix_hi[:, k, i * P:(i + 1) * P],
                                      mix_lo[:, k, i * P:(i + 1) * P], whi[:, g % 2, k, :], wlo[:, g % 2, k, :],
                                      k == 0, k == KT - 1)
                    last.then_inc(op_done, 1)

                for jo in range(3):
                    pe.wait_ge(w_lo_done, FIRST_OUT_CHUNK[s] + jo + 1)
                    for i in range(nt):
                        project(jo, i)
                pe.wait_ge(w_lo_done, FIRST_OUT_CHUNK[s] + 4)
                for i in range(nt + 4):
                    if i < nt:
                        project(3, i)
                    if 3 <= i < nt + 3:
                        t = t0 + i - 3
                        pe.wait_ge(h2_done, t + 1)
                        if t > t0:
                            pe.wait_ge(h2T_out, 2 * t)
                        for q in range(2):
                            for kk in range(4):
                                k = 4 * q + kk
                                last = pe.transpose(pb[6 + q][:, kk * P:(kk + 1) * P], h2[:, t % 4, k * P:(k + 1) * P],
                                                    ident)
                            last.then_inc(h2_turned, 1)
                    if i >= 4:
                        j = i - 4
                        pe.wait_ge(h2T_out, 2 * (t0 + j) + 2)
                        for k in range(KT):
                            last = mm(psum[0:NE, 2048 + j * P:2048 + (j + 1) * P], p_("router", k * NE, NE),
                                      h2T[:, (t0 + j) % 2, k, :], start=(k == 0), stop=(k == KT - 1))
                        last.then_inc(lg_done, 1)

                phase(pe, ph + 6)
                pe.wait_ge(rt_v, 3 * s + 1)
                for i in range(nt):
                    last = pe.transpose(pb[0][:, i * NE:(i + 1) * NE], lgT[:, i * P:(i + 1) * P], ident[0:NE, 0:NE])
                last.then_inc(rt_p, 1)
                pe.wait_ge(rt_v, 3 * s + 3)
                for i in range(nt):
                    last = pe.transpose(pb[6 + i // 4][0:NE, (i % 4) * P:(i % 4 + 1) * P], aff[:, i * NE:(i + 1) * NE],
                                        ident)
                last.then_inc(rt_p, 1)
            pe.wait_ge(rt_v, 7)
            for i in range(2):
                n = SEQS[i][3]
                cols = slice(128 * i, 128 * i + n)
                pe.transpose(pb[4 + i][0:n, 0:NE], topv[:, cols], ident[0:NE, 0:NE])
                last = pe.transpose(pb[4 + i][0:n, 16:16 + NE], topf[:, cols], ident[0:NE, 0:NE])
            last.then_inc(rt_p, 1)

            phase(pe, 14)
            pe.wait_ge(hm_done, 2)

            def turn(n, pairs):
                pe.wait_ge(xs_in, n * 16 + 16)
                pe.wait_ge(xp_in, n * 16 + 16)
                for kk in pairs:
                    if kk >= 2:
                        pe.wait_ge(xlo_done, n * 4 + kk - 1)
                    for i in range(2):
                        k = 2 * kk + i
                        bank = pb[6 + kk % 2]
                        pe.transpose(bank[:, i * TOK:i * TOK + P], xe_s[:, k * P:(k + 1) * P], ident)
                        last = pe.transpose(bank[:, i * TOK + P:(i + 1) * TOK], xe_p[:, k * P:(k + 1) * P],
                                            ident[0:64, 0:64])
                    last.then_inc(xturn, 1)

            def expert(e, last_one):
                pe.wait_ge(xlo_done, e * 4 + 4)
                for j in range(8):
                    hi, lo = moe_hi[j % 3], moe_lo[j % 3]
                    pe.wait_ge(w_lo_done, e * ECH + MOE_CHUNK + j + 1)
                    for ft in range(2):
                        q = 2 * j + ft
                        pe.wait_ge(red_done, e * 16 + q + 1)
                        bank = pb[2 * (j % 2) + ft]
                        cols = slice(ft * P, (ft + 1) * P)
                        for k in range(KT):
                            mm(bank[:, 0:2 * TOK], hi[:, k, cols], xT[:, k, :], start=(k == 0), stop=False)
                            last = mm(bank[:, 0:TOK], lo[:, k, cols], xT[:, k, 0:TOK], start=False,
                                      stop=(k == KT - 1))
                        last.then_inc(tile_done, 1)
                if not last_one:
                    turn(e + 1, (0, 1))
                pe.wait_ge(hlo_done, e * 8 + 6)
                for j in range(8, ECH):
                    hi, lo = moe_hi[j % 3], moe_lo[j % 3]
                    dc = j - 8
                    pe.wait_ge(w_lo_done, e * ECH + MOE_CHUNK + j + 1)
                    pe.wait_ge(yp_done, e * 4 + dc + 1)
                    bank = pb[4 + dc % 2]
                    for k in range(KT):
                        if j == 8 and k == 6:
                            pe.wait_ge(hlo_done, e * 8 + 8)
                        last = split3(bank[:, 0:CW], hid[:, k, 0:P], hid[:, k, 256:384], hi[:, k, :],
                                      lo[:, k, :], k == 0, k == KT - 1)
                    last.then_inc(tile_done, 1)
                    for k in range(KT):
                        mm(bank[:, CW:2 * CW], hid[:, k, P:256], hi[:, k, :], start=(k == 0), stop=False)
                        last = mm(bank[:, CW:2 * CW], hid[:, k, P:256], lo[:, k, :], start=False,
                                  stop=(k == KT - 1))
                    last.then_inc(tile_done, 1)
                    if j == 8 and not last_one:
                        turn(e + 1, (2, 3))

            turn(0, range(4))
            with pe.Fori(0, NE - 1) as e:
                expert(e, False)
            expert(NE - 1, True)


def _chunks(w, cols):
    import numpy as np
    return np.stack([np.ascontiguousarray(w[:, c0:c0 + 256].reshape(8, 128, 256).transpose(1, 0, 2)).reshape(128, 2048)
                     for c0 in cols])


def _shape_constants():
    import numpy as np
    i = np.arange(128)
    ident = np.eye(128, dtype=np.float32)
    cum_f = (i[:, None] <= i[None, :]).astype(np.float32)
    cum_b = (i[:, None] >= i[None, :]).astype(np.float32)
    rot = np.zeros((128, 128), np.float32)
    cos = np.ones((128, 1024), np.float32)
    sin = np.zeros((128, 1024), np.float32)
    inv = np.power(np.float32(500000.0), -np.arange(8, dtype=np.float32) * np.float32(2.0) / np.float32(16))
    ang = np.arange(1024, dtype=np.float32)[None, :] * inv.astype(np.float32)[:, None]
    for half in (0, 64):
        for r in range(8):
            rot[half + 8 + r, half + r] = -1.0
            rot[half + r, half + 8 + r] = 1.0
        for q in (0, 8):
            cos[half + q:half + q + 8] = np.cos(ang)
            sin[half + q:half + q + 8] = np.sin(ang)
    big = np.float32(-1e30)
    consts = np.concatenate([ident, cum_f, cum_b, (1 - cum_f) * big, (1 - cum_b) * big, rot,
                             np.ones((128, 128), np.float32)], 1).astype(np.float32)
    return consts, np.stack([cos, sin])


def kernel(x_prompt, x_sample, norm1_g, w_in, lam_qk, attn_sub_g, conv_w, conv_b, dt_bias, a_log, d_skip, ssm_norm_g,
           w_out, norm2_g, w_router, w_gate, w_up, w_down, final_g):
    import numpy as np
    import concourse.bacc as _bacc
    from concourse import mybir as _mybir
    from concourse.bass_utils import run_bass_kernel_spmd as _run

    A = np.asarray
    x = np.concatenate([A(x_sample)[0], A(x_prompt)[0]], 0)
    wi = A(w_in)[0]
    in_cols = [2048 + 256 * i for i in range(4)] + [256 * i for i in range(8)] + [wi.shape[1] - 256]
    wg, wu, wd = A(w_gate)[0], A(w_up)[0], A(w_down)[0]
    cols = [0, 256, 512, 768]
    moe = np.empty((16 * 12, 128, 2048), wg.dtype)
    for e in range(16):
        moe[12 * e:12 * e + 8:2] = _chunks(wg[e], cols)
        moe[12 * e + 1:12 * e + 8:2] = _chunks(wu[e], cols)
        moe[12 * e + 8:12 * e + 12] = _chunks(wd[e], cols)
    row = lambda a: np.broadcast_to(A(a).reshape(1, -1), (128, A(a).size))
    part = lambda a: A(a).reshape(-1, 128).T
    params = np.concatenate([
        A(conv_w)[0].T.reshape(8, 128, 5).transpose(1, 0, 2).reshape(128, 40), part(conv_b),
        part(np.repeat(A(d_skip)[0], 64)), part(ssm_norm_g), part(attn_sub_g), row(dt_bias), row(a_log), row(lam_qk),
        A(w_router)[0].reshape(8, 128, 16).transpose(1, 0, 2).reshape(128, 128)], 1)
    gains = np.stack([np.broadcast_to(A(g).reshape(1, -1), (128, 1024)) for g in (norm1_g, norm2_g, final_g)])
    consts, rope = _shape_constants()
    arrays = {"x": x, "w_in_chunks": _chunks(wi, in_cols), "w_out_chunks": _chunks(A(w_out)[0], cols),
              "moe_chunks": moe, "params": params, "consts": consts, "rope": rope, "gains": gains}
    arrays = {k: np.ascontiguousarray(a) for k, a in arrays.items()}

    nc = _bacc.Bacc("TRN2", target_bir_lowering=False, num_devices=1)
    args = [nc.dram_tensor(k, a.shape, _mybir.dt.from_np(a.dtype), kind="ExternalInput").ap()
            for k, a in arrays.items()]
    args.append(nc.dram_tensor("y", x.shape, _mybir.dt.float32, kind="ExternalOutput").ap())
    hybrid_encoder(nc, *args)
    r = _run(nc, [arrays], core_ids=[0])
    y = r.results[0]["y"]
    return y[None, 1024:], y[None, :1024]
```
